# Optimizing a Trainium2 kernel written in Bass

```python
import jax, jax.numpy as jnp
from jax import lax
import numpy as np

D_MODEL = 1024
BATCH = 1
SEQ = 256
DEPTH = 1
DEC_BATCH = 8
DEC_SEQ = 16
PAST_LEN = 512

CHUNK = 64
Q_BLOCK = 128
N_MEM = 256
EPS = 1e-6
NEG_INF = -1e30
FOX_HEADS = 8
FOX_HEAD_DIM = 64
FOX_WIDTH = FOX_HEADS * FOX_HEAD_DIM
FOX_SCALE = FOX_HEAD_DIM ** -0.5
FORGET_BIAS_INIT = 2.0
MLA_HEADS = 8
MLA_NOPE = 64
MLA_ROPE = 32
MLA_V = 64
MLA_Q_LORA = 256
MLA_KV_LORA = 256
MLA_SCALE = (MLA_NOPE + MLA_ROPE) ** -0.5
ROPE_BASE = 10000.0
X_HEADS = 4
X_HEAD_DIM = 128
X_WIDTH = X_HEADS * X_HEAD_DIM
X_SCALE = X_HEAD_DIM ** -0.5
N_EXPERTS = 32
TOP_K = 4
EXPERT_FF = D_MODEL
SWIGLU_LIMIT = 7.0
SWIGLU_ALPHA = 1.702
MOE_BLOCK = 128
IN_SIZES = (FOX_WIDTH, FOX_WIDTH, FOX_WIDTH, FOX_HEADS, MLA_Q_LORA, MLA_KV_LORA, MLA_ROPE, D_MODEL, D_MODEL)
IN_DIM = 3 * FOX_WIDTH + FOX_HEADS + MLA_Q_LORA + MLA_KV_LORA + MLA_ROPE + 2 * D_MODEL

kernel_name = 'hybrid_fox_mla_moe_streaming_step'

def rmsnorm(x, g):
    xf = x.astype(jnp.float32)
    y = xf * lax.rsqrt(jnp.mean(xf * xf, axis=-1, keepdims=True) + EPS)
    return (y * g.astype(jnp.float32)).astype(x.dtype)

def rope(x, pos):
    half = x.shape[-1] // 2
    inv_freq = ROPE_BASE ** (-jnp.arange(half, dtype=jnp.float32) / half)
    ang = pos.astype(jnp.float32)[:, None] * inv_freq[None, :]
    ang = ang.reshape((ang.shape[0],) + (1,) * (x.ndim - 3) + (half,))
    cos, sin = jnp.cos(ang), jnp.sin(ang)
    xf = x.astype(jnp.float32)
    x1, x2 = xf[..., :half], xf[..., half:]
    return jnp.concatenate([x1 * cos - x2 * sin, x2 * cos + x1 * sin], axis=-1).astype(x.dtype)

def split_points():
    pts, acc = [], 0
    for s in IN_SIZES[:-1]:
        acc += s
        pts.append(acc)
    return pts

def mixer_inputs(h, pos, p):
    B, T = h.shape[:2]
    z = h @ p['w_in']
    fq, fk, fv, f_logit, q_c, kv_c, k_r, g_a, g_b = jnp.split(z, split_points(), axis=-1)
    fq = fq.reshape(B, T, FOX_HEADS, FOX_HEAD_DIM)
    fk = fk.reshape(B, T, FOX_HEADS, FOX_HEAD_DIM)
    fv = fv.reshape(B, T, FOX_HEADS, FOX_HEAD_DIM)
    logf = jax.nn.log_sigmoid((f_logit + p['b_f']).astype(jnp.float32))
    q = (rmsnorm(q_c, p['g_q']) @ p['w_uq']).reshape(B, T, MLA_HEADS, MLA_NOPE + MLA_ROPE)
    q_nope = q[..., :MLA_NOPE]
    q_rope = rope(q[..., MLA_NOPE:], pos)
    q_lat = jnp.einsum('bthn,chn->bthc', q_nope, p['w_uk'])
    ckv = rmsnorm(kv_c, p['g_kv'])
    krope = rope(k_r, pos)
    return fq, fk, fv, logf, q_lat, q_rope, ckv, krope, jax.nn.sigmoid(g_a), jax.nn.sigmoid(g_b)

def fox_attend(q, k, v, cum_q, cum_k, qpos, kpos):
    s = jnp.einsum('bqhd,bkhd->bhqk', q, k).astype(jnp.float32) * FOX_SCALE
    s = s + jnp.swapaxes(cum_q, 1, 2)[..., :, None] - jnp.swapaxes(cum_k, 1, 2)[..., None, :]
    mask = kpos[None, :] <= qpos[:, None]
    pr = jax.nn.softmax(jnp.where(mask, s, NEG_INF), axis=-1)
    return jnp.einsum('bhqk,bkhd->bqhd', pr.astype(v.dtype), v)

def mla_attend(q_lat, q_rope, ckv, krope, qpos, kpos):
    s = (jnp.einsum('bqhc,bkc->bhqk', q_lat, ckv) + jnp.einsum('bqhr,bkr->bhqk', q_rope, krope)).astype(jnp.float32) * MLA_SCALE
    mask = (kpos[None, :] // CHUNK) <= (qpos[:, None] // CHUNK)
    pr = jax.nn.softmax(jnp.where(mask, s, NEG_INF), axis=-1)
    return jnp.einsum('bhqk,bkc->bqhc', pr.astype(ckv.dtype), ckv)

def sweep_query_blocks(block_fn, seq_len):
    starts = jnp.arange(seq_len // Q_BLOCK, dtype=jnp.int32) * Q_BLOCK
    out = jnp.swapaxes(lax.map(block_fn, starts), 0, 1)
    return out.reshape((out.shape[0], seq_len) + out.shape[3:])

def qslice(a, s0):
    return lax.dynamic_slice_in_dim(a, s0, Q_BLOCK, axis=1)

def mixer_output(fox_o, mla_lat, g_fox, g_mla, p):
    B, T = fox_o.shape[:2]
    a = fox_o.reshape(B, T, FOX_WIDTH) @ p['w_o_fox']
    mla_o = jnp.einsum('bthc,chv->bthv', mla_lat, p['w_uv']).reshape(B, T, MLA_HEADS * MLA_V)
    b = mla_o @ p['w_o_mla']
    return (g_fox * a + g_mla * b) @ p['w_out']

def mem_kv(mem, p):
    B, M = mem.shape[:2]
    m = rmsnorm(mem, p['g_mem'])
    k = (m @ p['w_xk']).reshape(B, M, X_HEADS, X_HEAD_DIM)
    v = (m @ p['w_xv']).reshape(B, M, X_HEADS, X_HEAD_DIM)
    return k, v

def cross_attend(h, mk, mv, p):
    B, T = h.shape[:2]
    q = (h @ p['w_xq']).reshape(B, T, X_HEADS, X_HEAD_DIM)
    s = jnp.einsum('bthd,bmhd->bhtm', q, mk).astype(jnp.float32) * X_SCALE
    pr = jax.nn.softmax(s, axis=-1)
    o = jnp.einsum('bhtm,bmhd->bthd', pr.astype(mv.dtype), mv).reshape(B, T, X_WIDTH)
    return o @ p['w_xo']

def moe(h, p):
    T, D = h.shape
    logits = (h @ p['w_router']).astype(jnp.float32) + p['b_router'].astype(jnp.float32)
    top_val, top_idx = lax.top_k(logits, TOP_K)
    gate_w = jax.nn.softmax(top_val, axis=-1)
    n_assign = T * TOP_K
    flat_e = top_idx.reshape(-1).astype(jnp.int32)
    flat_tok = jnp.repeat(jnp.arange(T, dtype=jnp.int32), TOP_K)
    flat_w = gate_w.reshape(-1)
    order = jnp.argsort(flat_e)
    sorted_e = flat_e[order]
    counts = jnp.zeros((N_EXPERTS,), jnp.int32).at[flat_e].add(1)
    padded = (counts + MOE_BLOCK - 1) // MOE_BLOCK * MOE_BLOCK
    pad_end = jnp.cumsum(padded)
    pad_start = pad_end - padded
    grp_start = jnp.cumsum(counts) - counts
    dest = pad_start[sorted_e] + jnp.arange(n_assign, dtype=jnp.int32) - grp_start[sorted_e]
    n_blocks = -(-(n_assign + N_EXPERTS * (MOE_BLOCK - 1)) // MOE_BLOCK)
    n_rows = n_blocks * MOE_BLOCK
    row_tok = jnp.zeros((n_rows,), jnp.int32).at[dest].set(flat_tok[order])
    row_w = jnp.zeros((n_rows,), jnp.float32).at[dest].set(flat_w[order])
    block_e = jnp.minimum(jnp.searchsorted(pad_end, jnp.arange(n_blocks, dtype=jnp.int32) * MOE_BLOCK, side='right'), N_EXPERTS - 1)
    xb = h[row_tok].reshape(n_blocks, MOE_BLOCK, D)

    def expert_block(args):
        xblk, e = args
        gu = xblk @ p['w_gu'][e] + p['b_gu'][e]
        gate = jnp.minimum(gu[..., :EXPERT_FF], SWIGLU_LIMIT)
        up = jnp.clip(gu[..., EXPERT_FF:], -SWIGLU_LIMIT, SWIGLU_LIMIT)
        glu = gate * jax.nn.sigmoid(gate * SWIGLU_ALPHA)
        return ((up + 1.0) * glu) @ p['w_down'][e] + p['b_down'][e]

    yb = lax.map(expert_block, (xb, block_e)).reshape(n_rows, D)
    y = jnp.zeros((T, D), jnp.float32).at[row_tok].add(yb.astype(jnp.float32) * row_w[:, None])
    return y.astype(h.dtype)

def residual_tail(x, mix, mk, mv, p):
    x = x + mix
    x = x + cross_attend(rmsnorm(x, p['g_x']), mk, mv, p)
    h = rmsnorm(x, p['g_ffn'])
    B, T, D = h.shape
    return x + moe(h.reshape(B * T, D), p).reshape(B, T, D)

def prompt_layer(x, mem, p):
    S = x.shape[1]
    pos = jnp.arange(S, dtype=jnp.int32)
    h = rmsnorm(x, p['g_mix'])
    fq, fk, fv, logf, q_lat, q_rope, ckv, krope, g_a, g_b = mixer_inputs(h, pos, p)
    cum = jnp.cumsum(logf, axis=1)

    def fox_block(s0):
        qpos = s0 + jnp.arange(Q_BLOCK, dtype=jnp.int32)
        return fox_attend(qslice(fq, s0), fk, fv, qslice(cum, s0), cum, qpos, pos)

    def mla_block(s0):
        qpos = s0 + jnp.arange(Q_BLOCK, dtype=jnp.int32)
        return mla_attend(qslice(q_lat, s0), qslice(q_rope, s0), ckv, krope, qpos, pos)

    fox_o = sweep_query_blocks(fox_block, S)
    mla_lat = sweep_query_blocks(mla_block, S)
    mix = mixer_output(fox_o, mla_lat, g_a, g_b, p)
    mk, mv = mem_kv(mem, p)
    x = residual_tail(x, mix, mk, mv, p)
    return x, fk, fv, logf, ckv, krope, mk, mv

def sample_layer(x, c_fk, c_fv, c_logf, c_ckv, c_krope, c_mk, c_mv, p):
    past, T = c_fk.shape[1], x.shape[1]
    qpos = past + jnp.arange(T, dtype=jnp.int32)
    kpos = jnp.arange(past + T, dtype=jnp.int32)
    h = rmsnorm(x, p['g_mix'])
    fq, fk, fv, logf, q_lat, q_rope, ckv, krope, g_a, g_b = mixer_inputs(h, qpos, p)
    k_all = jnp.concatenate([c_fk.astype(fk.dtype), fk], axis=1)
    v_all = jnp.concatenate([c_fv.astype(fv.dtype), fv], axis=1)
    cum = jnp.cumsum(jnp.concatenate([c_logf.astype(jnp.float32), logf], axis=1), axis=1)
    fox_o = fox_attend(fq, k_all, v_all, cum[:, past:], cum, qpos, kpos)
    ckv_all = jnp.concatenate([c_ckv.astype(ckv.dtype), ckv], axis=1)
    krope_all = jnp.concatenate([c_krope.astype(krope.dtype), krope], axis=1)
    mla_lat = mla_attend(q_lat, q_rope, ckv_all, krope_all, qpos, kpos)
    mix = mixer_output(fox_o, mla_lat, g_a, g_b, p)
    x = residual_tail(x, mix, c_mk.astype(x.dtype), c_mv.astype(x.dtype), p)
    return x, fk, fv, logf, ckv, krope

def setup_inputs(seed: int = 0) -> dict:
    key = jax.random.key(seed)
    ks = jax.random.split(key, 40)
    f32 = jnp.float32

    def nrm(i, shape, scale=1.0):
        return scale * jax.random.normal(ks[i], shape, f32)

    def gain(i, shape):
        return 1.0 + 0.05 * jax.random.normal(ks[i], shape, f32)

    L = DEPTH
    return {
        'x_prompt': nrm(0, (BATCH, SEQ, D_MODEL)),
        'x_sample': nrm(1, (DEC_BATCH, DEC_SEQ, D_MODEL)),
        'mem_prompt': nrm(2, (BATCH, N_MEM, D_MODEL)),
        'cache_fox_k': nrm(3, (L, DEC_BATCH, PAST_LEN, FOX_HEADS, FOX_HEAD_DIM)),
        'cache_fox_v': nrm(4, (L, DEC_BATCH, PAST_LEN, FOX_HEADS, FOX_HEAD_DIM)),
        'cache_fox_logf': jax.nn.log_sigmoid(FORGET_BIAS_INIT + nrm(5, (L, DEC_BATCH, PAST_LEN, FOX_HEADS))),
        'cache_mla_ckv': nrm(6, (L, DEC_BATCH, PAST_LEN, MLA_KV_LORA)),
        'cache_mla_krope': nrm(7, (L, DEC_BATCH, PAST_LEN, MLA_ROPE)),
        'cache_mem_k': nrm(8, (L, DEC_BATCH, N_MEM, X_HEADS, X_HEAD_DIM)),
        'cache_mem_v': nrm(9, (L, DEC_BATCH, N_MEM, X_HEADS, X_HEAD_DIM)),
        'g_mix': gain(10, (L, D_MODEL)),
        'w_in': nrm(11, (L, D_MODEL, IN_DIM), D_MODEL ** -0.5),
        'b_f': FORGET_BIAS_INIT + nrm(12, (L, FOX_HEADS), 0.1),
        'g_q': gain(13, (L, MLA_Q_LORA)),
        'w_uq': nrm(14, (L, MLA_Q_LORA, MLA_HEADS * (MLA_NOPE + MLA_ROPE)), MLA_Q_LORA ** -0.5),
        'g_kv': gain(15, (L, MLA_KV_LORA)),
        'w_uk': nrm(16, (L, MLA_KV_LORA, MLA_HEADS, MLA_NOPE), MLA_KV_LORA ** -0.5),
        'w_uv': nrm(17, (L, MLA_KV_LORA, MLA_HEADS, MLA_V), MLA_KV_LORA ** -0.5),
        'w_o_fox': nrm(18, (L, FOX_WIDTH, D_MODEL), FOX_WIDTH ** -0.5),
        'w_o_mla': nrm(19, (L, MLA_HEADS * MLA_V, D_MODEL), (MLA_HEADS * MLA_V) ** -0.5),
        'w_out': nrm(20, (L, D_MODEL, D_MODEL), D_MODEL ** -0.5),
        'g_x': gain(21, (L, D_MODEL)),
        'g_mem': gain(22, (L, D_MODEL)),
        'w_xq': nrm(23, (L, D_MODEL, X_WIDTH), D_MODEL ** -0.5),
        'w_xk': nrm(24, (L, D_MODEL, X_WIDTH), D_MODEL ** -0.5),
        'w_xv': nrm(25, (L, D_MODEL, X_WIDTH), D_MODEL ** -0.5),
        'w_xo': nrm(26, (L, X_WIDTH, D_MODEL), X_WIDTH ** -0.5),
        'g_ffn': gain(27, (L, D_MODEL)),
        'w_router': nrm(28, (L, D_MODEL, N_EXPERTS), D_MODEL ** -0.5),
        'b_router': nrm(29, (L, N_EXPERTS), 0.01),
        'w_gu': nrm(30, (L, N_EXPERTS, D_MODEL, 2 * EXPERT_FF), D_MODEL ** -0.5),
        'b_gu': nrm(31, (L, N_EXPERTS, 2 * EXPERT_FF), 0.01),
        'w_down': nrm(32, (L, N_EXPERTS, EXPERT_FF, D_MODEL), EXPERT_FF ** -0.5),
        'b_down': nrm(33, (L, N_EXPERTS, D_MODEL), 0.01),
        'g_final': gain(34, (D_MODEL,)),
    }

def reference(x_prompt, x_sample, mem_prompt, cache_fox_k, cache_fox_v, cache_fox_logf, cache_mla_ckv,
              cache_mla_krope, cache_mem_k, cache_mem_v, g_mix, w_in, b_f, g_q, w_uq, g_kv, w_uk, w_uv,
              w_o_fox, w_o_mla, w_out, g_x, g_mem, w_xq, w_xk, w_xv, w_xo, g_ffn, w_router, b_router,
              w_gu, b_gu, w_down, b_down, g_final):
    xp, xs = x_prompt, x_sample
    pk, pv, pl, pc, pr, pmk, pmv = [], [], [], [], [], [], []
    sk, sv, sl, sc, sr = [], [], [], [], []
    for l in range(DEPTH):
        p = {'g_mix': g_mix[l], 'w_in': w_in[l], 'b_f': b_f[l], 'g_q': g_q[l], 'w_uq': w_uq[l],
             'g_kv': g_kv[l], 'w_uk': w_uk[l], 'w_uv': w_uv[l], 'w_o_fox': w_o_fox[l],
             'w_o_mla': w_o_mla[l], 'w_out': w_out[l], 'g_x': g_x[l], 'g_mem': g_mem[l],
             'w_xq': w_xq[l], 'w_xk': w_xk[l], 'w_xv': w_xv[l], 'w_xo': w_xo[l], 'g_ffn': g_ffn[l],
             'w_router': w_router[l], 'b_router': b_router[l], 'w_gu': w_gu[l], 'b_gu': b_gu[l],
             'w_down': w_down[l], 'b_down': b_down[l]}
        xp, fk, fv, lf, ck, kr, mk, mv = prompt_layer(xp, mem_prompt, p)
        pk.append(fk); pv.append(fv); pl.append(lf); pc.append(ck); pr.append(kr); pmk.append(mk); pmv.append(mv)
        xs, fk2, fv2, lf2, ck2, kr2 = sample_layer(xs, cache_fox_k[l], cache_fox_v[l], cache_fox_logf[l],
                                                   cache_mla_ckv[l], cache_mla_krope[l], cache_mem_k[l],
                                                   cache_mem_v[l], p)
        sk.append(fk2); sv.append(fv2); sl.append(lf2); sc.append(ck2); sr.append(kr2)
    y_prompt = rmsnorm(xp, g_final)
    y_sample = rmsnorm(xs, g_final)
    p_fox_k = jnp.stack(pk); p_fox_v = jnp.stack(pv); p_fox_logf = jnp.stack(pl)
    p_mla_ckv = jnp.stack(pc); p_mla_krope = jnp.stack(pr)
    p_mem_k = jnp.stack(pmk); p_mem_v = jnp.stack(pmv)
    s_fox_k = jnp.stack(sk); s_fox_v = jnp.stack(sv); s_fox_logf = jnp.stack(sl)
    s_mla_ckv = jnp.stack(sc); s_mla_krope = jnp.stack(sr)
    return (y_prompt, y_sample, p_fox_k, p_fox_v, p_fox_logf, p_mla_ckv, p_mla_krope, p_mem_k, p_mem_v,
            s_fox_k, s_fox_v, s_fox_logf, s_mla_ckv, s_mla_krope)


_drawn_inputs = setup_inputs


def setup_inputs(seed=0):
    import zlib

    import numpy as np

    out = dict(_drawn_inputs(seed))
    spreads = {}
    factors = {'g_q': 2.774, 'b_gu': 8.0, 'b_down': 8.0}
    for name, (base, spread) in spreads.items():
        noise = np.random.default_rng([zlib.crc32(name.encode()), seed]).standard_normal(out[name].shape)
        drawn = base * np.exp(spread * noise) if base else spread * noise
        out[name] = __import__('jax').numpy.asarray(drawn.astype(out[name].dtype))
    for name, factor in factors.items():
        out[name] = (out[name] * factor).astype(out[name].dtype)
    return out
```

```python
from contextlib import ExitStack

import numpy as np

import concourse.bass as bass
from concourse import mybir

F32 = mybir.dt.float32
BF16 = mybir.dt.bfloat16
I32 = mybir.dt.int32
U32 = mybir.dt.uint32
ALU = mybir.AluOpType
ACT = mybir.ActivationFunctionType
X = mybir.AxisListType.X

P = 128
D = 1024
KD = D // P
NT = 3
TOK = NT * P
NB, NQ = 8, 16
PAST = 512
KT = PAST // P
H = 8
FW = 512
LORA = 256
ROPE = 32
QH = 96
XH, XD, MEM = 4, 128, 256
NE = 32
TOPK = 4
CAP = 64
OVER = 24
NBLK = NE + OVER
EPS = 1e-6
NEG = -1e30
FOX_SCALE = 64 ** -0.5
MLA_SCALE = 96 ** -0.5
X_SCALE = 128 ** -0.5
LIMIT, ALPHA = 7.0, 1.702
SLOT = 2048
NRING = 8
C_FQ, C_FK, C_FV, C_FL, C_QC, C_KV, C_KR, C_G = 0, 512, 1024, 1536, 1544, 1800, 2056, 2088

CONST = {}
_at = 0
for _name, _n in (("ident", 128), ("tri", 1024), ("blocktri", 128), ("z1", 128), ("causal", 128), ("z2", 128), ("chunk", 128),
                  ("foxnew", 240), ("mlanew", 240), ("cos", 48), ("sin", 48), ("iota", 64), ("i64", 64),
                  ("tokid", 3), ("pmod", 1), ("neg8", 64), ("zero", 32)):
    CONST[_name] = (_at, _n)
    _at += _n
NCONST = _at


def constants():
    c = np.zeros((P, NCONST), np.float32)

    def put(name, value):
        a, n = CONST[name]
        c[:value.shape[0], a:a + n] = value.reshape(value.shape[0], n)

    p = np.arange(P)
    incl = (p[:, None] <= p[None, :]).astype(np.float32)
    strict = (p[:, None] < p[None, :]).astype(np.float32)
    put("ident", np.eye(P, dtype=np.float32))
    put("tri", np.concatenate([strict] * 3 + [incl] * 4 + [np.ones((P, P), np.float32)], 1))
    same = p[:, None] // NQ == p[None, :] // NQ
    put("blocktri", incl * same)
    put("causal", np.where(p[None, :] <= p[:, None], 0, NEG).astype(np.float32))
    put("chunk", np.where(p[None, :] // 64 <= p[:, None] // 64, 0, NEG).astype(np.float32))
    q = p % NQ
    j = np.arange(NQ)
    new = np.full((P, 15, NQ), NEG, np.float32)
    new[:, 7] = np.where(j[None, :] <= q[:, None], 0, NEG)
    put("foxnew", new)
    new = np.full((P, 15, NQ), NEG, np.float32)
    new[:, 7] = 0
    put("mlanew", new)
    half = ROPE // 2
    freq = np.float32(10000.0) ** (-np.arange(half, dtype=np.float32) / np.float32(half))
    pos = np.stack([p, p + P, PAST + q], 1).astype(np.float32)
    ang = pos[:, :, None] * freq[None, None, :].astype(np.float32)
    put("cos", np.cos(ang))
    put("sin", np.sin(ang))
    put("iota", np.tile(np.arange(64, dtype=np.float32), (P, 1)))
    put("i64", np.tile(64 * np.arange(64, dtype=np.float32), (P, 1)))
    put("tokid", np.stack([p, p + P, p + 2 * P], 1).astype(np.float32))
    put("pmod", (p % NE).astype(np.float32)[:, None])
    put("neg8", np.concatenate([-8 * np.eye(64, dtype=np.float32)] * 2, 0))
    return c


def bc(ap, shape):
    return ap.broadcast_to(shape)


def build(nc, d, out):
    ctx = ExitStack()
    with ctx:
        def sb(name, shape, dt=F32):
            return ctx.enter_context(nc.sbuf_tensor(name, shape, dt))

        def sem(name):
            return ctx.enter_context(nc.semaphore(name))

        ring = sb("ring", [P, 12, SLOT])
        low = ring[:, 8:11, :].rearrange("p s n -> p (s n)")
        gates = low.rearrange("p (n t) -> p n t", n=16)
        fk = low[:, 0:1536].rearrange("p (t n) -> p t n", t=NT)
        qc = low[:, 1536:2304].rearrange("p (t n) -> p t n", t=NT)
        qcT = low[:, 2304:3072].rearrange("p (c t) -> p c t", c=2)
        qnT = low[:, 3072:4608].rearrange("p (c t) -> p c t", c=4)
        qrope = low[:, 4608:5376].rearrange("p (t h r) -> p t h r", t=NT, r=ROPE)
        skT = [low[:, 3072 * i:3072 * i + 2048].rearrange("p (g s) -> p g s", g=4) for i in range(2)]
        scT = [low[:, 3072 * i + 2048:3072 * i + 3072].rearrange("p (c s) -> p c s", c=2) for i in range(2)]
        xkT = [low[:, 1024 * i:1024 * i + 1024].rearrange("p (h s) -> p h s", h=XH) for i in range(2)]
        prob = [ring[:, 11, 512 * i:512 * i + 512] for i in range(4)]
        sprob = [ring[:, 11, 640 * i:640 * i + 640] for i in range(3)]
        probTs = sb("probTs", [P, SLOT])
        probT = [probTs[:, 512 * i:512 * i + 512] for i in range(4)]
        sprobT = [probTs[:, 640 * i:640 * i + 640].rearrange("p (k m) -> p k m", k=5) for i in range(3)]
        ukT = probTs[:, 0:1024].rearrange("p (g c) -> p g c", g=4)
        con = sb("con", [P, NCONST])
        xr = sb("xr", [P, NT, D])
        xflat = xr[:, :, :].rearrange("p t n -> p (t n)")
        qpair = xflat[:, 0:1024].rearrange("p (b g m) -> p b g m", b=NB, g=4)
        qrS = xflat[0:ROPE, 1024:2048].rearrange("p (b h q) -> p b h q", b=NB, h=H)
        cumS = xflat[64:128, 2048:2688]
        sel8 = xflat[64:128, 1024:2048].rearrange("p (b m) -> p b m", b=NB)
        logfw = xflat[:, 2944:3008]
        hT = sb("hT", [P, KD, TOK])
        fqT = sb("fqT", [P, 4, TOK])
        fkT = sb("fkT", [P, 4, TOK])
        fv = sb("fv", [P, NT, FW])
        att = sb("att", [P, 2688])
        ckv = att[:, 0:768].rearrange("p (t n) -> p t n", t=NT)
        ckvT = att[:, 768:1536].rearrange("p (c t) -> p c t", c=2)
        krT = att[:, 1536:1920]
        qrT = att[:, 1920:2688].rearrange("p (c t) -> p c t", c=2)
        xn2 = low[:, 2048:5120].rearrange("p (t n) -> p t n", t=NT)
        qlf = sb("latent", [P, 2 * H * TOK])
        ql = qlf[:, 0:4096].rearrange("p (c h t) -> p c h t", c=2, h=H)
        qs = qlf[:, 4096:6144].rearrange("p (c b h q) -> p c b h q", c=2, b=NB, h=H)
        foxT = sb("foxT", [P, 4, TOK])
        mlaT = sb("mlaT", [P, 4, TOK])
        mlaf = mlaT[:, :, :].rearrange("p g t -> p (g t)")
        junk = probTs[:, 1024:2048]
        junk2 = low[:, 5376:5632]
        srT = [mlaf[0:ROPE, 512 * i:512 * i + 512] for i in range(2)]
        lgc = foxT[:, 0, 0:256].rearrange("p (k b h) -> p k b h", k=KT, b=NB)
        small = sb("small", [P, 160])
        memx = qlf[:, 0:2048].rearrange("p (t n) -> p t n", t=2)
        memT = qlf[:, 2048:4096].rearrange("p (k t) -> p k t", k=KD)
        mk = qlf[:, 4096:5120].rearrange("p (t n) -> p t n", t=2)
        mv = qlf[:, 5120:6144].rearrange("p (t n) -> p t n", t=2)
        mkTs = foxT[:, :, :].rearrange("p g t -> p (g t)")[:, 0:1024].rearrange("p (h s) -> p h s", h=XH)
        xqT, xoT = fqT, fkT
        xpair = fv[:, :, :].rearrange("p t n -> p (t n)")[:, 0:1024].rearrange("p (b h m) -> p b h m", b=NB, h=XH)
        cols = small[:, 0:64]
        bf_b = small[:, 64:72]
        br_b = small[:, 72:104]
        logf = small[:, 104:128].rearrange("p (t h) -> p t h", t=NT)
        gq_c = small[:, 128:130]
        gx_c = small[:, 130:138]
        gf_c = small[:, 138:146]
        gm_c = small[:, 146:154]
        gmem_c = sb("gmem_c", [P, KD])
        gkv_b = sb("gkv_b", [P, LORA])
        krope = sb("krope", [P, NT, ROPE])
        cumT = xflat[0:72, 2688:2944]
        wr = sb("wr", [P, KD, NE])
        chosen = probTs[:, 0:96].rearrange("p (t e) -> p t e", t=NT)
        logit = probTs[:, 96:192].rearrange("p (t e) -> p t e", t=NT)
        onehot = probTs[:, 192:576].rearrange("p (n e) -> p n e", e=NE)
        blk1 = probTs[:, 576:1248].rearrange("p (n b) -> p n b", b=NBLK)
        dist = probTs[:, 1248:1920].rearrange("p (n b) -> p n b", b=NBLK)
        fqf = fqT[:, :, :].rearrange("p g t -> p (g t)")
        pick = fqf[:, 0:768].rearrange("p (n m) -> p n m", m=CAP)
        slot_e = fqf[:, 768:864].rearrange("p (t e) -> p t e", t=NT)
        slot_d = fqf[:, 864:960].rearrange("p (t e) -> p t e", t=NT)
        e_tmp = fqf[:, 960:1344].rearrange("p (n e) -> p n e", e=NE)
        fkf = fkT[:, :, :].rearrange("p g t -> p (g t)")
        cnt = fkf[:, 0:32]
        novr = fkf[:, 32:64]
        oincl = fkf[:, 64:96]
        moved = fkf[:, 96:128]
        o_cmp = fkf[:, 128:896].rearrange("p (j e) -> p j e", e=NE)
        route = sb("route", [P, 256])
        top8 = route[:, 0:24].rearrange("p (t n) -> p t n", t=NT)
        idx8 = route[:, 24:48].bitcast(U32).rearrange("p (t n) -> p t n", t=NT)
        idxf = route[:, 48:72].rearrange("p (t n) -> p t n", t=NT)
        gatew = route[:, 72:84]
        slotf = route[:, 84:96]
        inblk = route[:, 96:108]
        ntop = route[:, 120:123]
        esum = route[:, 123:126]
        blocks_i = route[:, 126:127].bitcast(I32)
        bexp = route[:, 128:185]
        bexp_i = route[0:1, 186:242].bitcast(I32)
        idx_all = sb("idx_all", [CAP, NBLK + 1], I32)
        idx_col = sb("idx_col", [CAP, 1], I32)
        gS, uS, tS, hid = (qlf[:, 512 * i:512 * i + 512] for i in range(4))
        sS = probTs[:, 0:512]
        actT = qlf[:, 2048:2560].rearrange("p (k t) -> p k t", t=CAP)
        xT = qlf[:, 2560:3072].rearrange("p (k t) -> p k t", t=CAP)
        ysb = qlf[:, 3072:3584]
        xg = qlf[0:CAP, 3584:4608]
        sel = qlf[0:96, 4608:4640].bitcast(BF16)
        bias3 = att[0:96, 0:1536].bitcast(BF16)
        bstage = att[0:NE, 1536:2560]
        bmid = low[0:NE, 5120:5632].bitcast(BF16)
        slot_cols = [sb(f"slot_col{n}", [P, 1], I32)[:, 0:1] for n in range(NT * TOPK)]
        ygs = [ring[:, i // 2, 1024 * (i % 2):1024 * (i % 2) + 1024] for i in range(4)]
        gfin = ring[:, 2, 0:1024]
        yout = ring[:, 3:5, :].rearrange("p s n -> p (s n)")[:, 0:3072].rearrange("p (t n) -> p t n", t=NT)

        psum = [ctx.enter_context(nc.psum_tensor(f"bank{i}", [P, 512], F32))[:, :] for i in range(8)]

        def cc(name, rows=P):
            a, n = CONST[name]
            return con[0:rows, a:a + n]

        ident = cc("ident")
        t0 = CONST["tri"][0]
        ones = con[:, t0 + 896:t0 + 1024]
        incl_ones = con[:, t0 + 768:t0 + 1024]

        x3_dram = nc.dram_tensor("x3_normed", [TOK, D], F32).ap()
        y_dram = nc.dram_tensor("block_rows", [NBLK * CAP, D], F32).ap()

        bank_full = [sem(f"bank_full{i}") for i in range(8)]
        bank_free = [sem(f"bank_free{i}") for i in range(8)]
        ring_loaded = [sem(f"ring_loaded{i}") for i in range(12)]
        ring_used = [sem(f"ring_used{i}") for i in range(12)]
        consts_loaded = sem("consts_loaded")
        x_loaded = [sem(f"x_loaded{t}") for t in range(NT)]
        ckv_written = sem("ckv_written")
        fv_written = sem("fv_written")
        bias_step = sem("bias_step")
        zeroed = sem("zeroed")
        logf_wide = sem("logf_wide")
        gates_ready = sem("gates_ready")
        up_clipped = sem("up_clipped")
        product = sem("product")
        y_out = sem("y_out")
        lgc_loaded = sem("lgc_loaded")
        mem_loaded = sem("mem_loaded")
        x_again = sem("x_again")
        dve_step = sem("dve_step")
        act_step = sem("act_step")
        square_sum = sem("square_sum")
        xn_ready = sem("xn_ready")
        logit_exp = sem("logit_exp")
        logf_part = sem("logf_part")
        logf_ready = sem("logf_ready")
        krope_ready = sem("krope_ready")
        ckv_ready = sem("ckv_ready")
        qc_ready = sem("qc_ready")
        qrope_ready = sem("qrope_ready")
        outputs_written = sem("outputs_written")
        fk_written = sem("fk_written")
        score_max = sem("score_max")
        exp_done = sem("exp_done")
        prob_ready = sem("prob_ready")
        pairs_ready = sem("pairs_ready")
        mix_ready = sem("mix_ready")
        top_shift = sem("top_shift")
        top_exp = sem("top_exp")
        scratch_written = sem("scratch_written")
        masks_ready = sem("masks_ready")
        pick_ready = sem("pick_ready")
        idx_ready = sem("idx_ready")
        blocks_ready = sem("blocks_ready")
        bias_loaded = sem("bias_loaded")
        bias_moved = sem("bias_moved")
        mk_written = sem("mk_written")
        first_copied = sem("first_copied")
        idx_copied = sem("idx_copied")
        first_rows = sem("first_rows")
        rows_gathered = sem("rows_gathered")
        xT_full = sem("xT_full")
        xT_ready = sem("xT_ready")
        gate_clipped = sem("gate_clipped")
        gate_sig = sem("gate_sig")
        act_ready = sem("act_ready")
        actT_full = sem("actT_full")
        actT_ready = sem("actT_ready")
        y_copied = sem("y_copied")
        y_written = sem("y_written")
        y_gathered = [sem(f"y_gathered{i}") for i in range(4)]
        y_added = sem("y_added")
        gfin_loaded = sem("gfin_loaded")
        fin_ready = sem("fin_ready")

        groups = {}

        def open_bank(pe, key):
            n = groups[key] = len(groups)
            if n >= 8:
                pe.wait_ge(bank_free[n % 8], n // 8)
            return psum[n % 8]

        def full(key):
            return bank_full[groups[key] % 8]

        def free(key):
            return bank_free[groups[key] % 8]

        def count(key):
            return groups[key] // 8 + 1

        def bank(key):
            return psum[groups[key] % 8]

        w_in = d["w_in"][0].rearrange("(k p) n -> p k n", p=P)
        stream = []

        def kview(slot, k, n):
            return ring[:, slot, 0:k * n].rearrange("p (k n) -> p k n", k=k)

        def tile(key, parts):
            stream.append((key, parts))

        def whole(k, n, src):
            return [(lambda s: kview(s, k, n), src)]

        for j in range(2):
            tile(("fq", j), whole(KD, 256, w_in[:, :, C_FQ + 256 * j:C_FQ + 256 * j + 256]))
        for j in range(2):
            tile(("fk", j), whole(KD, 256, w_in[:, :, C_FK + 256 * j:C_FK + 256 * j + 256]))
        tile("fl", [(lambda s: kview(s, KD, 40)[:, :, 0:8], w_in[:, :, C_FL:C_FL + 8]),
                    (lambda s: kview(s, KD, 40)[:, :, 8:40], w_in[:, :, C_KR:C_KR + ROPE])])
        tile("kv", whole(KD, 256, w_in[:, :, C_KV:C_KV + 256]))
        tile("qc", whole(KD, 256, w_in[:, :, C_QC:C_QC + 256]))
        tile("uk", whole(2, 512, d["w_uk"][0].rearrange("(k p) h n -> p k (h n)", p=P)))
        tile("uq", whole(2, 768, d["w_uq"][0].rearrange("(k p) n -> p k n", p=P)))
        for j in range(2):
            tile(("fv", j), whole(KD, 256, w_in[:, :, C_FV + 256 * j:C_FV + 256 * j + 256]))
        for b in range(NB):
            tile(("sk", b), whole(KT, FW, d["cache_fox_k"][0, b].rearrange("(p k) h n -> p k (h n)", k=KT)))
            tile(("sc", b), [(lambda s: kview(s, KT, LORA), d["cache_mla_ckv"][0, b].rearrange("(p k) n -> p k n", k=KT)),
                             (lambda s: ring[:, s, 1024:1152].rearrange("p (k n) -> p k n", k=KT),
                              d["cache_mla_krope"][0, b].rearrange("(p k) n -> p k n", k=KT))])
            tile(("sv", b), whole(KT, FW, d["cache_fox_v"][0, b].rearrange("(p k) h n -> p k (h n)", k=KT)))
        tile("uv", whole(2, 512, d["w_uv"][0].rearrange("(k p) h n -> p k (h n)", p=P)))
        for j in range(8):
            tile(("g", j), whole(KD, 256, w_in[:, :, C_G + 256 * j:C_G + 256 * j + 256]))
        for w in ("xk", "xv"):
            for j in range(2):
                tile((w, j), whole(KD, 256, d["w_" + w][0].rearrange("(k p) n -> p k n", p=P)[:, :, 256 * j:256 * j + 256]))
        for j in range(2):
            for w in ("w_o_fox", "w_o_mla"):
                tile((w, j), whole(4, 512, d[w][0].rearrange("(k p) n -> p k n", p=P)[:, :, 512 * j:512 * j + 512]))
        for j in range(4):
            tile(("out", j), whole(KD, 256, d["w_out"][0].rearrange("(k p) n -> p k n", p=P)[:, :, 256 * j:256 * j + 256]))
        for j in range(2):
            tile(("xq", j), whole(KD, 256, d["w_xq"][0].rearrange("(k p) n -> p k n", p=P)[:, :, 256 * j:256 * j + 256]))
        for b in range(NB):
            tile(("cm", b), [(lambda s: kview(s, 2, FW), d["cache_mem_k"][0, b].rearrange("(p k) h n -> p k (h n)", k=2)),
                             (lambda s: ring[:, s, 1024:2048].rearrange("p (k n) -> p k n", k=2),
                              d["cache_mem_v"][0, b].rearrange("(p k) h n -> p k (h n)", k=2))])
        for j in range(2):
            tile(("xo", j), whole(4, 512, d["w_xo"][0].rearrange("(k p) n -> p k n", p=P)[:, :, 512 * j:512 * j + 512]))

        place = {key: n for n, (key, _) in enumerate(stream)}
        NPRE = len(stream)
        loads = {}
        loaded_at = []
        for n, (key, parts) in enumerate(stream):
            loads[n % NRING] = loads.get(n % NRING, 0) + 16 * len(parts)
            loaded_at.append(loads[n % NRING])
        GU_SLOT = [(NPRE + c) % NRING for c in range(KD)]
        GU_LOADS = [loads[s] for s in GU_SLOT]
        DOWN_SLOT = [8, 9, 10, 11]

        last_group = {}

        def used_last(pe, ins, key):
            last_group[key] = len(groups) - 1

        def arrived(pe, key):
            n = place[key]
            pe.wait_ge(ring_loaded[n % NRING], loaded_at[n])
            return n % NRING

        def prompt_units(kind):
            if kind == "fox":
                return [("fox", t, hs) for t in range(2) for hs in ((0, 2), (1, 3), (4, 6), (5, 7))]
            if kind == "mla":
                return [("mla", t, (g, g + 4)) for t in range(2) for g in range(4)]
            return [("mem", t, (2 * g, 2 * g + 1)) for t in range(2) for g in range(2)]

        UNITS = prompt_units("fox") + prompt_units("mla")
        XUNITS = prompt_units("mem")
        NU, NXU = len(UNITS), len(XUNITS)
        NLOADS = 10
        SU = 2 * NB
        LAG_T, LAG_V = 2, 3
        U_SAMPLE = NU
        U_MEM = NU + SU
        U_SMEM = NU + SU + NXU

        def width(kind, t):
            return 2 * P if kind == "mem" else P * (t + 1)

        S_COL = {}
        def col(name, n=1):
            if name not in S_COL:
                S_COL[name] = sum(v[1] for v in S_COL.values())
                S_COL[name] = (S_COL[name], n)
            a, m = S_COL[name]
            return cols[:, a:a + m]

        block = ctx.enter_context(nc.Block())

        @block.tensor
        def _(pe):
            def mm(o, l, r, start, stop):
                return pe.matmul(o, l, r, start=start, stop=stop, skip_group_check=True)

            def done(ins, key):
                ins.then_inc(bank_full[groups[key] % 8], 1)

            def rms_turn(name, src, tiles):
                rows = {"hT": xr, "mT": memx}.get(name, xn2)
                for t in range(tiles):
                    if src is not None:
                        pe.wait_ge(*src(t))
                    for half in range(2):
                        ps = open_bank(pe, (name, t, half))
                        for c in range(4):
                            k = 4 * half + c
                            i = pe.transpose(ps[:, P * c:P * c + P], rows[:, t, P * k:P * k + P], ident)
                        done(i, (name, t, half))

            def project(key, w, t, src, n=256, kn=256):
                ps = open_bank(pe, key)
                s = place[w] % NRING
                for k in range(KD):
                    i = mm(ps[:, 0:n], src[:, k, P * t:P * t + P], kview(s, KD, kn)[:, k, 0:n], k == 0, k == KD - 1)
                done(i, key)
                return i

            def project_T(key, slot, col0, src):
                ps = open_bank(pe, key)
                for k in range(KD):
                    i = mm(ps[:, 0:TOK], kview(slot, KD, 256)[:, k, col0:col0 + P], src[:, k, :], k == 0, k == KD - 1)
                done(i, key)
                return i

            pe.wait_ge(consts_loaded, 16 * NLOADS)
            rms_turn("hT", lambda t: (xn_ready, t + 1), NT)
            for t in range(NT):
                for half in range(2):
                    pe.wait_ge(free(("hT", t, half)), count(("hT", t, half)))
            for j in range(2):
                s = arrived(pe, ("fq", j))
                for m in range(2):
                    i = project_T(("fqT", 2 * j + m), s, P * m, hT)
                used_last(pe, i, ("fq", j))
            for j in range(2):
                arrived(pe, ("fk", j))
                for t in range(NT):
                    i = project(("fk", t, j), ("fk", j), t, hT)
                used_last(pe, i, ("fk", j))
            arrived(pe, "fl")
            for t in range(NT):
                i = project(("fl", t), "fl", t, hT, n=40, kn=40)
            used_last(pe, i, "fl")
            arrived(pe, "kv")
            for t in range(NT):
                i = project(("kv", t), "kv", t, hT)
            used_last(pe, i, "kv")
            arrived(pe, "qc")
            for t in range(NT):
                i = project(("qc", t), "qc", t, hT)
            used_last(pe, i, "qc")
            s = arrived(pe, "uk")
            for c in range(2):
                ps = open_bank(pe, ("ukT", c))
                for g in range(4):
                    i = pe.transpose(ps[:, P * g:P * g + P], kview(s, 2, 512)[:, c, P * g:P * g + P], ident)
                done(i, ("ukT", c))
            used_last(pe, i, "uk")
            for t in range(NT):
                for j in range(2):
                    pe.wait_ge(free(("fk", t, j)), count(("fk", t, j)))
            for g in range(4):
                ps = open_bank(pe, ("fkT", g))
                for t in range(NT):
                    i = pe.transpose(ps[:, P * t:P * t + P], fk[:, t, P * g:P * g + P], ident)
                done(i, ("fkT", g))
            pe.wait_ge(krope_ready, NT)
            ps = open_bank(pe, "krT")
            for t in range(NT):
                i = pe.transpose(ps[0:ROPE, P * t:P * t + P], krope[:, t, :], ident)
            done(i, "krT")
            pe.wait_ge(ckv_ready, NT)
            for c in range(2):
                ps = open_bank(pe, ("ckvT", c))
                for t in range(NT):
                    i = pe.transpose(ps[:, P * t:P * t + P], ckv[:, t, P * c:P * c + P], ident)
                done(i, ("ckvT", c))
            pe.wait_ge(qc_ready, NT)
            for c in range(2):
                ps = open_bank(pe, ("qcT", c))
                for t in range(NT):
                    i = pe.transpose(ps[:, P * t:P * t + P], qc[:, t, P * c:P * c + P], ident)
                done(i, ("qcT", c))
            pe.wait_ge(logf_ready, NT)
            ps = open_bank(pe, "cumP")
            mm(ps[0:H, 0:256], logf[:, 0, :], incl_ones, True, False)
            i = mm(ps[0:H, P:256], logf[:, 1, :], incl_ones[:, 0:P], False, True)
            done(i, "cumP")
            pe.wait_ge(lgc_loaded, 16 * KT)
            pe.wait_ge(logf_wide, 1)
            ps = open_bank(pe, "cumS")
            for k in range(KT):
                i = mm(ps[0:64, :], lgc[:, k, :, :].rearrange("p b h -> p (b h)"), con[:, t0 + 128 * (3 - k):t0 + 128 * (3 - k) + 512], k == 0, k == KT - 1)
            done(i, "cumS")
            ps = open_bank(pe, "cumN")
            for k in range(KT):
                mm(ps[0:64, 0:P], lgc[:, k, :, :].rearrange("p b h -> p (b h)"), ones, k == 0, False)
            i = mm(ps[0:64, 0:P], logfw, cc("blocktri"), False, True)
            done(i, "cumN")
            for j in range(2):
                arrived(pe, ("fv", j))
                for t in range(NT):
                    i = project(("fv", t, j), ("fv", j), t, hT)
                used_last(pe, i, ("fv", j))
            for c in range(2):
                pe.wait_ge(free(("qcT", c)), count(("qcT", c)))
            s = arrived(pe, "uq")
            uq = kview(s, 2, 768)
            for t in range(NT):
                ps = open_bank(pe, ("qr", t))
                for k in range(2):
                    i = mm(ps[:, 0:256], qcT[:, k, P * t:P * t + P],
                           uq[:, k, :].rearrange("p (h n) -> p h n", n=QH)[:, :, 64:QH], k == 0, k == 1)
                done(i, ("qr", t))
            for g in range(4):
                ps = open_bank(pe, ("qn", g))
                for e in range(2):
                    for k in range(2):
                        h = 2 * g + e
                        i = mm(ps[64 * e:64 * e + 64, 0:TOK], uq[:, k, QH * h:QH * h + 64], qcT[:, k, :], k == 0, k == 1)
                done(i, ("qn", g))
            used_last(pe, i, "uq")
            for c in range(2):
                pe.wait_ge(free(("ukT", c)), count(("ukT", c)))
            for h in range(H):
                g, e = h // 2, 64 * (h % 2)
                if e == 0:
                    pe.wait_ge(free(("qn", g)), count(("qn", g)))
                for c in range(2):
                    ps = open_bank(pe, ("ql", h, c))
                    i = mm(ps[:, 0:TOK], ukT[e:e + 64, g, P * c:P * c + P], qnT[e:e + 64, g, :], True, True)
                    done(i, ("ql", h, c))
            pe.wait_ge(qrope_ready, NT)
            for c in range(2):
                ps = open_bank(pe, ("qrT", c))
                for t in range(NT):
                    i = pe.transpose(ps[:, P * t:P * t + P], qrope[:, t, 4 * c:4 * c + 4, :], ident)
                done(i, ("qrT", c))

            def scores(u, unit):
                kind, t, hs = unit
                ps = open_bank(pe, ("S", u))
                w = width(kind, t)
                for n, h in enumerate(hs):
                    o = ps[:, w * n:w * n + w]
                    if kind == "fox":
                        e = 64 * (h % 2)
                        mm(o, fqT[e:e + 64, h // 2, P * t:P * t + P], fkT[e:e + 64, h // 2, 0:w], n == 0, False)
                        i = mm(o, bc(con[e:e + H, CONST["neg8"][0] + h:CONST["neg8"][0] + h + 1], [H, P]),
                               cumT[e:e + H, 0:w], False, True)
                    elif kind == "mla":
                        e = 32 * (h % 4)
                        for c in range(2):
                            mm(o, ql[:, c, h, P * t:P * t + P], ckvT[:, c, 0:w], n == 0 and c == 0, False)
                        i = mm(o, qrT[e:e + 32, h // 4, P * t:P * t + P], krT[e:e + 32, 0:w], False, True)
                    else:
                        i = mm(o, xqT[:, h, P * t:P * t + P], mkTs[:, h, :], n == 0, n == 1)
                done(i, ("S", u))

            def turn(u, unit):
                kind, t, hs = unit
                pe.wait_ge(prob_ready, u + 1)
                ps = open_bank(pe, ("T", u))
                w = width(kind, t)
                nk = w // P
                for s in range(nk):
                    for n in range(2):
                        i = pe.transpose(ps[:, P * (2 * s + n):P * (2 * s + n) + P],
                                         prob[u % 4][:, w * n + P * s:w * n + P * s + P], ident)
                done(i, ("T", u))

            def values(u, unit):
                kind, t, hs = unit
                nk = width(kind, t) // P
                pt = probT[u % 4].rearrange("p (s n q) -> p s n q", n=2, q=P)
                pe.wait_ge(free(("T", u)), count(("T", u)))
                ps = open_bank(pe, ("V", u))
                for n, h in enumerate(hs):
                    if kind == "fox":
                        e = 64 * (h % 2)
                        for s in range(nk):
                            i = mm(ps[e:e + 64, P * n:P * n + P], fv[:, s, 64 * h:64 * h + 64], pt[:, s, n, :],
                                   n == 0 and s == 0, s == nk - 1)
                    elif kind == "mem":
                        for s in range(nk):
                            i = mm(ps[:, P * n:P * n + P], mv[:, s, P * h:P * h + P], pt[:, s, n, :],
                                   n == 0 and s == 0, s == nk - 1)
                if kind == "mla":
                    for c in range(2):
                        for s in range(nk):
                            i = mm(ps[:, 256 * c:256 * c + 256], ckv[:, s, P * c:P * c + P], pt[:, s, :, :],
                                   c == 0 and s == 0, s == nk - 1)
                done(i, ("V", u))

            def pipeline(units, u0):
                n = len(units)
                for i in range(n + LAG_V):
                    if i < n:
                        scores(u0 + i, units[i])
                    if LAG_T <= i < n + LAG_T:
                        turn(u0 + i - LAG_T, units[i - LAG_T])
                    if i >= LAG_V:
                        values(u0 + i - LAG_V, units[i - LAG_V])

            for g in range(4):
                pe.wait_ge(free(("fqT", g)), count(("fqT", g)))
                pe.wait_ge(free(("fkT", g)), count(("fkT", g)))
            for key in ["cumP", "krT", ("ckvT", 0), ("ckvT", 1), ("qrT", 0), ("qrT", 1)]:
                pe.wait_ge(free(key), count(key))
            for t in range(NT):
                for j in range(2):
                    pe.wait_ge(free(("fv", t, j)), count(("fv", t, j)))
            for h in range(H):
                for c in range(2):
                    pe.wait_ge(free(("ql", h, c)), count(("ql", h, c)))
            pipeline(UNITS, 0)

            def turn_cache(b):
                s = arrived(pe, ("sk", b))
                k3 = kview(s, KT, FW)
                for g in range(4):
                    ps = open_bank(pe, ("skT", b, g))
                    for k in range(KT):
                        i = pe.transpose(ps[:, P * k:P * k + P], k3[:, k, P * g:P * g + P], ident)
                    done(i, ("skT", b, g))
                used_last(pe, i, ("sk", b))
                s = arrived(pe, ("sc", b))
                c3 = kview(s, KT, LORA)
                for c in range(2):
                    ps = open_bank(pe, ("scT", b, c))
                    for k in range(KT):
                        i = pe.transpose(ps[:, P * k:P * k + P], c3[:, k, P * c:P * c + P], ident)
                    done(i, ("scT", b, c))
                ps = open_bank(pe, ("srT", b))
                for k in range(KT):
                    i = pe.transpose(ps[0:ROPE, P * k:P * k + P],
                                     ring[:, s, 1024:1152].rearrange("p (k n) -> p k n", k=KT)[:, k, :], ident)
                done(i, ("srT", b))

            def sample_scores(b):
                sel = sel8[:, b, :]
                rot = qrS[:, b, :, :].rearrange("p h q -> p (h q)")
                lat = [qs[:, c, b, :, :].rearrange("p h q -> p (h q)") for c in range(2)]
                for g in range(4):
                    pe.wait_ge(free(("skT", b, g)), count(("skT", b, g)))
                if b == 0:
                    pe.wait_ge(pairs_ready, 1)
                ps = open_bank(pe, ("sS", 2 * b))
                mm(ps[:, :], sel, cumS[:, 0:512], True, False)
                for g in range(4):
                    i = mm(ps[32 * g:32 * g + 32, :], qpair[:, b, g, :], skT[b % 2][:, g, :], False, True)
                done(i, ("sS", 2 * b))
                ps = open_bank(pe, ("sN", b))
                mm(ps[:, 0:P], sel, cumS[:, 512:640], True, False)
                for g in range(4):
                    i = mm(ps[32 * g:32 * g + 32, 0:P], qpair[:, b, g, :], fkT[:, g, 256:384], False, True)
                for c in range(2):
                    mm(ps[:, P:256], lat[c], ckvT[:, c, 256:384], False, False)
                i = mm(ps[:, P:256], rot, krT[0:ROPE, 256:384], False, True)
                done(i, ("sN", b))
                for c in range(2):
                    pe.wait_ge(free(("scT", b, c)), count(("scT", b, c)))
                pe.wait_ge(free(("srT", b)), count(("srT", b)))
                ps = open_bank(pe, ("sS", 2 * b + 1))
                for c in range(2):
                    mm(ps[:, :], lat[c], scT[b % 2][:, c, :], c == 0, False)
                i = mm(ps[:, :], rot, srT[b % 2], False, True)
                done(i, ("sS", 2 * b + 1))

            def sample_turn(n):
                pe.wait_ge(prob_ready, U_SAMPLE + n + 1)
                ps = open_bank(pe, ("sT", n))
                for k in range(KT):
                    i = pe.transpose(ps[:, P * k:P * k + P], sprob[n % 3][:, P * k:P * k + P], ident)
                done(i, ("sT", n))
                ps = open_bank(pe, ("sTn", n))
                i = pe.transpose(ps[:, 0:P], sprob[n % 3][:, 512:640], ident)
                done(i, ("sTn", n))

            def sample_values(n):
                b = n // 2
                pt = sprobT[n % 3]
                pe.wait_ge(free(("sT", n)), count(("sT", n)))
                pe.wait_ge(free(("sTn", n)), count(("sTn", n)))
                if n % 2 == 0:
                    s = arrived(pe, ("sv", b))
                    v3 = kview(s, KT, FW)
                    ps = open_bank(pe, ("sV", n))
                    for g in range(4):
                        for k in range(5):
                            v = v3[:, k, P * g:P * g + P] if k < KT else fv[:, 2, P * g:P * g + P]
                            i = mm(ps[:, 32 * g:32 * g + 32], v, pt[:, k, 32 * g:32 * g + 32], g == 0 and k == 0, k == 4)
                    done(i, ("sV", n))
                    used_last(pe, i, ("sv", b))
                else:
                    c3 = kview(place[("sc", b)] % NRING, KT, LORA)
                    ps = open_bank(pe, ("sV", n))
                    for c in range(2):
                        for k in range(5):
                            v = c3[:, k, P * c:P * c + P] if k < KT else ckv[:, 2, P * c:P * c + P]
                            i = mm(ps[:, P * c:P * c + P], v, pt[:, k, :], c == 0 and k == 0, k == 4)
                    done(i, ("sV", n))
                    used_last(pe, i, ("sc", b))

            pe.wait_ge(free("cumS"), count("cumS"))
            pe.wait_ge(free("cumN"), count("cumN"))
            turn_cache(0)
            for b in range(NB + 1):
                if b < NB:
                    sample_scores(b)
                if b >= 1:
                    for n in (2 * b - 2, 2 * b - 1):
                        sample_turn(n)
                if b + 1 < NB:
                    turn_cache(b + 1)
                if b >= 1:
                    for n in (2 * b - 2, 2 * b - 1):
                        sample_values(n)

            s = arrived(pe, "uv")
            uv = kview(s, 2, 512)
            pe.wait_ge(free(("sV", SU - 1)), count(("sV", SU - 1)))
            for g in range(4):
                ps = open_bank(pe, ("mo", g))
                for e in range(2):
                    for c in range(2):
                        h = 2 * g + e
                        o, w = ps[64 * e:64 * e + 64, :], uv[:, c, 64 * h:64 * h + 64]
                        mm(o[:, 0:256], w, ql[:, c, h, :], c == 0, c == 1)
                        i = mm(o[:, 256:TOK].rearrange("p (b q) -> p b q", q=NQ), w, qs[:, c, :, h, :], False, c == 1)
                done(i, ("mo", g))
            used_last(pe, i, "uv")
            for j in range(8):
                s = arrived(pe, ("g", j))
                for m in range(2):
                    i = project_T(("g", 2 * j + m), s, P * m, hT)
                used_last(pe, i, ("g", j))
            rms_turn("mT", lambda t: (xn_ready, NT + t + 1), 2)
            for t in range(2):
                for half in range(2):
                    pe.wait_ge(free(("mT", t, half)), count(("mT", t, half)))
            for w in ("xk", "xv"):
                for j in range(2):
                    arrived(pe, (w, j))
                    for t in range(2):
                        i = project((w, t, j), (w, j), t, memT)
                    used_last(pe, i, (w, j))
            for g in range(4):
                pe.wait_ge(free(("mo", g)), count(("mo", g)))
            for j in range(2):
                for w, src in (("w_o_fox", foxT), ("w_o_mla", mlaT)):
                    arrived(pe, (w, j))
                for n in range(4):
                    for w, src in (("w_o_fox", foxT), ("w_o_mla", mlaT)):
                        s = place[(w, j)] % NRING
                        key = (w, 4 * j + n)
                        ps = open_bank(pe, key)
                        for k in range(4):
                            i = mm(ps[:, 0:TOK], kview(s, 4, 512)[:, k, P * n:P * n + P], src[:, k, :], k == 0, k == 3)
                        done(i, key)
                        if n == 3:
                            used_last(pe, i, (w, j))
            for t in range(2):
                for j in range(2):
                    pe.wait_ge(free(("xk", t, j)), count(("xk", t, j)))
            for h in range(XH):
                ps = open_bank(pe, ("mkT", h))
                for t in range(2):
                    i = pe.transpose(ps[:, P * t:P * t + P], mk[:, t, P * h:P * h + P], ident)
                done(i, ("mkT", h))
            pe.wait_ge(mix_ready, KD)
            for j in range(4):
                arrived(pe, ("out", j))
                for t in range(NT):
                    i = project(("out", t, j), ("out", j), t, hT)
                used_last(pe, i, ("out", j))
            rms_turn("xT", lambda t: (xn_ready, NT + 2 + t + 1), NT)
            for t in range(NT):
                for half in range(2):
                    pe.wait_ge(free(("xT", t, half)), count(("xT", t, half)))
            for j in range(2):
                s = arrived(pe, ("xq", j))
                for m in range(2):
                    i = project_T(("xq", 2 * j + m), s, P * m, hT)
                used_last(pe, i, ("xq", j))
            for h in range(XH):
                pe.wait_ge(free(("xq", h)), count(("xq", h)))
                pe.wait_ge(free(("mkT", h)), count(("mkT", h)))
            for t in range(2):
                for j in range(2):
                    pe.wait_ge(free(("xv", t, j)), count(("xv", t, j)))
            pipeline(XUNITS, U_MEM)

            def mem_turn(b):
                s = arrived(pe, ("cm", b))
                k3 = kview(s, 2, FW)
                for hh in range(2):
                    ps = open_bank(pe, ("cK", b, hh))
                    for h in range(2):
                        for k in range(2):
                            i = pe.transpose(ps[:, 256 * h + P * k:256 * h + P * k + P],
                                             k3[:, k, P * (2 * hh + h):P * (2 * hh + h) + P], ident)
                    done(i, ("cK", b, hh))

            def mem_scores(b):
                for hh in range(2):
                    pe.wait_ge(free(("cK", b, hh)), count(("cK", b, hh)))
                if b == 0:
                    pe.wait_ge(pairs_ready, 2)
                ps = open_bank(pe, ("cS", b))
                for h in range(XH):
                    i = mm(ps[32 * h:32 * h + 32, 0:MEM], xpair[:, b, h, :], xkT[b % 2][:, h, :], True, True)
                done(i, ("cS", b))

            def mem_probs(b):
                pe.wait_ge(prob_ready, U_SMEM + b + 1)
                ps = open_bank(pe, ("cT", b))
                for k in range(2):
                    i = pe.transpose(ps[:, P * k:P * k + P], prob[b % 4][:, P * k:P * k + P], ident)
                done(i, ("cT", b))

            def mem_values(b):
                pe.wait_ge(free(("cT", b)), count(("cT", b)))
                s = place[("cm", b)] % NRING
                v3 = ring[:, s, 1024:2048].rearrange("p (k n) -> p k n", k=2)
                ps = open_bank(pe, ("cV", b))
                for h in range(XH):
                    for k in range(2):
                        i = mm(ps[:, NQ * h:NQ * h + NQ], v3[:, k, P * h:P * h + P],
                               probT[b % 4][:, P * k + 32 * h:P * k + 32 * h + NQ], h == 0 and k == 0, k == 1)
                done(i, ("cV", b))
                used_last(pe, i, ("cm", b))

            mem_turn(0)
            for b in range(NB + 1):
                if b < NB:
                    mem_scores(b)
                if b + 1 < NB:
                    mem_turn(b + 1)
                if b >= 1:
                    mem_probs(b - 1)
                    mem_values(b - 1)
            pe.wait_ge(free(("cV", NB - 1)), count(("cV", NB - 1)))
            for j in range(2):
                s = arrived(pe, ("xo", j))
                for t in range(NT):
                    ps = open_bank(pe, ("xo", t, j))
                    for k in range(4):
                        i = mm(ps[:, :], xoT[:, k, P * t:P * t + P], kview(s, 4, 512)[:, k, :], k == 0, k == 3)
                    done(i, ("xo", t, j))
                used_last(pe, i, ("xo", j))
            rms_turn("rT", lambda t: (xn_ready, 2 * NT + 2 + t + 1), NT)
            for t in range(NT):
                for half in range(2):
                    pe.wait_ge(free(("rT", t, half)), count(("rT", t, half)))
                ps = open_bank(pe, ("lg", t))
                for k in range(KD):
                    i = mm(ps[:, 0:NE], hT[:, k, P * t:P * t + P], wr[:, k, :], k == 0, k == KD - 1)
                done(i, ("lg", t))
            pe.wait_ge(masks_ready, 1)
            ps = open_bank(pe, "rank")
            first = True
            for t in range(NT):
                mm(ps[:, NE * t:NE * t + NE], con[:, t0:t0 + P], chosen[:, t, :], first, t == 0)
                first = False
                for s in range(t):
                    mm(ps[:, NE * t:NE * t + NE], ones, chosen[:, s, :], False, s == t - 1)
            for t in range(NT):
                i = mm(ps[:, 96:128], ones, chosen[:, t, :], False, t == NT - 1)
            done(i, "rank")
            pe.wait_ge(pick_ready, 1)
            ps = open_bank(pe, "index")
            for n in range(NT * TOPK):
                i = mm(ps[0:CAP, 0:NBLK], pick[:, n, :], blk1[:, n, :], n == 0, n == NT * TOPK - 1)
            done(i, "index")
            for key in list(groups)[-8:]:
                pe.wait_ge(free(key), count(key))

            gate, up, xTp, aTp, yp = psum[0], psum[1], psum[2], psum[3], psum[4]

            def turn_rows():
                for k in range(KD):
                    i = pe.transpose(xTp[:, CAP * k:CAP * k + CAP], xg[:, P * k:P * k + P], ident[0:CAP, 0:CAP])
                i.then_inc(xT_full, 1)

            pe.wait_ge(blocks_ready, 1)
            nblk = pe.value_load(blocks_i[0:1, 0:1], min_val=NE, max_val=NBLK)
            pe.wait_ge(bias_moved, 96)
            pe.wait_ge(rows_gathered, 16)
            turn_rows()
            with pe.Fori(0, nblk) as b:
                pe.wait_ge(xT_ready, b + 1)
                for half in range(2):
                    o = slice(CAP * half, CAP * half + CAP)
                    mm(gate[o, :], sel, bias3[:, 512 * half:512 * half + 512], True, False)
                    mm(up[o, :], sel, bias3[:, 1024 + 512 * half:1536 + 512 * half], True, False)
                for c in range(KD):
                    s = GU_SLOT[c]
                    pe.wait_ge(ring_loaded[s], b * 16 + (GU_LOADS[c] + 16))
                    for q in range(4):
                        o = (gate, up)[q // 2][CAP * (q % 2):CAP * (q % 2) + CAP, :]
                        i = mm(o, xT[:, c, :], ring[:, s, 512 * q:512 * q + 512], False, c == KD - 1)
                    i.then_inc(ring_used[s], 1)
                pe.wait_ge(y_copied, b + 1)
                pe.wait_ge(rows_gathered, b * 16 + 32)
                for half in range(2):
                    mm(yp[CAP * half:CAP * half + CAP, :], sel, bias3[:, 2048 + 512 * half:2560 + 512 * half], True, False)
                turn_rows()
                pe.wait_ge(act_ready, b + 1)
                for k in range(4):
                    i = pe.transpose(aTp[:, P * k:P * k + P], hid[:, P * k:P * k + P], ident)
                i.then_inc(actT_full, 1)
                pe.wait_ge(actT_ready, b + 1)
                for c in range(KD):
                    s = DOWN_SLOT[c // 2]
                    if c % 2 == 0:
                        pe.wait_ge(ring_loaded[s], b * 16 + 16)
                    l = actT[:, 2 * (c % 4) + c // 4, :]
                    for half in range(2):
                        a = 1024 * (c % 2) + 512 * half
                        i = mm(yp[CAP * half:CAP * half + CAP, :], l, ring[:, s, a:a + 512], False, c == KD - 1)
                    if c % 2:
                        i.then_inc(ring_used[s], 1)

        @block.sync
        def _(sp):
            for t in range(NT):
                src = d["x_prompt"][0, P * t:P * t + P, :] if t < 2 else d["x_sample"].rearrange("b q n -> (b q) n")
                sp.dma_start(xr[:, t, :], src).then_inc(x_loaded[t], 16)
            for n, (key, parts) in enumerate(stream):
                if n >= NRING:
                    g = last_group[stream[n - NRING][0]]
                    sp.wait_ge(bank_full[g % 8], g // 8 + 1)
                for dst, src in parts:
                    sp.dma_start(dst(n % NRING), src).then_inc(ring_loaded[n % NRING], 16)
            w_gu = d["w_gu"][0].rearrange("e (k p) n -> e p k n", p=P)
            w_down = d["w_down"][0].rearrange("e (k p) n -> e p k n", p=P)

            def load_in(expert, c):
                sp.dma_start(ring[:, GU_SLOT[c], :], w_gu[expert, :, c, :]).then_inc(ring_loaded[GU_SLOT[c]], 16)

            def load_down(expert, c):
                sp.dma_start(kview(DOWN_SLOT[c], 2, D), w_down[expert, :, 2 * c:2 * c + 2, :])\
                    .then_inc(ring_loaded[DOWN_SLOT[c]], 16)

            for c in range(KD):
                g = last_group[stream[NPRE + c - NRING][0]]
                sp.wait_ge(bank_full[g % 8], g // 8 + 1)
                load_in(0, c)
            sp.wait_ge(bias_moved, 96)
            sp.wait_ge(full(("cT", NB - 1)), count(("cT", NB - 1)))
            sp.wait_ge(full(("rT", 2, 1)), count(("rT", 2, 1)))
            sp.wait_ge(scratch_written, 16)
            for c in range(4):
                load_down(0, c)

            def block_loads(expert, b):
                for c in range(KD):
                    sp.wait_ge(ring_used[GU_SLOT[c]], b)
                    load_in(expert, c)
                for c in range(4):
                    sp.wait_ge(ring_used[DOWN_SLOT[c]], b)
                    load_down(expert, c)

            with sp.Fori(1, NE) as b:
                block_loads(b, b)
            sp.wait_ge(blocks_ready, 1)
            nblk = sp.value_load(blocks_i[0:1, 0:1], min_val=NE, max_val=NBLK)
            with sp.If(nblk > NE):
                with sp.Fori(NE, nblk) as b:
                    expert = sp.value_load(bexp_i[0:1, bass.ds(b, 1)], min_val=0, max_val=NE - 1)
                    block_loads(expert, b)
            for t in range(NT):
                sp.wait_ge(fin_ready, t + 1)
                dst = out["y_prompt"][0, P * t:P * t + P, :] if t < 2 else out["y_sample"].rearrange("b q n -> (b q) n")
                sp.dma_start(dst, yout[:, t, :]).then_inc(y_out, 16)
            sp.wait_ge(y_out, 16 * NT)

        @block.gpsimd
        def _(pool):
            def rows3(name, width):
                a = out["p_" + name]
                b = out["s_" + name]
                pa = a.rearrange("l b (t p) h n -> p (l b t) (h n)" if len(a.shape) == 5 else "l b (t p) n -> p (l b t) n", p=P)
                sa = b.rearrange("l b q h n -> (l b q) (h n)" if len(b.shape) == 5 else "l b q n -> (l b q) n")
                return pa, sa

            def put(name, tile3, s):
                pa, sa = rows3(name, 0)
                pool.dma_start(pa, tile3[:, 0:2, :]).then_inc(s, 16)
                pool.dma_start(sa, tile3[:, 2, :]).then_inc(s, 16)

            pool.wait_ge(free(("fk", 2, 1)), count(("fk", 2, 1)))
            put("fox_k", fk, fk_written)
            pool.wait_ge(krope_ready, NT)
            put("mla_krope", krope, outputs_written)
            pool.wait_ge(ckv_ready, NT)
            put("mla_ckv", ckv, ckv_written)
            pool.wait_ge(logf_ready, NT)
            put("fox_logf", logf, outputs_written)
            pool.wait_ge(free(("fv", 2, 1)), count(("fv", 2, 1)))
            put("fox_v", fv, fv_written)
            pool.wait_ge(full(("sS", SU - 1)), count(("sS", SU - 1)))
            pool.wait_ge(full(("mo", 3)), count(("mo", 3)))
            pool.dma_start(memx, d["mem_prompt"].rearrange("b (t p) n -> p (b t) n", p=P)).then_inc(mem_loaded, 16)
            pool.dma_start(xr[:, 0:2, :], d["x_prompt"].rearrange("b (t p) n -> p (b t) n", p=P)).then_inc(x_again, 16)
            pool.dma_start(xr[:, 2, :], d["x_sample"].rearrange("b q n -> (b q) n")).then_inc(x_again, 16)
            for w, m, o in (("xk", mk, "p_mem_k"), ("xv", mv, "p_mem_v")):
                pool.wait_ge(free((w, 1, 1)), count((w, 1, 1)))
                pool.dma_start(out[o].rearrange("l b (t p) h n -> p (l b t) (h n)", p=P), m).then_inc(mk_written, 16)
            pool.wait_ge(mix_ready, KD)
            pool.wait_ge(ckv_written, 32)
            for c in range(3):
                src = d["b_gu"][0, :, 1024 * c:1024 * c + 1024] if c < 2 else d["b_down"][0]
                pool.dma_start(bstage, src).then_inc(bias_loaded, 16)
                pool.wait_ge(bias_loaded, 16 * c + 16)
                o = slice(1024 * c, 1024 * c + 1024)
                nc.gpsimd.tensor_copy(bias3[0:NE, o], bstage).then_inc(bias_step, 1)
                pool.wait_ge(bias_step, 5 * c + 1)
                nc.gpsimd.tensor_tensor(bstage, bstage, bias3[0:NE, o], ALU.subtract).then_inc(bias_step, 1)
                pool.wait_ge(bias_step, 5 * c + 2)
                nc.gpsimd.tensor_copy(bmid, bstage).then_inc(bias_step, 1)
                pool.wait_ge(bias_step, 5 * c + 3)
                pool.dma_start(bias3[32:64, o], bmid).then_inc(bias_moved, 16)
                nc.gpsimd.tensor_tensor(bstage, bstage, bmid, ALU.subtract).then_inc(bias_step, 1)
                pool.wait_ge(bias_moved, 32 * c + 16)
                pool.wait_ge(bias_step, 5 * c + 4)
                nc.gpsimd.tensor_copy(bmid, bstage).then_inc(bias_step, 1)
                pool.wait_ge(bias_step, 5 * c + 5)
                pool.dma_start(bias3[64:96, o], bmid).then_inc(bias_moved, 16)
                pool.wait_ge(bias_moved, 32 * c + 32)
            for t in range(NT):
                pool.wait_ge(xn_ready, 2 * NT + 2 + t + 1)
            pool.dma_start(x3_dram.rearrange("(t p) n -> p t n", p=P), xn2).then_inc(scratch_written, 16)
            pool.wait_ge(idx_ready, 1)
            pool.wait_ge(blocks_ready, 1)
            pool.wait_ge(scratch_written, 16)
            nblk = pool.value_load(blocks_i[0:1, 0:1], min_val=NE, max_val=NBLK)

            def gather(n, copied, copies):
                nc.gpsimd.tensor_copy(idx_col[:, :], idx_all[:, bass.ds(n, 1)]).then_inc(copied, 1)
                pool.wait_ge(blocks_ready, 1)
                pool.wait_ge(copied, copies)
                pool.indirect_dma_start(out=xg, out_offset=None, in_=x3_dram,
                                        in_offset=bass.IndirectOffsetOnAxis(ap=idx_col[:, 0:1], axis=0))\
                    .then_inc(rows_gathered, 16)

            gather(0, first_copied, 1)
            with pool.Fori(1, nblk + 1) as n:
                pool.wait_ge(rows_gathered, n * 16)
                pool.wait_ge(xT_full, n)
                gather(n, idx_copied, n)
            pool.wait_ge(first_rows, 1)
            for n in range(NT * TOPK):
                if n >= 4:
                    pool.wait_ge(y_added, n - 3)
                pool.indirect_dma_start(out=ygs[n % 4], out_offset=None, in_=y_dram,
                                        in_offset=bass.IndirectOffsetOnAxis(ap=slot_cols[n], axis=0))\
                    .then_inc(y_gathered[n % 4], 16)
            pool.wait_ge(outputs_written, 64)
            pool.wait_ge(fk_written, 32)
            pool.wait_ge(fv_written, 32)
            pool.wait_ge(mk_written, 32)

        def softmax_cols(u):
            a = 10 * (u % 4)
            return cols[:, a:a + 2], cols[:, a + 2:a + 4], cols[:, a + 4:a + 6], cols[:, a + 6:a + 8], cols[:, a + 8:a + 9]

        ssq = cols[:, 40:54]
        lz, lneg, lexp, lln = (probTs[:, 1536 + 24 * i:1560 + 24 * i].rearrange("p (t h) -> p t h", t=NT) for i in range(4))
        rtmp = probTs[:, 1024:1536].rearrange("p (a h r) -> p a h r", a=4, h=H)
        rstd = sb("rstd", [P, 32])
        nrt = rstd[:, 24:32]
        btmp = [probTs[:, TOK * i:TOK * i + TOK] for i in range(2)]

        def turn_key(u):
            return ("T", u) if u < U_SMEM else ("cT", u - U_SMEM)

        @block.vector
        def _(dve):
            v = nc.vector
            steps = [0]

            def link(ins):
                steps[0] += 1
                ins.then_inc(dve_step, 1)
                dve.wait_ge(dve_step, steps[0])

            def take(key):
                dve.wait_ge(full(key), count(key))
                return bank(key)

            def give(ins, key):
                ins.then_inc(free(key), 1)

            def inverse_root(y, square, width):
                n = y.shape[1]
                x, w = nrt[:, 0:n], nrt[:, 4:4 + n]
                link(v.tensor_scalar(x, square, 1.0 / width, EPS, ALU.mult, ALU.add))
                link(v.tensor_scalar(y.bitcast(I32), x.bitcast(I32), 1, None, ALU.logical_shift_right))
                link(v.tensor_scalar(y.bitcast(I32), y.bitcast(I32), -1.0, float(0x5F3759DF), ALU.mult, ALU.add))
                link(v.tensor_scalar(x, x, -0.5, None, ALU.mult))
                for _ in range(3):
                    link(v.tensor_tensor(w, y, y, ALU.mult))
                    link(v.tensor_tensor(w, w, x, ALU.mult))
                    link(v.scalar_tensor_tensor(y, w, 1.5, y, ALU.add, ALU.mult))

            def rms_rows(n, tiles, src, dst):
                dve.wait_ge(square_sum, n + tiles)
                inverse_root(rstd[:, n:n + tiles], ssq[:, n:n + tiles], D)
                for t in range(tiles):
                    v.tensor_scalar(dst[:, t, :], src[:, t, :], rstd[:, n + t:n + t + 1], None, ALU.mult).then_inc(xn_ready, 1)

            def scale_turned(name, t, g, dst):
                for half in range(2):
                    ps = take((name, t, half))
                    give(v.tensor_tensor(dst[:, 4 * half:4 * half + 4, P * t:P * t + P],
                                         ps[:, :].rearrange("p (c q) -> p c q", c=4),
                                         bc(g[:, 4 * half:4 * half + 4].unsqueeze(2), [P, 4, P]), ALU.mult), (name, t, half))

            def copy_out(key, dst, n=None):
                ps = take(key)
                give(v.tensor_copy(dst, ps[:, 0:n] if n else ps), key)

            def rope(src, dst, t, heads, signal, key):
                h2 = ROPE // 2
                c, s = (bc(cc(n)[:, h2 * t:h2 * t + h2].unsqueeze(1), [P, heads, h2]) for n in ("cos", "sin"))
                x1, x2 = src[:, :, 0:h2], src[:, :, h2:ROPE]
                a = [rtmp[:, n, 0:heads, :] for n in range(4)]
                if t:
                    dve.wait_ge(signal, t)
                v.tensor_tensor(a[0], x1, c, ALU.mult)
                v.tensor_tensor(a[1], x2, s, ALU.mult)
                v.tensor_tensor(a[2], x2, c, ALU.mult)
                give(v.tensor_tensor(a[3], x1, s, ALU.mult), key)
                dve.wait_ge(free(key), count(key))
                link(v.tensor_tensor(dst[:, :, 0:h2], a[0], a[1], ALU.subtract))
                v.tensor_tensor(dst[:, :, h2:ROPE], a[2], a[3], ALU.add).then_inc(signal, 1)

            dve.wait_ge(consts_loaded, 16 * NLOADS)
            rms_rows(0, NT, xr, xr)
            for t in range(NT):
                scale_turned("hT", t, gm_c, hT)
            v.memset(xflat[:, 0:1024], 0.0).then_inc(zeroed, 1)
            for j in range(2):
                for t in range(NT):
                    copy_out(("fk", t, j), fk[:, t, 256 * j:256 * j + 256], 256)
            for t in range(NT):
                ps = take(("fl", t))
                link(v.tensor_tensor(lz[:, t, :], ps[:, 0:H], bf_b, ALU.add))
                link(v.tensor_scalar(lneg[:, t, :], lz[:, t, :], -1.0, None, ALU.mult))
                v.tensor_tensor(lneg[:, t, :], lz[:, t, :], lneg[:, t, :], ALU.min).then_inc(logf_part, 1)
                rope(ps[:, H:H + ROPE].unsqueeze(1), krope[:, t:t + 1, :], t, 1, krope_ready, ("fl", t))
            for name, rows, c0 in (("kv", ckv, 54), ("qc", qc, 57)):
                for t in range(NT):
                    copy_out((name, t), rows[:, t, :], 256)
                    dve.wait_ge(free((name, t)), count((name, t)))
                    last = v.tensor_tensor_reduce(junk2, rows[:, t, :], rows[:, t, :], 1.0, 0.0, ALU.mult, ALU.add, cols[:, c0 + t:c0 + t + 1])
                link(last)
                a = 14 if name == "kv" else 17
                inverse_root(rstd[:, a:a + NT], cols[:, c0:c0 + NT], LORA)
                for t in range(NT):
                    if name == "kv":
                        v.scalar_tensor_tensor(ckv[:, t, :], ckv[:, t, :], rstd[:, a + t:a + t + 1], gkv_b[:, :], ALU.mult, ALU.mult)\
                            .then_inc(ckv_ready, 1)
                    else:
                        v.tensor_scalar(qc[:, t, :], qc[:, t, :], rstd[:, a + t:a + t + 1], None, ALU.mult).then_inc(qc_ready, 1)
            for t in range(NT):
                dve.wait_ge(logit_exp, t + 1)
                v.scalar_tensor_tensor(logf[:, t, :], lz[:, t, :], 0.0, lln[:, t, :], ALU.min, ALU.subtract).then_inc(logf_ready, 1)
            dve.wait_ge(logf_ready, NT)
            v.tensor_copy(logfw.rearrange("p (b h) -> p b h", b=NB), bc(logf[:, 2:3, :], [P, NB, H])).then_inc(logf_wide, 1)
            for c in range(2):
                ps = take(("qcT", c))
                give(v.tensor_scalar(qcT[:, c, :], ps[:, 0:TOK], gq_c[:, c:c + 1], None, ALU.mult), ("qcT", c))
            ps = take("cumP")
            v.tensor_copy(cumT[0:H, :], ps[0:H, 0:256])
            give(v.tensor_copy(cumT[64:64 + H, :], ps[0:H, 0:256]), "cumP")
            ps = take("cumS")
            give(v.tensor_copy(cumS[:, 0:512], ps[0:64, :]), "cumS")
            ps = take("cumN")
            give(v.tensor_copy(cumS[:, 512:640], ps[0:64, 0:P]), "cumN")
            for t in range(NT):
                ps = take(("qr", t))
                rope(ps[:, 0:256].rearrange("p (h r) -> p h r", r=ROPE), qrope[:, t, :, :], t, H, qrope_ready, ("qr", t))
            for h in range(H):
                ps = take(("ql", h, 0))
                v.tensor_copy(ql[:, 0, h, :], ps[:, 0:256])
                give(v.tensor_copy(qs[:, 0, :, h, :], ps[:, 256:TOK].rearrange("p (b q) -> p b q", q=NQ)), ("ql", h, 0))
            dve.wait_ge(zeroed, 1)
            dve.wait_ge(free(("fqT", 3)), count(("fqT", 3)))
            dve.wait_ge(free(("qrT", 1)), count(("qrT", 1)))
            a8 = CONST["neg8"][0]
            v.tensor_copy(sel8.rearrange("p b (h q) -> p (b h) q", h=H), bc(con[64:128, a8:a8 + 64].unsqueeze(2), [64, 64, NQ]))
            for e in range(2):
                v.tensor_copy(qpair[64 * e:64 * e + 64, :, :, NQ * e:NQ * e + NQ],
                              fqT[64 * e:64 * e + 64, :, 256:384].rearrange("p g (b q) -> p b g q", q=NQ))
            for e in range(4):
                for c in range(2):
                    last = v.tensor_copy(qrS[:, :, 4 * c + e, :],
                                         qrT[32 * e:32 * e + 32, c, 256:384].rearrange("p (b q) -> p b q", q=NQ))
            last.then_inc(pairs_ready, 1)

            def part1(u, unit):
                kind, t, hs = unit
                w = width(kind, t)
                mx, nm, sm, rc, _ = softmax_cols(u)
                ps = take(("S", u))
                src = ps[:, 0:2 * w].rearrange("p (n w) -> p n w", n=2)
                if kind != "mem":
                    if u >= 4:
                        dve.wait_ge(full(("T", u - 4)), count(("T", u - 4)))
                    a = CONST["z1" if kind == "fox" else "z2"][0]
                    mask = con[:, a + P * (1 - t):a + 2 * P]
                    dst = prob[u % 4][:, 0:2 * w].rearrange("p (n w) -> p n w", n=2)
                    give(v.tensor_tensor(dst, src, bc(mask.unsqueeze(1), [P, 2, w]), ALU.add), ("S", u))
                    dve.wait_ge(free(("S", u)), count(("S", u)))
                    src = dst
                link(v.tensor_reduce(mx, src, X, ALU.max))
                v.tensor_scalar(nm, mx, -{"fox": FOX_SCALE, "mla": MLA_SCALE, "mem": X_SCALE}[kind], None, ALU.mult)\
                    .then_inc(score_max, 1)

            def part2(u, unit):
                kind, t, hs = unit
                w = width(kind, t)
                mx, nm, sm, rc, _ = softmax_cols(u)
                dve.wait_ge(exp_done, u + 1)
                link(v.reciprocal(rc, sm))
                dst = prob[u % 4][:, 0:2 * w].rearrange("p (n w) -> p n w", n=2)
                v.tensor_tensor(dst, dst, bc(rc.unsqueeze(2), [P, 2, w]), ALU.mult).then_inc(prob_ready, 1)

            def pipeline(units, u0):
                for i in range(len(units) + 1):
                    if i < len(units):
                        part1(u0 + i, units[i])
                    if i:
                        part2(u0 + i - 1, units[i - 1])

            pipeline(UNITS, 0)

            def sample_part1(n):
                b, u = n // 2, U_SAMPLE + n
                mx, nm, sm, rc, m1 = softmax_cols(u)
                p = sprob[n % 3]
                new = take(("sN", b))
                if n >= 3:
                    dve.wait_ge(full(("sTn", n - 3)), count(("sTn", n - 3)))
                a = CONST["mlanew" if n % 2 else "foxnew"][0] + NQ * (7 - b)
                i = v.tensor_tensor(p[:, 512:640], new[:, P * (n % 2):P * (n % 2) + P], con[:, a:a + P], ALU.add)
                if n % 2:
                    give(i, ("sN", b))
                    dve.wait_ge(free(("sN", b)), count(("sN", b)))
                else:
                    link(i)
                ps = take(("sS", n))
                v.tensor_reduce(mx[:, 0:1], ps[:, :], X, ALU.max)
                link(v.tensor_reduce(mx[:, 1:2], p[:, 512:640], X, ALU.max))
                link(v.tensor_reduce(m1, mx, X, ALU.max))
                v.tensor_scalar(nm[:, 0:1], m1, -(MLA_SCALE if n % 2 else FOX_SCALE), None, ALU.mult).then_inc(score_max, 1)

            def sample_part2(n):
                u = U_SAMPLE + n
                mx, nm, sm, rc, m1 = softmax_cols(u)
                dve.wait_ge(exp_done, u + 1)
                link(v.tensor_tensor(rc[:, 0:1], sm[:, 0:1], sm[:, 1:2], ALU.add))
                link(v.reciprocal(rc[:, 1:2], rc[:, 0:1]))
                v.tensor_scalar(sprob[n % 3], sprob[n % 3], rc[:, 1:2], None, ALU.mult).then_inc(prob_ready, 1)

            def cache_out(b):
                if b >= 2:
                    dve.wait_ge(full(("sS", 2 * b - 3)), count(("sS", 2 * b - 3)))
                for g in range(2):
                    copy_out(("skT", b, g), skT[b % 2][:, g, :])
                copy_out(("scT", b, 0), scT[b % 2][:, 0, :])

            dve.wait_ge(fk_written, 32)
            cache_out(0)
            for b in range(NB):
                sample_part1(2 * b)
                sample_part1(2 * b + 1)
                if b + 1 < NB:
                    cache_out(b + 1)
                sample_part2(2 * b)
                sample_part2(2 * b + 1)
            dve.wait_ge(mem_loaded, 16)
            rms_rows(NT, 2, memx, memx)
            for t in range(2):
                scale_turned("mT", t, gmem_c, memT)
            for n in range(KD):
                ps = take(("w_o_fox", n))
                dve.wait_ge(gates_ready, KD + n + 1)
                give(v.tensor_tensor(hT[:, n, :], ps[:, 0:TOK], gates[:, n, :], ALU.mult), ("w_o_fox", n))
                ps = take(("w_o_mla", n))
                if n >= 2:
                    dve.wait_ge(mix_ready, n - 1)
                give(v.tensor_tensor(btmp[n % 2], ps[:, 0:TOK], gates[:, KD + n, :], ALU.mult), ("w_o_mla", n))
                dve.wait_ge(free(("w_o_mla", n)), count(("w_o_mla", n)))
                v.tensor_tensor(hT[:, n, :], hT[:, n, :], btmp[n % 2], ALU.add).then_inc(mix_ready, 1)
            dve.wait_ge(x_again, 32)
            for j in range(4):
                for t in range(NT):
                    ps = take(("out", t, j))
                    o = xr[:, t, 256 * j:256 * j + 256]
                    give(v.tensor_tensor(o, o, ps[:, 0:256], ALU.add), ("out", t, j))
            rms_rows(NT + 2, NT, xr, xn2)
            for t in range(NT):
                scale_turned("xT", t, gx_c, hT)
            dve.wait_ge(fv_written, 32)
            link(v.memset(xpair, 0.0))
            dve.wait_ge(free(("xq", 3)), count(("xq", 3)))
            v.tensor_copy(xpair[:, :, :, 0:NQ], xqT[:, :, 256:384].rearrange("p h (b q) -> p b h q", q=NQ)).then_inc(pairs_ready, 1)
            pipeline(XUNITS, U_MEM)

            def mem_part1(b):
                u = U_SMEM + b
                mx, nm, sm, rc, _ = softmax_cols(u)
                ps = take(("cS", b))
                link(v.tensor_reduce(mx[:, 0:1], ps[:, 0:MEM], X, ALU.max))
                v.tensor_scalar(nm[:, 0:1], mx[:, 0:1], -X_SCALE, None, ALU.mult).then_inc(score_max, 1)

            def mem_part2(b):
                u = U_SMEM + b
                mx, nm, sm, rc, _ = softmax_cols(u)
                dve.wait_ge(exp_done, u + 1)
                link(v.reciprocal(rc[:, 0:1], sm[:, 0:1]))
                p = prob[b % 4][:, 0:MEM]
                v.tensor_scalar(p, p, rc[:, 0:1], None, ALU.mult).then_inc(prob_ready, 1)

            def mem_out(b):
                if b >= 2:
                    dve.wait_ge(full(("cS", b - 2)), count(("cS", b - 2)))
                ps = take(("cK", b, 0))
                give(v.tensor_copy(xkT[b % 2][:, 0:2, :], ps[:, :].rearrange("p (h s) -> p h s", h=2)), ("cK", b, 0))

            mem_out(0)
            for b in range(NB):
                mem_part1(b)
                if b + 1 < NB:
                    mem_out(b + 1)
                mem_part2(b)
            for j in range(2):
                for t in range(NT):
                    ps = take(("xo", t, j))
                    o = xr[:, t, 512 * j:512 * j + 512]
                    give(v.tensor_tensor(o, o, ps[:, :], ALU.add), ("xo", t, j))
            rms_rows(2 * NT + 2, NT, xr, xn2)
            for t in range(NT):
                scale_turned("rT", t, gf_c, hT)

            iota32 = cc("iota")[:, 0:NE]
            for t in range(NT):
                ps = take(("lg", t))
                give(v.tensor_tensor(logit[:, t, :], ps[:, 0:NE], br_b, ALU.add), ("lg", t))
                dve.wait_ge(free(("lg", t)), count(("lg", t)))
                link(v.max(top8[:, t, :], logit[:, t, :]))
                link(v.max_index(idx8[:, t, :], top8[:, t, :], logit[:, t, :]))
                link(v.tensor_copy(idxf[:, t, :], idx8[:, t, :]))
                v.tensor_scalar(ntop[:, t:t + 1], top8[:, t, 0:1], -1.0, None, ALU.mult).then_inc(top_shift, 1)
                for k in range(TOPK):
                    last = v.tensor_scalar(onehot[:, 4 * t + k, :], iota32, idxf[:, t, k:k + 1], None, ALU.is_equal)
                link(last)
                last = v.tensor_reduce(chosen[:, t, :], onehot[:, 4 * t:4 * t + 4, :].rearrange("p k e -> p e k"), X, ALU.add)
                if t < NT - 1:
                    link(last)
            last.then_inc(masks_ready, 1)
            for t in range(NT):
                dve.wait_ge(top_exp, t + 1)
                link(v.reciprocal(esum[:, t:t + 1], esum[:, t:t + 1]))
                link(v.tensor_scalar(gatew[:, 4 * t:4 * t + 4], top8[:, t, 0:TOPK], esum[:, t:t + 1], None, ALU.mult))
            ps = take("rank")
            link(v.tensor_copy(cnt, ps[:, 96:128]))
            link(v.tensor_scalar(novr, cnt, float(CAP), None, ALU.is_gt))
            for n in range(2, TOK // CAP):
                link(v.scalar_tensor_tensor(novr, cnt, float(CAP * n), novr, ALU.is_gt, ALU.add))
            link(v.tensor_tensor_scan(oincl, novr, cc("zero"), 0.0, ALU.add, ALU.add))
            link(v.tensor_tensor(moved, oincl, novr, ALU.subtract))
            link(v.tensor_scalar(moved, moved, float(CAP), float(CAP * (NE - 1)), ALU.mult, ALU.add))
            link(v.tensor_tensor(moved, moved, cc("i64")[:, 0:NE], ALU.subtract))
            rank = ps[:, 0:96].rearrange("p (t e) -> p t e", t=NT)
            link(v.tensor_scalar(slot_d, rank, float(CAP), None, ALU.is_ge))
            link(v.tensor_tensor(slot_d, slot_d, bc(moved.unsqueeze(1), [P, NT, NE]), ALU.mult))
            link(v.tensor_tensor(slot_d, slot_d, bc(cc("i64")[:, 0:NE].unsqueeze(1), [P, NT, NE]), ALU.add))
            give(v.tensor_tensor(slot_e, slot_d, rank, ALU.add), "rank")
            dve.wait_ge(free("rank"), count("rank"))
            for t in range(NT):
                last = v.tensor_tensor(e_tmp[:, 4 * t:4 * t + 4, :], onehot[:, 4 * t:4 * t + 4, :],
                                       bc(slot_e[:, t:t + 1, :], [P, TOPK, NE]), ALU.mult)
            link(last)
            link(v.tensor_reduce(slotf, e_tmp, X, ALU.add))
            for n in range(1, NT * TOPK):
                last = v.tensor_copy(slot_cols[n], slotf[:, n:n + 1])
            link(last)
            n12 = NT * TOPK
            link(v.tensor_tensor(dist, bc(slotf.unsqueeze(2), [P, n12, NBLK]), bc(cc("i64")[:, 0:NBLK].unsqueeze(1), [P, n12, NBLK]), ALU.subtract))
            link(v.tensor_scalar(blk1, dist, 0.0, None, ALU.is_ge))
            link(v.scalar_tensor_tensor(blk1, dist, float(CAP), blk1, ALU.is_lt, ALU.mult))
            link(v.tensor_tensor(dist, dist, blk1, ALU.mult))
            link(v.tensor_reduce(inblk, dist, X, ALU.add))
            for n in range(n12):
                last = v.tensor_scalar(pick[:, n, :], cc("iota"), inblk[:, n:n + 1], cc("tokid")[:, n // TOPK:n // TOPK + 1], ALU.is_equal, ALU.mult)
            last.then_inc(pick_ready, 1)
            link(v.tensor_tensor(o_cmp, bc(oincl.unsqueeze(1), [P, OVER, NE]), bc(cc("iota")[:, 0:OVER].unsqueeze(2), [P, OVER, NE]), ALU.is_le))
            link(v.tensor_reduce(bexp[:, NE:NBLK], o_cmp, X, ALU.add))
            link(v.tensor_copy(bexp[:, 0:NE], iota32))
            link(v.memset(bexp[:, NBLK:NBLK + 1], 0.0))
            link(v.tensor_scalar(bexp_i, bexp[0:1, 0:NBLK], float(NE - 1), None, ALU.min))
            v.tensor_scalar(blocks_i[0:1, :], oincl[0:1, NE - 1:NE], float(NE), None, ALU.add).then_inc(blocks_ready, 1)
            dve.wait_ge(mk_written, 32)
            link(v.memset(idx_all[:, NBLK:NBLK + 1], 0))
            ps = take("index")
            give(v.tensor_copy(idx_all[:, 0:NBLK], ps[0:CAP, 0:NBLK]), "index")
            dve.wait_ge(free("index"), count("index"))
            v.nop().then_inc(idx_ready, 1)

            gate, up, xTp = psum[0], psum[1], psum[2]

            def xT_out(n):
                dve.wait_ge(xT_full, n)
                v.tensor_tensor(xT, xTp[:, :].rearrange("p (k t) -> p k t", k=KD), bc(gf_c.unsqueeze(2), [P, KD, CAP]), ALU.mult)\
                    .then_inc(xT_ready, 1)

            def choose(dst, b):
                return v.tensor_scalar(dst, bc(cc("pmod", 96), [96, CAP]), bexp[0:96, b], None, ALU.is_equal)

            dve.wait_ge(blocks_ready, 1)
            nblk = dve.value_load(blocks_i[0:1, 0:1], min_val=NE, max_val=NBLK)
            choose(sel, slice(0, 1))
            xT_out(1)
            with dve.Fori(0, nblk) as b:
                dve.wait_ge(ring_used[GU_SLOT[KD - 1]], b + 1)
                v.tensor_scalar(gS, gate[:, :], LIMIT, None, ALU.min).then_inc(gate_clipped, 1)
                v.tensor_scalar(uS, up[:, :], LIMIT, -LIMIT, ALU.min, ALU.max).then_inc(up_clipped, 1)
                dve.wait_ge(gate_clipped, b + 1)
                dve.wait_ge(up_clipped, b + 1)
                v.scalar_tensor_tensor(tS, uS, 1.0, gS, ALU.add, ALU.mult).then_inc(product, 1)
                dve.wait_ge(gate_sig, b + 1)
                dve.wait_ge(product, b + 1)
                v.tensor_tensor(hid, tS, sS, ALU.mult).then_inc(act_ready, 1)
                dve.wait_ge(xT_full, b + 2)
                choose(sel, bass.ds(b + 1, 1))
                v.tensor_tensor(xT, xTp[:, :].rearrange("p (k t) -> p k t", k=KD), bc(gf_c.unsqueeze(2), [P, KD, CAP]), ALU.mult)\
                    .then_inc(xT_ready, 1)
            for n in range(n12):
                dve.wait_ge(y_gathered[n % 4], 16 * (n // 4 + 1))
                if n:
                    dve.wait_ge(y_added, n)
                x = xr[:, n // TOPK, :]
                v.scalar_tensor_tensor(x, ygs[n % 4], gatew[:, n:n + 1], x, ALU.mult, ALU.add).then_inc(y_added, 1)
            dve.wait_ge(gfin_loaded, 16)
            n0 = 3 * NT + 2
            dve.wait_ge(square_sum, n0 + NT)
            inverse_root(rstd[:, n0:n0 + NT], ssq[:, n0:n0 + NT], D)
            for t in range(NT):
                n = n0 + t
                v.scalar_tensor_tensor(yout[:, t, :], xr[:, t, :], rstd[:, n:n + 1], gfin, ALU.mult, ALU.mult).then_inc(fin_ready, 1)

        @block.scalar
        def _(act):
            a = nc.scalar

            def load(dst, src, slow=False):
                act.dma_start(dst, src, allow_slow_non_contiguous=slow).then_inc(consts_loaded, 16)

            def turned(g, k):
                return g.rearrange("(k p) -> p k", p=P)

            load(con[:, :], d["constants"])
            load(gm_c, turned(d["g_mix"][0], KD), slow=True)
            load(gx_c, turned(d["g_x"][0], KD), slow=True)
            load(gf_c, turned(d["g_ffn"][0], KD), slow=True)
            load(gmem_c[:, :], turned(d["g_mem"][0], KD), slow=True)
            load(gq_c, turned(d["g_q"][0], 2), slow=True)
            load(gkv_b[:, :], bc(d["g_kv"], [P, LORA]))
            load(bf_b, bc(d["b_f"], [P, H]))
            load(br_b, bc(d["b_router"], [P, NE]))
            load(wr[:, :, :], d["w_router"][0].rearrange("(k p) e -> p k e", p=P))
            for k in range(KT):
                act.dma_start(lgc[:, k, :, :], d["cache_fox_logf"][0].rearrange("b (p k) h -> p k b h", k=KT)[:, k, :, :])\
                    .then_inc(lgc_loaded, 16)

            def take(key):
                act.wait_ge(full(key), count(key))
                return bank(key)

            def give(ins, key):
                ins.then_inc(free(key), 1)

            def copy_out(key, dst, n=None, rows=P):
                ps = take(key)
                give(a.copy(dst, ps[0:rows, 0:n] if n else ps), key)

            def squares(n, src):
                if n:
                    act.wait_ge(square_sum, n)
                a.activation(junk, src, ACT.Square, accum_out=ssq[:, n:n + 1]).then_inc(square_sum, 1)

            for t in range(NT):
                act.wait_ge(x_loaded[t], 16)
                squares(t, xr[:, t, :])
            for g in range(4):
                copy_out(("fqT", g), fqT[:, g, :], TOK)
            for t in range(NT):
                act.wait_ge(logf_part, t + 1)
                a.activation(lexp[:, t, :], lneg[:, t, :], ACT.Exp).then_inc(act_step, 1)
                act.wait_ge(act_step, t + 1)
                a.activation(lln[:, t, :], lexp[:, t, :], ACT.Ln, bias=1.0).then_inc(logit_exp, 1)
            for c in range(2):
                copy_out(("ukT", c), ukT[:, :, P * c:P * c + P])
            for g in range(4):
                copy_out(("fkT", g), fkT[:, g, :], TOK)
            ps = take("krT")
            for e in range(4):
                last = a.copy(krT[32 * e:32 * e + 32, :], ps[0:ROPE, 0:TOK])
            give(last, "krT")
            for c in range(2):
                copy_out(("ckvT", c), ckvT[:, c, :], TOK)
            for j in range(2):
                for t in range(NT):
                    copy_out(("fv", t, j), fv[:, t, 256 * j:256 * j + 256], 256)
            for g in range(4):
                copy_out(("qn", g), qnT[:, g, :], TOK)
            for h in range(H):
                ps = take(("ql", h, 1))
                a.copy(ql[:, 1, h, :], ps[:, 0:256])
                give(a.copy(qs[:, 1, :, h, :], ps[:, 256:TOK].rearrange("p (b q) -> p b q", q=NQ)), ("ql", h, 1))
            for c in range(2):
                copy_out(("qrT", c), qrT[:, c, :], TOK)

            SCALES = {"fox": FOX_SCALE, "mla": MLA_SCALE, "mem": X_SCALE}

            def exps(u, unit):
                kind, t, hs = unit
                w = width(kind, t)
                mx, nm, sm, rc, _ = softmax_cols(u)
                act.wait_ge(score_max, u + 1)
                if kind == "mem" and u - 4 >= U_MEM:
                    act.wait_ge(full(turn_key(u - 4)), count(turn_key(u - 4)))
                for n in range(2):
                    dst = prob[u % 4][:, w * n:w * n + w]
                    src = bank(("S", u))[:, w * n:w * n + w] if kind == "mem" else dst
                    last = a.activation(dst, src, ACT.Exp, bias=nm[:, n:n + 1], scale=SCALES[kind], accum_out=sm[:, n:n + 1])
                last.then_inc(exp_done, 1)
                if kind == "mem":
                    act.wait_ge(exp_done, u + 1)
                    give(a.nop(), ("S", u))

            def probs_out(u, unit):
                kind, t, hs = unit
                n = 2 * width(kind, t)
                if u - 4 >= (0 if kind != "mem" else U_MEM):
                    act.wait_ge(full(("V", u - 4)), count(("V", u - 4)))
                copy_out(("T", u), probT[u % 4][:, 0:n], n)

            def values_out(u, unit):
                kind, t, hs = unit
                ps = take(("V", u))
                c = slice(P * t, P * t + P)
                if kind == "fox":
                    e, g = 64 * (hs[0] % 2), hs[0] // 2
                    last = a.copy(foxT[e:e + 64, g:g + 2, c], ps[e:e + 64, 0:256].rearrange("p (n q) -> p n q", n=2))
                elif kind == "mla":
                    last = a.copy(ql[:, :, hs[0]::4, c], ps[:, :].rearrange("p (c n q) -> p c n q", c=2, n=2))
                else:
                    last = a.copy(xoT[:, hs[0]:hs[0] + 2, c], ps[:, 0:256].rearrange("p (n q) -> p n q", n=2))
                give(last, ("V", u))

            def pipeline(units, u0):
                n = len(units)
                for i in range(n + LAG_V):
                    if i < n:
                        exps(u0 + i, units[i])
                    if LAG_T <= i < n + LAG_T:
                        probs_out(u0 + i - LAG_T, units[i - LAG_T])
                    if i >= LAG_V:
                        values_out(u0 + i - LAG_V, units[i - LAG_V])

            pipeline(UNITS, 0)

            def cache_out(b):
                if b >= 2:
                    act.wait_ge(full(("sS", 2 * b - 3)), count(("sS", 2 * b - 3)))
                for g in range(2, 4):
                    copy_out(("skT", b, g), skT[b % 2][:, g, :])
                copy_out(("scT", b, 1), scT[b % 2][:, 1, :])
                copy_out(("srT", b), srT[b % 2], 512, ROPE)

            act.wait_ge(consts_loaded, 16 * NLOADS)
            for half in range(2):
                act.dma_start(y_dram[NE * CAP:NBLK * CAP, 512 * half:512 * half + 512].rearrange("(j p) n -> p j n", p=P),
                              bc(con[:, 0:512].unsqueeze(1), [P, OVER * CAP // P, 512])).then_inc(y_written, 16)

            def sample_exps(n):
                u = U_SAMPLE + n
                mx, nm, sm, rc, m1 = softmax_cols(u)
                act.wait_ge(score_max, u + 1)
                p = sprob[n % 3]
                sc = MLA_SCALE if n % 2 else FOX_SCALE
                give(a.activation(p[:, 0:512], bank(("sS", n))[:, :], ACT.Exp, bias=nm[:, 0:1], scale=sc, accum_out=sm[:, 0:1]), ("sS", n))
                a.activation(p[:, 512:640], p[:, 512:640], ACT.Exp, bias=nm[:, 0:1], scale=sc, accum_out=sm[:, 1:2]).then_inc(exp_done, 1)

            def sample_probs_out(n):
                if n >= 3:
                    act.wait_ge(full(("sV", n - 3)), count(("sV", n - 3)))
                ps = take(("sT", n))
                give(a.copy(sprobT[n % 3][:, 0:4, :], ps[:, :].rearrange("p (k m) -> p k m", k=4)), ("sT", n))
                copy_out(("sTn", n), sprobT[n % 3][:, 4, :], P)

            def sample_values_out(n):
                b = n // 2
                c = slice(256 + NQ * b, 256 + NQ * b + NQ)
                ps = take(("sV", n))
                if n % 2:
                    last = a.copy(qs[:, :, b, :, :], ps[:, 0:256].rearrange("p (c h q) -> p c h q", c=2, h=H))
                else:
                    pair = ps[:, 0:P].rearrange("p (g m) -> p g m", g=4)
                    a.copy(foxT[0:64, :, c], pair[0:64, :, 0:NQ])
                    last = a.copy(foxT[64:128, :, c], pair[64:128, :, NQ:2 * NQ])
                give(last, ("sV", n))

            act.wait_ge(fk_written, 32)
            cache_out(0)
            for b in range(NB + 1):
                if b < NB:
                    sample_exps(2 * b)
                    sample_exps(2 * b + 1)
                if b >= 1:
                    for n in (2 * b - 2, 2 * b - 1):
                        sample_probs_out(n)
                if b + 1 < NB:
                    cache_out(b + 1)
                if b >= 1:
                    for n in (2 * b - 2, 2 * b - 1):
                        sample_values_out(n)
            for g in range(4):
                copy_out(("mo", g), mlaT[:, g, :], TOK)
            for n in range(16):
                ps = take(("g", n))
                give(a.activation(gates[:, n, :], ps[:, 0:TOK], ACT.Sigmoid), ("g", n))
                act.wait_ge(free(("g", n)), count(("g", n)))
                a.nop().then_inc(gates_ready, 1)
            act.wait_ge(mem_loaded, 16)
            for t in range(2):
                squares(NT + t, memx[:, t, :])
            for w, m in (("xk", mk), ("xv", mv)):
                for j in range(2):
                    for t in range(2):
                        copy_out((w, t, j), m[:, t, 256 * j:256 * j + 256], 256)
            for h in range(XH):
                copy_out(("mkT", h), mkTs[:, h, :], MEM)
            for t in range(NT):
                act.wait_ge(free(("out", t, 3)), count(("out", t, 3)))
                squares(NT + 2 + t, xr[:, t, :])
            for h in range(XH):
                copy_out(("xq", h), xqT[:, h, :], TOK)
            pipeline(XUNITS, U_MEM)

            def mem_out(b):
                if b >= 2:
                    act.wait_ge(full(("cS", b - 2)), count(("cS", b - 2)))
                ps = take(("cK", b, 1))
                give(a.copy(xkT[b % 2][:, 2:4, :], ps[:, :].rearrange("p (h s) -> p h s", h=2)), ("cK", b, 1))

            def mem_exps(b):
                u = U_SMEM + b
                mx, nm, sm, rc, _ = softmax_cols(u)
                act.wait_ge(score_max, u + 1)
                act.wait_ge(full(turn_key(u - 4)), count(turn_key(u - 4)))
                give(a.activation(prob[b % 4][:, 0:MEM], bank(("cS", b))[:, 0:MEM], ACT.Exp, bias=nm[:, 0:1], scale=X_SCALE,
                                  accum_out=sm[:, 0:1]), ("cS", b))
                act.wait_ge(free(("cS", b)), count(("cS", b)))
                a.nop().then_inc(exp_done, 1)

            def mem_probs_out(b):
                key = ("V", U_MEM + b) if b < 4 else ("cV", b - 4)
                act.wait_ge(full(key), count(key))
                copy_out(("cT", b), probT[b % 4][:, 0:256], 256)

            def mem_values_out(b):
                ps = take(("cV", b))
                c = slice(256 + NQ * b, 256 + NQ * b + NQ)
                give(a.copy(xoT[:, :, c], ps[:, 0:64].rearrange("p (h q) -> p h q", h=XH)), ("cV", b))

            mem_out(0)
            for b in range(NB + 1):
                if b < NB:
                    mem_exps(b)
                if b + 1 < NB:
                    mem_out(b + 1)
                if b >= 1:
                    mem_probs_out(b - 1)
                    mem_values_out(b - 1)
            for t in range(NT):
                act.wait_ge(free(("xo", t, 1)), count(("xo", t, 1)))
                squares(2 * NT + 2 + t, xr[:, t, :])
            for t in range(NT):
                act.wait_ge(top_shift, t + 1)
                a.activation(top8[:, t, 0:TOPK], top8[:, t, 0:TOPK], ACT.Exp, bias=ntop[:, t:t + 1],
                             accum_out=esum[:, t:t + 1]).then_inc(top_exp, 1)

            act.wait_ge(blocks_ready, 1)
            nblk = act.value_load(blocks_i[0:1, 0:1], min_val=NE, max_val=NBLK)
            aTp, yp = psum[3], psum[4]
            a.nop().then_inc(y_copied, 1)
            act.wait_ge(y_copied, 1)
            with act.Fori(0, nblk) as b:
                act.wait_ge(gate_clipped, b + 1)
                a.activation(sS, gS, ACT.Sigmoid, scale=ALPHA).then_inc(gate_sig, 1)
                act.wait_ge(actT_full, b + 1)
                a.copy(actT, aTp[:, :].rearrange("p (k t) -> p k t", t=CAP)).then_inc(actT_ready, 1)
                act.wait_ge(ring_used[DOWN_SLOT[3]], b + 1)
                act.wait_ge(y_written, b * 32 + 32)
                a.copy(ysb, yp[:, :]).then_inc(y_copied, 1)
                act.wait_ge(y_copied, b + 2)
                for half in range(2):
                    act.dma_start(y_dram[bass.ds(b * CAP, CAP), 512 * half:512 * half + 512],
                                  ysb[CAP * half:CAP * half + CAP, :]).then_inc(y_written, 16)
            act.wait_ge(y_written, nblk * 32 + 32)
            a.copy(slot_cols[0], slotf[:, 0:1]).then_inc(first_rows, 1)
            act.dma_start(gfin, bc(d["g_final"].unsqueeze(0), [P, D])).then_inc(gfin_loaded, 16)
            for t in range(NT):
                act.wait_ge(y_added, 4 * t + 4)
                squares(3 * NT + 2 + t, xr[:, t, :])


_INS = ["x_prompt", "x_sample", "mem_prompt", "cache_fox_k", "cache_fox_v", "cache_fox_logf", "cache_mla_ckv",
        "cache_mla_krope", "cache_mem_k", "cache_mem_v", "g_mix", "w_in", "b_f", "g_q", "w_uq", "g_kv", "w_uk", "w_uv",
        "w_o_fox", "w_o_mla", "w_out", "g_x", "g_mem", "w_xq", "w_xk", "w_xv", "w_xo", "g_ffn", "w_router", "b_router",
        "w_gu", "b_gu", "w_down", "b_down", "g_final"]
_OUTS = [("y_prompt", (1, 256, 1024)), ("y_sample", (8, 16, 1024)), ("p_fox_k", (1, 1, 256, 8, 64)),
         ("p_fox_v", (1, 1, 256, 8, 64)), ("p_fox_logf", (1, 1, 256, 8)), ("p_mla_ckv", (1, 1, 256, 256)),
         ("p_mla_krope", (1, 1, 256, 32)), ("p_mem_k", (1, 1, 256, 4, 128)), ("p_mem_v", (1, 1, 256, 4, 128)),
         ("s_fox_k", (1, 8, 16, 8, 64)), ("s_fox_v", (1, 8, 16, 8, 64)), ("s_fox_logf", (1, 8, 16, 8)),
         ("s_mla_ckv", (1, 8, 16, 256)), ("s_mla_krope", (1, 8, 16, 32))]


def kernel(**inputs):
    import concourse.bacc as _bacc
    from concourse.bass_utils import run_bass_kernel_spmd as _run

    nc = _bacc.Bacc("TRN2", target_bir_lowering=False, num_devices=1)
    arrays = {"in_" + name: np.ascontiguousarray(inputs[name]) for name in _INS}
    arrays["in_constants"] = constants()
    ins = {name[3:]: nc.dram_tensor(name, a.shape, F32, kind="ExternalInput").ap() for name, a in arrays.items()}
    outs = {name: nc.dram_tensor(name, shape, F32, kind="ExternalOutput").ap() for name, shape in _OUTS}
    build(nc, ins, outs)
    r = _run(nc, [arrays], core_ids=[0])
    return tuple(r.results[0][name] for name, _ in _OUTS)
```

```python
from contextlib import ExitStack

import numpy as np

import concourse.bass as bass
from concourse import mybir

F32 = mybir.dt.float32
BF16 = mybir.dt.bfloat16
I32 = mybir.dt.int32
U32 = mybir.dt.uint32
ALU = mybir.AluOpType
ACT = mybir.ActivationFunctionType
X = mybir.AxisListType.X

P = 128
D = 1024
KD = D // P
NT = 3
TOK = NT * P
NB, NQ = 8, 16
PAST = 512
KT = PAST // P
H = 8
FW = 512
LORA = 256
ROPE = 32
QH = 96
XH, XD, MEM = 4, 128, 256
NE = 32
TOPK = 4
CAP = 64
OVER = 24
NBLK = NE + OVER
EPS = 1e-6
NEG = -1e30
FOX_SCALE = 64 ** -0.5
MLA_SCALE = 96 ** -0.5
X_SCALE = 128 ** -0.5
LIMIT, ALPHA = 7.0, 1.702
SLOT = 2048
NRING = 8
C_FQ, C_FK, C_FV, C_FL, C_QC, C_KV, C_KR, C_G = 0, 512, 1024, 1536, 1544, 1800, 2056, 2088

CONST = {}
_at = 0
for _name, _n in (("ident", 128), ("tri", 1024), ("blocktri", 128), ("z1", 128), ("causal", 128), ("z2", 128), ("chunk", 128),
                  ("foxnew", 240), ("mlanew", 240), ("cos", 48), ("sin", 48), ("iota", 64), ("i64", 64),
                  ("tokid", 3), ("pmod", 1), ("row", 1), ("neg8", 64), ("zero", 32)):
    CONST[_name] = (_at, _n)
    _at += _n
NCONST = _at


def constants():
    c = np.zeros((P, NCONST), np.float32)

    def put(name, value):
        a, n = CONST[name]
        c[:value.shape[0], a:a + n] = value.reshape(value.shape[0], n)

    p = np.arange(P)
    incl = (p[:, None] <= p[None, :]).astype(np.float32)
    strict = (p[:, None] < p[None, :]).astype(np.float32)
    put("ident", np.eye(P, dtype=np.float32))
    put("tri", np.concatenate([strict] * 3 + [incl] * 4 + [np.ones((P, P), np.float32)], 1))
    same = p[:, None] // NQ == p[None, :] // NQ
    put("blocktri", incl * same)
    put("causal", np.where(p[None, :] <= p[:, None], 0, NEG).astype(np.float32))
    put("chunk", np.where(p[None, :] // 64 <= p[:, None] // 64, 0, NEG).astype(np.float32))
    q = p % NQ
    j = np.arange(NQ)
    new = np.full((P, 15, NQ), NEG, np.float32)
    new[:, 7] = np.where(j[None, :] <= q[:, None], 0, NEG)
    put("foxnew", new)
    new = np.full((P, 15, NQ), NEG, np.float32)
    new[:, 7] = 0
    put("mlanew", new)
    half = ROPE // 2
    freq = np.float32(10000.0) ** (-np.arange(half, dtype=np.float32) / np.float32(half))
    pos = np.stack([p, p + P, PAST + q], 1).astype(np.float32)
    ang = pos[:, :, None] * freq[None, None, :].astype(np.float32)
    put("cos", np.cos(ang))
    put("sin", np.sin(ang))
    put("iota", np.tile(np.arange(64, dtype=np.float32), (P, 1)))
    put("i64", np.tile(64 * np.arange(64, dtype=np.float32), (P, 1)))
    put("tokid", np.stack([p, p + P, p + 2 * P], 1).astype(np.float32))
    put("pmod", (p % NE).astype(np.float32)[:, None])
    put("row", (-(p % CAP)).astype(np.float32)[:, None])
    put("neg8", np.concatenate([-8 * np.eye(64, dtype=np.float32)] * 2, 0))
    return c


def bc(ap, shape):
    return ap.broadcast_to(shape)


def build(nc, d, out):
    ctx = ExitStack()
    with ctx:
        def sb(name, shape, dt=F32):
            return ctx.enter_context(nc.sbuf_tensor(name, shape, dt))

        def sem(name):
            return ctx.enter_context(nc.semaphore(name))

        ring = sb("ring", [P, 12, SLOT])
        low = ring[:, 8:11, :].rearrange("p s n -> p (s n)")
        gates = low.rearrange("p (n t) -> p n t", n=16)
        fk = low[:, 0:1536].rearrange("p (t n) -> p t n", t=NT)
        qc = low[:, 1536:2304].rearrange("p (t n) -> p t n", t=NT)
        qcT = low[:, 2304:3072].rearrange("p (c t) -> p c t", c=2)
        qnT = low[:, 3072:4608].rearrange("p (c t) -> p c t", c=4)
        qrope = low[:, 4608:5376].rearrange("p (t h r) -> p t h r", t=NT, r=ROPE)
        skT = [low[:, 3072 * i:3072 * i + 2048].rearrange("p (g s) -> p g s", g=4) for i in range(2)]
        scT = [low[:, 3072 * i + 2048:3072 * i + 3072].rearrange("p (c s) -> p c s", c=2) for i in range(2)]
        xkT = [low[:, 1024 * i:1024 * i + 1024].rearrange("p (h s) -> p h s", h=XH) for i in range(2)]
        prob = [ring[:, 11, 512 * i:512 * i + 512] for i in range(4)]
        sprob = [ring[:, 11, 640 * i:640 * i + 640] for i in range(3)]
        probTs = sb("probTs", [P, SLOT])
        probT = [probTs[:, 512 * i:512 * i + 512] for i in range(4)]
        sprobT = [probTs[:, 640 * i:640 * i + 640].rearrange("p (k m) -> p k m", k=5) for i in range(3)]
        ukT = probTs[:, 0:1024].rearrange("p (g c) -> p g c", g=4)
        con = sb("con", [P, NCONST])
        xr = sb("xr", [P, NT, D])
        xflat = xr[:, :, :].rearrange("p t n -> p (t n)")
        qpair = xflat[:, 0:1024].rearrange("p (b g m) -> p b g m", b=NB, g=4)
        qrS = xflat[0:ROPE, 1024:2048].rearrange("p (b h q) -> p b h q", b=NB, h=H)
        cumS = xflat[64:128, 2048:2688]
        sel8 = xflat[64:128, 1024:2048].rearrange("p (b m) -> p b m", b=NB)
        logfw = xflat[:, 2944:3008]
        hT = sb("hT", [P, KD, TOK])
        fqT = sb("fqT", [P, 4, TOK])
        fkT = sb("fkT", [P, 4, TOK])
        fv = sb("fv", [P, NT, FW])
        att = sb("att", [P, 2688])
        ckv = att[:, 0:768].rearrange("p (t n) -> p t n", t=NT)
        ckvT = att[:, 768:1536].rearrange("p (c t) -> p c t", c=2)
        krT = att[:, 1536:1920]
        qrT = att[:, 1920:2688].rearrange("p (c t) -> p c t", c=2)
        xn2 = low[:, 2048:5120].rearrange("p (t n) -> p t n", t=NT)
        qlf = sb("latent", [P, 2 * H * TOK])
        kn = qlf[:, 0:1024].rearrange("p (g s) -> p g s", g=4)
        vn = qlf[:, 1024:2048].rearrange("p (t n) -> p t n", t=2)
        qs = qlf[:, 4096:6144].rearrange("p (c b h q) -> p c b h q", c=2, b=NB, h=H)
        foxT = sb("foxT", [P, 4, TOK])
        mlaT = sb("mlaT", [P, 4, TOK])
        junk = probTs[:, 1024:2048]
        junk2 = low[:, 5376:5632]
        srT = [qlf[0:ROPE, 2048 + 512 * i:2560 + 512 * i] for i in range(2)]
        fox_rows = [qlf[:, 3072 + P * i:3072 + P * i + P] for i in range(2)]
        mlaf = mlaT[:, :, :].rearrange("p g t -> p (g t)")
        foxf = foxT[:, :, :].rearrange("p g t -> p (g t)")
        mem_rows = [foxf[:, 1024 + P * i:1024 + P * i + P] for i in range(2)]
        lgc = foxT[:, 0, 0:256].rearrange("p (k b h) -> p k b h", k=KT, b=NB)
        small = sb("small", [P, 160])
        memx = qlf[:, 0:2048].rearrange("p (t n) -> p t n", t=2)
        memT = qlf[:, 2048:4096].rearrange("p (k t) -> p k t", k=KD)
        mk = qlf[:, 4096:5120].rearrange("p (t n) -> p t n", t=2)
        mv = qlf[:, 5120:6144].rearrange("p (t n) -> p t n", t=2)
        mkTs = foxT[:, :, :].rearrange("p g t -> p (g t)")[:, 0:1024].rearrange("p (h s) -> p h s", h=XH)
        xqT, xoT = fqT, fkT
        xpair = fv[:, :, :].rearrange("p t n -> p (t n)")[:, 0:1024].rearrange("p (b h m) -> p b h m", b=NB, h=XH)
        cols = small[:, 0:64]
        bf_b = small[:, 64:72]
        br_b = small[:, 72:104]
        logf = small[:, 104:128].rearrange("p (t h) -> p t h", t=NT)
        gq_c = small[:, 128:130]
        gx_c = small[:, 130:138]
        gf_c = small[:, 138:146]
        gm_c = small[:, 146:154]
        gmem_c = sb("gmem_c", [P, KD])
        gkv_b = sb("gkv_b", [P, LORA])
        krope = sb("krope", [P, NT, ROPE])
        cumT = xflat[0:72, 2688:2944]
        wr = sb("wr", [P, KD, NE])
        chosen = probTs[:, 0:96].rearrange("p (t e) -> p t e", t=NT)
        logit = probTs[:, 96:192].rearrange("p (t e) -> p t e", t=NT)
        onehot = probTs[:, 192:576].rearrange("p (n e) -> p n e", e=NE)
        blk1 = probTs[:, 576:1248].rearrange("p (n b) -> p n b", b=NBLK)
        fqf = fqT[:, :, :].rearrange("p g t -> p (g t)")
        pick = fqf[:, 0:768].rearrange("p (n m) -> p n m", m=CAP)
        slot_e = fqf[:, 768:864].rearrange("p (t e) -> p t e", t=NT)
        slot_d = fqf[:, 864:960].rearrange("p (t e) -> p t e", t=NT)
        e_tmp = fqf[:, 960:1344].rearrange("p (n e) -> p n e", e=NE)
        fkf = fkT[:, :, :].rearrange("p g t -> p (g t)")
        cnt = fkf[:, 0:32].bitcast(I32)
        novr = fkf[:, 32:64]
        oincl = fkf[:, 64:96]
        moved = fkf[:, 96:128]
        o_cmp = fkf[:, 128:896].rearrange("p (j e) -> p j e", e=NE)
        route = sb("route", [P, 256])
        top8 = route[:, 0:24].rearrange("p (t n) -> p t n", t=NT)
        idx8 = route[:, 24:48].bitcast(U32).rearrange("p (t n) -> p t n", t=NT)
        idxf = route[:, 48:72].rearrange("p (t n) -> p t n", t=NT)
        gatew = route[:, 72:84]
        slotf = route[:, 84:96]
        inblk = route[:, 96:108]
        ntop = route[:, 120:123]
        slot_i = route[:, 108:120].bitcast(I32)
        row_i = route[:, 242:254].bitcast(I32)
        blk_i = route[:, 24:36].bitcast(I32)
        blkf = route[:, 36:48]
        esum = route[:, 123:126]
        blocks_i = route[:, 126:127].bitcast(I32)
        bexp = route[:, 128:185]
        bexp_i = route[0:1, 186:242].bitcast(I32)
        idx_all = sb("idx_all", [CAP, NBLK + 1], I32)
        idx_col = sb("idx_col", [CAP, 1], I32)
        gS, uS, tS, hid = (qlf[:, 512 * i:512 * i + 512] for i in range(4))
        sS = probTs[:, 0:512]
        actT = qlf[:, 2048:2560].rearrange("p (k t) -> p k t", t=CAP)
        xT = qlf[:, 2560:3072].rearrange("p (k t) -> p k t", t=CAP)
        ysb = qlf[:, 3072:3584]
        xg = qlf[0:CAP, 3584:4608]
        sel = qlf[0:96, 4608:4640].bitcast(BF16)
        bias3 = att[0:96, 0:1536].bitcast(BF16)
        bstage = att[0:NE, 1536:2560]
        bmid = low[0:NE, 5120:5632].bitcast(BF16)
        pair_row = hT[:, 0:4, :]
        pair_gate = hT[:, 4:8, :]
        pair_hit = fqT[:, :, :]
        share = fkT[:, 0, :]
        gfin = fv[:, :, :].rearrange("p t n -> p (t n)")[:, 0:D]
        yout = ring[:, 3:5, :].rearrange("p s n -> p (s n)")[:, 0:3072].rearrange("p (t n) -> p t n", t=NT)

        psum = [ctx.enter_context(nc.psum_tensor(f"bank{i}", [P, 512], F32))[:, :] for i in range(8)]

        def cc(name, rows=P):
            a, n = CONST[name]
            return con[0:rows, a:a + n]

        ident = cc("ident")
        t0 = CONST["tri"][0]
        ones = con[:, t0 + 896:t0 + 1024]
        incl_ones = con[:, t0 + 768:t0 + 1024]

        x3_dram = nc.dram_tensor("x3_normed", [TOK, D], F32).ap()

        bank_full = [sem(f"bank_full{i}") for i in range(8)]
        bank_free = [sem(f"bank_free{i}") for i in range(8)]
        ring_loaded = [sem(f"ring_loaded{i}") for i in range(12)]
        ring_used = [sem(f"ring_used{i}") for i in range(12)]
        ident_loaded = sem("ident_loaded")
        g_mix_loaded = sem("g_mix_loaded")
        consts_loaded = sem("consts_loaded")
        x_loaded = [sem(f"x_loaded{t}") for t in range(NT)]
        ckv_written = sem("ckv_written")
        fv_written = sem("fv_written")
        bias_step = sem("bias_step")
        zeroed = sem("zeroed")
        logf_wide = sem("logf_wide")
        gates_ready = sem("gates_ready")
        up_clipped = sem("up_clipped")
        product = sem("product")
        y_out = sem("y_out")
        lgc_loaded = sem("lgc_loaded")
        mem_loaded = sem("mem_loaded")
        x_again = sem("x_again")
        dve_step = sem("dve_step")
        act_step = sem("act_step")
        square_sum = sem("square_sum")
        xn_ready = sem("xn_ready")
        logit_exp = sem("logit_exp")
        logf_part = sem("logf_part")
        logf_ready = sem("logf_ready")
        krope_ready = sem("krope_ready")
        ckv_ready = sem("ckv_ready")
        qc_ready = sem("qc_ready")
        qrope_ready = sem("qrope_ready")
        outputs_written = sem("outputs_written")
        fk_written = sem("fk_written")
        score_max = sem("score_max")
        exp_done = sem("exp_done")
        prob_ready = sem("prob_ready")
        pairs_ready = sem("pairs_ready")
        mix_ready = sem("mix_ready")
        top_shift = sem("top_shift")
        top_exp = sem("top_exp")
        scratch_written = sem("scratch_written")
        masks_ready = sem("masks_ready")
        pick_ready = sem("pick_ready")
        bexp_ready = sem("bexp_ready")
        blocks_ready = sem("blocks_ready")
        bias_loaded = sem("bias_loaded")
        bias_moved = sem("bias_moved")
        mk_written = sem("mk_written")
        first_copied = sem("first_copied")
        idx_copied = sem("idx_copied")
        rows_gathered = sem("rows_gathered")
        xT_full = sem("xT_full")
        xT_ready = sem("xT_ready")
        gate_clipped = sem("gate_clipped")
        gate_sig = sem("gate_sig")
        act_ready = sem("act_ready")
        actT_full = sem("actT_full")
        actT_ready = sem("actT_ready")
        y_copied = sem("y_copied")
        share_ready = sem("share_ready")
        gate_ready = sem("gate_ready")
        slot_ready = sem("slot_ready")
        hits_ready = sem("hits_ready")
        shares_full = sem("shares_full")
        shares_added = sem("shares_added")
        gfin_loaded = sem("gfin_loaded")
        fin_ready = sem("fin_ready")

        groups = {}

        def open_bank(pe, key):
            n = groups[key] = len(groups)
            if n >= 8:
                pe.wait_ge(bank_free[n % 8], n // 8)
            return psum[n % 8]

        def full(key):
            return bank_full[groups[key] % 8]

        def free(key):
            return bank_free[groups[key] % 8]

        def count(key):
            return groups[key] // 8 + 1

        def bank(key):
            return psum[groups[key] % 8]

        w_in = d["w_in"][0].rearrange("(k p) n -> p k n", p=P)
        stream = []

        def kview(slot, k, n):
            return ring[:, slot, 0:k * n].rearrange("p (k n) -> p k n", k=k)

        def tile(key, parts):
            stream.append((key, parts))

        def whole(k, n, src):
            return [(lambda s: kview(s, k, n), src)]

        for j in range(2):
            tile(("fq", j), whole(KD, 256, w_in[:, :, C_FQ + 256 * j:C_FQ + 256 * j + 256]))
        for j in range(2):
            tile(("fk", j), whole(KD, 256, w_in[:, :, C_FK + 256 * j:C_FK + 256 * j + 256]))
        tile("fl", [(lambda s: kview(s, KD, 40)[:, :, 0:8], w_in[:, :, C_FL:C_FL + 8]),
                    (lambda s: kview(s, KD, 40)[:, :, 8:40], w_in[:, :, C_KR:C_KR + ROPE])])
        tile("kv", whole(KD, 256, w_in[:, :, C_KV:C_KV + 256]))
        tile("qc", whole(KD, 256, w_in[:, :, C_QC:C_QC + 256]))
        tile("uk", whole(2, 512, d["w_uk"][0].rearrange("(k p) h n -> p k (h n)", p=P)))
        tile("uv prompt", whole(2, 512, d["w_uv"][0].rearrange("(k p) h n -> p k (h n)", p=P)))
        tile("uq", whole(2, 768, d["w_uq"][0].rearrange("(k p) n -> p k n", p=P)))
        for j in range(2):
            tile(("fv", j), whole(KD, 256, w_in[:, :, C_FV + 256 * j:C_FV + 256 * j + 256]))
        for b in range(NB):
            tile(("sk", b), whole(KT, FW, d["cache_fox_k"][0, b].rearrange("(p k) h n -> p k (h n)", k=KT)))
            tile(("sc", b), [(lambda s: kview(s, KT, LORA), d["cache_mla_ckv"][0, b].rearrange("(p k) n -> p k n", k=KT)),
                             (lambda s: ring[:, s, 1024:1152].rearrange("p (k n) -> p k n", k=KT),
                              d["cache_mla_krope"][0, b].rearrange("(p k) n -> p k n", k=KT))])
            tile(("sv", b), whole(KT, FW, d["cache_fox_v"][0, b].rearrange("(p k) h n -> p k (h n)", k=KT)))
        tile("uv", whole(2, 512, d["w_uv"][0].rearrange("(k p) h n -> p k (h n)", p=P)))
        for j in range(8):
            tile(("g", j), whole(KD, 256, w_in[:, :, C_G + 256 * j:C_G + 256 * j + 256]))

        def mem_tiles(w):
            for j in range(2):
                tile((w, j), whole(KD, 256, d["w_" + w][0].rearrange("(k p) n -> p k n", p=P)[:, :, 256 * j:256 * j + 256]))

        for j in range(2):
            for w in ("w_o_fox", "w_o_mla"):
                tile((w, j), whole(4, 512, d[w][0].rearrange("(k p) n -> p k n", p=P)[:, :, 512 * j:512 * j + 512]))
        mem_tiles("xk")
        for j in range(4):
            tile(("out", j), whole(KD, 256, d["w_out"][0].rearrange("(k p) n -> p k n", p=P)[:, :, 256 * j:256 * j + 256]))
        mem_tiles("xv")
        for j in range(2):
            tile(("xq", j), whole(KD, 256, d["w_xq"][0].rearrange("(k p) n -> p k n", p=P)[:, :, 256 * j:256 * j + 256]))
        for b in range(NB):
            if b == 2:
                for j in range(2):
                    tile(("xo", j), whole(4, 512, d["w_xo"][0].rearrange("(k p) n -> p k n", p=P)[:, :, 512 * j:512 * j + 512]))
            tile(("cm", b), [(lambda s: kview(s, 2, FW), d["cache_mem_k"][0, b].rearrange("(p k) h n -> p k (h n)", k=2)),
                             (lambda s: ring[:, s, 1024:2048].rearrange("p (k n) -> p k n", k=2),
                              d["cache_mem_v"][0, b].rearrange("(p k) h n -> p k (h n)", k=2))])
        place = {key: n for n, (key, _) in enumerate(stream)}
        NPRE = len(stream)
        loads = {}
        loaded_at = []
        for n, (key, parts) in enumerate(stream):
            loads[n % NRING] = loads.get(n % NRING, 0) + 16 * len(parts)
            loaded_at.append(loads[n % NRING])
        GU_SLOT = [(NPRE + c) % NRING for c in range(KD)]
        GU_LOADS = [loads[s] for s in GU_SLOT]
        DOWN_SLOT = [8, 9, 10, 11]

        last_group = {}

        def used_last(pe, ins, key):
            last_group[key] = len(groups) - 1

        def arrived(pe, key):
            n = place[key]
            pe.wait_ge(ring_loaded[n % NRING], loaded_at[n])
            return n % NRING

        def prompt_units(kind):
            if kind == "fox":
                return [("fox", t, hs) for t in range(2) for hs in ((0, 2), (1, 3), (4, 6), (5, 7))]
            if kind == "mla":
                return [("mla", t, (g, g + 4)) for t in range(2) for g in range(4)]
            return [("mem", t, (2 * g, 2 * g + 1)) for t in range(2) for g in range(2)]

        UNITS = prompt_units("fox") + prompt_units("mla")
        XUNITS = prompt_units("mem")
        NU, NXU = len(UNITS), len(XUNITS)
        NLOADS = 9
        SU = 2 * NB
        LAG_T, LAG_V = 2, 3
        CROSS_AT = {2: (0, 0), 3: (0, 1), 4: (1, 0), 5: (1, 1)}
        U_SAMPLE = NU
        U_MEM = NU + SU
        U_SMEM = NU + SU + NXU

        def width(kind, t):
            return 2 * P if kind == "mem" else P * (t + 1)

        S_COL = {}
        def col(name, n=1):
            if name not in S_COL:
                S_COL[name] = sum(v[1] for v in S_COL.values())
                S_COL[name] = (S_COL[name], n)
            a, m = S_COL[name]
            return cols[:, a:a + m]

        block = ctx.enter_context(nc.Block())

        @block.tensor
        def _(pe):
            def mm(o, l, r, start, stop):
                return pe.matmul(o, l, r, start=start, stop=stop, skip_group_check=True)

            def done(ins, key):
                ins.then_inc(bank_full[groups[key] % 8], 1)

            def rms_turn(name, src, tiles):
                rows = {"hT": xr, "mT": memx}.get(name, xn2)
                for t in tiles:
                    pe.wait_ge(*src(t))
                    for half in range(2):
                        ps = open_bank(pe, (name, t, half))
                        for c in range(4):
                            k = 4 * half + c
                            i = pe.transpose(ps[:, P * c:P * c + P], rows[:, t, P * k:P * k + P], ident)
                        done(i, (name, t, half))

            def project(key, w, t, src, n=256, kn=256):
                ps = open_bank(pe, key)
                s = place[w] % NRING
                for k in range(KD):
                    i = mm(ps[:, 0:n], src[:, k, P * t:P * t + P], kview(s, KD, kn)[:, k, 0:n], k == 0, k == KD - 1)
                done(i, key)
                return i

            def project_T(key, slot, col0, src):
                ps = open_bank(pe, key)
                for k in range(KD):
                    i = mm(ps[:, 0:TOK], kview(slot, KD, 256)[:, k, col0:col0 + P], src[:, k, :], k == 0, k == KD - 1)
                done(i, key)
                return i

            pe.wait_ge(ident_loaded, 16)
            rms_turn("hT", lambda t: (xn_ready, t + 1), range(NT))
            for t in range(NT):
                for half in range(2):
                    pe.wait_ge(free(("hT", t, half)), count(("hT", t, half)))
            for j in range(2):
                s = arrived(pe, ("fq", j))
                for m in range(2):
                    i = project_T(("fqT", 2 * j + m), s, P * m, hT)
                used_last(pe, i, ("fq", j))
            for j in range(2):
                arrived(pe, ("fk", j))
                for t in range(NT):
                    i = project(("fk", t, j), ("fk", j), t, hT)
                used_last(pe, i, ("fk", j))
            arrived(pe, "fl")
            for t in range(NT):
                i = project(("fl", t), "fl", t, hT, n=40, kn=40)
            used_last(pe, i, "fl")
            arrived(pe, "kv")
            for t in range(NT):
                i = project(("kv", t), "kv", t, hT)
            used_last(pe, i, "kv")
            arrived(pe, "qc")
            for t in range(NT):
                i = project(("qc", t), "qc", t, hT)
            used_last(pe, i, "qc")
            s = arrived(pe, "uk")
            for c in range(2):
                ps = open_bank(pe, ("ukT", c))
                for g in range(4):
                    i = pe.transpose(ps[:, P * g:P * g + P], kview(s, 2, 512)[:, c, P * g:P * g + P], ident)
                done(i, ("ukT", c))
            for t in range(NT):
                for j in range(2):
                    pe.wait_ge(free(("fk", t, j)), count(("fk", t, j)))
            for g in range(4):
                ps = open_bank(pe, ("fkT", g))
                for t in range(NT):
                    i = pe.transpose(ps[:, P * t:P * t + P], fk[:, t, P * g:P * g + P], ident)
                done(i, ("fkT", g))
            pe.wait_ge(krope_ready, NT)
            ps = open_bank(pe, "krT")
            for t in range(NT):
                i = pe.transpose(ps[0:ROPE, P * t:P * t + P], krope[:, t, :], ident)
            done(i, "krT")
            pe.wait_ge(ckv_ready, NT)
            for c in range(2):
                ps = open_bank(pe, ("ckvT", c))
                for t in range(NT):
                    i = pe.transpose(ps[:, P * t:P * t + P], ckv[:, t, P * c:P * c + P], ident)
                done(i, ("ckvT", c))
            pe.wait_ge(qc_ready, NT)
            for c in range(2):
                ps = open_bank(pe, ("qcT", c))
                for t in range(NT):
                    i = pe.transpose(ps[:, P * t:P * t + P], qc[:, t, P * c:P * c + P], ident)
                done(i, ("qcT", c))
            pe.wait_ge(consts_loaded, 16 * NLOADS)
            pe.wait_ge(logf_ready, NT)
            ps = open_bank(pe, "cumP")
            mm(ps[0:H, 0:256], logf[:, 0, :], incl_ones, True, False)
            i = mm(ps[0:H, P:256], logf[:, 1, :], incl_ones[:, 0:P], False, True)
            done(i, "cumP")
            pe.wait_ge(lgc_loaded, 16 * KT)
            pe.wait_ge(logf_wide, 1)
            ps = open_bank(pe, "cumS")
            for k in range(KT):
                i = mm(ps[0:64, :], lgc[:, k, :, :].rearrange("p b h -> p (b h)"), con[:, t0 + 128 * (3 - k):t0 + 128 * (3 - k) + 512], k == 0, k == KT - 1)
            done(i, "cumS")
            ps = open_bank(pe, "cumN")
            for k in range(KT):
                mm(ps[0:64, 0:P], lgc[:, k, :, :].rearrange("p b h -> p (b h)"), ones, k == 0, False)
            i = mm(ps[0:64, 0:P], logfw, cc("blocktri"), False, True)
            done(i, "cumN")
            def latent_keys(g):
                uk = kview(place["uk"] % NRING, 2, 512)
                if g == 0:
                    for c in range(2):
                        pe.wait_ge(free(("ckvT", c)), count(("ckvT", c)))
                ps = open_bank(pe, ("kn", g))
                for e in range(2):
                    for c in range(2):
                        h = 2 * g + e
                        i = mm(ps[64 * e:64 * e + 64, 0:256], uk[:, c, 64 * h:64 * h + 64], ckvT[:, c, 0:256], c == 0, c == 1)
                done(i, ("kn", g))
                if g == 3:
                    used_last(pe, i, "uk")

            def latent_values(t):
                s = arrived(pe, "uv prompt")
                ps = open_bank(pe, ("vn", t))
                for c in range(2):
                    i = mm(ps[:, :], ckvT[:, c, P * t:P * t + P], kview(s, 2, 512)[:, c, :], c == 0, c == 1)
                done(i, ("vn", t))
                used_last(pe, i, "uv prompt")

            def between_units(i):
                if 1 <= i < 1 + NT:
                    fox_values(1, i - 1)
                if 3 <= i < 7:
                    latent_keys(i - 3)
                if 4 <= i < 6:
                    latent_values(i - 4)

            def fox_values(j, t):
                if t == 0:
                    arrived(pe, ("fv", j))
                i = project(("fv", t, j), ("fv", j), t, hT)
                if t == NT - 1:
                    used_last(pe, i, ("fv", j))

            for c in range(2):
                pe.wait_ge(free(("qcT", c)), count(("qcT", c)))
            s = arrived(pe, "uq")
            uq = kview(s, 2, 768)
            for t in range(NT):
                ps = open_bank(pe, ("qr", t))
                for k in range(2):
                    i = mm(ps[:, 0:256], qcT[:, k, P * t:P * t + P],
                           uq[:, k, :].rearrange("p (h n) -> p h n", n=QH)[:, :, 64:QH], k == 0, k == 1)
                done(i, ("qr", t))
            for g in range(4):
                ps = open_bank(pe, ("qn", g))
                for e in range(2):
                    for k in range(2):
                        h = 2 * g + e
                        i = mm(ps[64 * e:64 * e + 64, 0:TOK], uq[:, k, QH * h:QH * h + 64], qcT[:, k, :], k == 0, k == 1)
                done(i, ("qn", g))
            used_last(pe, i, "uq")
            for c in range(2):
                pe.wait_ge(free(("ukT", c)), count(("ukT", c)))
            for t in range(2):
                fox_values(0, t)
            for g in range(4):
                pe.wait_ge(free(("qn", g)), count(("qn", g)))
            for odd in range(2):
                e = 64 * odd
                for c in range(2):
                    ps = open_bank(pe, ("ql", odd, c))
                    for g in range(4):
                        i = mm(ps[:, P * g:P * g + P], ukT[e:e + 64, g, P * c:P * c + P], qnT[e:e + 64, g, 256:384],
                               g == 0, g == 3)
                    done(i, ("ql", odd, c))
            pe.wait_ge(qrope_ready, NT)
            for c in range(2):
                ps = open_bank(pe, ("qrT", c))
                for t in range(NT):
                    i = pe.transpose(ps[:, P * t:P * t + P], qrope[:, t, 4 * c:4 * c + 4, :], ident)
                done(i, ("qrT", c))
            fox_values(0, 2)

            def scores(u, unit):
                kind, t, hs = unit
                if u == 8:
                    for key in [("kn", g) for g in range(4)] + [("vn", s) for s in range(2)]:
                        pe.wait_ge(free(key), count(key))
                ps = open_bank(pe, ("S", u))
                w = width(kind, t)
                for n, h in enumerate(hs):
                    o = ps[:, w * n:w * n + w]
                    if kind == "fox":
                        e = 64 * (h % 2)
                        mm(o, fqT[e:e + 64, h // 2, P * t:P * t + P], fkT[e:e + 64, h // 2, 0:w], n == 0, False)
                        i = mm(o, bc(con[e:e + H, CONST["neg8"][0] + h:CONST["neg8"][0] + h + 1], [H, P]),
                               cumT[e:e + H, 0:w], False, True)
                    elif kind == "mla":
                        e = 64 * (h % 2)
                        mm(o, qnT[e:e + 64, h // 2, P * t:P * t + P], kn[e:e + 64, h // 2, 0:w], n == 0, False)
                        e = 32 * (h % 4)
                        i = mm(o, qrT[e:e + 32, h // 4, P * t:P * t + P], krT[e:e + 32, 0:w], False, True)
                    else:
                        i = mm(o, xqT[:, h, P * t:P * t + P], mkTs[:, h, :], n == 0, n == 1)
                done(i, ("S", u))

            def turn(u, unit):
                kind, t, hs = unit
                pe.wait_ge(prob_ready, u + 1)
                ps = open_bank(pe, ("T", u))
                w = width(kind, t)
                nk = w // P
                for s in range(nk):
                    for n in range(2):
                        i = pe.transpose(ps[:, P * (2 * s + n):P * (2 * s + n) + P],
                                         prob[u % 4][:, w * n + P * s:w * n + P * s + P], ident)
                done(i, ("T", u))

            def values(u, unit):
                kind, t, hs = unit
                nk = width(kind, t) // P
                pt = probT[u % 4].rearrange("p (s n q) -> p s n q", n=2, q=P)
                pe.wait_ge(free(("T", u)), count(("T", u)))
                if u in (0, 2):
                    for s in range(NT):
                        pe.wait_ge(free(("fv", s, u // 2)), count(("fv", s, u // 2)))
                ps = open_bank(pe, ("V", u))
                for n, h in enumerate(hs):
                    if kind == "mem":
                        for s in range(nk):
                            i = mm(ps[:, P * n:P * n + P], mv[:, s, P * h:P * h + P], pt[:, s, n, :],
                                   n == 0 and s == 0, s == nk - 1)
                    else:
                        e = 64 * (h % 2)
                        v = fv if kind == "fox" else vn
                        for s in range(nk):
                            i = mm(ps[e:e + 64, P * n:P * n + P], v[:, s, 64 * h:64 * h + 64], pt[:, s, n, :],
                                   n == 0 and s == 0, s == nk - 1)
                done(i, ("V", u))

            def pipeline(units, u0, between=None):
                n = len(units)
                for i in range(n + LAG_V):
                    if i < n:
                        scores(u0 + i, units[i])
                    if between:
                        between(i)
                    if LAG_T <= i < n + LAG_T:
                        turn(u0 + i - LAG_T, units[i - LAG_T])
                    if i >= LAG_V:
                        values(u0 + i - LAG_V, units[i - LAG_V])

            for g in range(4):
                pe.wait_ge(free(("fqT", g)), count(("fqT", g)))
                pe.wait_ge(free(("fkT", g)), count(("fkT", g)))
            for key in ["cumP", "krT", ("ckvT", 0), ("ckvT", 1), ("qrT", 0), ("qrT", 1)]:
                pe.wait_ge(free(key), count(key))
            for odd in range(2):
                for c in range(2):
                    pe.wait_ge(free(("ql", odd, c)), count(("ql", odd, c)))
            pipeline(UNITS, 0, between_units)

            def turn_keys(b, pairs):
                s = arrived(pe, ("sk", b))
                k3 = kview(s, KT, FW)
                for g in pairs:
                    ps = open_bank(pe, ("skT", b, g))
                    for k in range(KT):
                        i = pe.transpose(ps[:, P * k:P * k + P], k3[:, k, P * g:P * g + P], ident)
                    done(i, ("skT", b, g))
                if g == 3:
                    used_last(pe, i, ("sk", b))

            def turn_latents(b):
                s = arrived(pe, ("sc", b))
                c3 = kview(s, KT, LORA)
                for c in range(2):
                    ps = open_bank(pe, ("scT", b, c))
                    for k in range(KT):
                        i = pe.transpose(ps[:, P * k:P * k + P], c3[:, k, P * c:P * c + P], ident)
                    done(i, ("scT", b, c))
                ps = open_bank(pe, ("srT", b))
                for k in range(KT):
                    i = pe.transpose(ps[0:ROPE, P * k:P * k + P],
                                     ring[:, s, 1024:1152].rearrange("p (k n) -> p k n", k=KT)[:, k, :], ident)
                done(i, ("srT", b))

            def sample_scores(b):
                sel = sel8[:, b, :]
                rot = qrS[:, b, :, :].rearrange("p h q -> p (h q)")
                lat = [qs[:, c, b, :, :].rearrange("p h q -> p (h q)") for c in range(2)]
                for g in range(4):
                    pe.wait_ge(free(("skT", b, g)), count(("skT", b, g)))
                if b == 0:
                    pe.wait_ge(pairs_ready, 1)
                ps = open_bank(pe, ("sS", 2 * b))
                mm(ps[:, :], sel, cumS[:, 0:512], True, False)
                for g in range(4):
                    i = mm(ps[32 * g:32 * g + 32, :], qpair[:, b, g, :], skT[b % 2][:, g, :], False, True)
                done(i, ("sS", 2 * b))
                ps = open_bank(pe, ("sN", b))
                mm(ps[:, 0:P], sel, cumS[:, 512:640], True, False)
                for g in range(4):
                    i = mm(ps[32 * g:32 * g + 32, 0:P], qpair[:, b, g, :], fkT[:, g, 256:384], False, True)
                for c in range(2):
                    mm(ps[:, P:256], lat[c], ckvT[:, c, 256:384], False, False)
                i = mm(ps[:, P:256], rot, krT[0:ROPE, 256:384], False, True)
                done(i, ("sN", b))
                for c in range(2):
                    pe.wait_ge(free(("scT", b, c)), count(("scT", b, c)))
                pe.wait_ge(free(("srT", b)), count(("srT", b)))
                ps = open_bank(pe, ("sS", 2 * b + 1))
                for c in range(2):
                    mm(ps[:, :], lat[c], scT[b % 2][:, c, :], c == 0, False)
                i = mm(ps[:, :], rot, srT[b % 2], False, True)
                done(i, ("sS", 2 * b + 1))

            def sample_turn(n):
                pe.wait_ge(prob_ready, U_SAMPLE + n + 1)
                ps = open_bank(pe, ("sT", n))
                for k in range(KT):
                    i = pe.transpose(ps[:, P * k:P * k + P], sprob[n % 3][:, P * k:P * k + P], ident)
                done(i, ("sT", n))
                ps = open_bank(pe, ("sTn", n))
                i = pe.transpose(ps[:, 0:P], sprob[n % 3][:, 512:640], ident)
                done(i, ("sTn", n))

            def sample_values(n):
                b = n // 2
                pt = sprobT[n % 3]
                pe.wait_ge(free(("sT", n)), count(("sT", n)))
                pe.wait_ge(free(("sTn", n)), count(("sTn", n)))
                if n % 2 == 0:
                    s = arrived(pe, ("sv", b))
                    v3 = kview(s, KT, FW)
                    ps = open_bank(pe, ("sV", n))
                    for k in range(5):
                        for g in range(4):
                            v = v3[:, k, P * g:P * g + P] if k < KT else fv[:, 2, P * g:P * g + P]
                            i = mm(ps[32 * g:32 * g + 32, 0:P], pt[:, k, 32 * g:32 * g + 32], v, k == 0, k == 4)
                    done(i, ("sV", n))
                    used_last(pe, i, ("sv", b))
                else:
                    c3 = kview(place[("sc", b)] % NRING, KT, LORA)
                    ps = open_bank(pe, ("sV", n))
                    for c in range(2):
                        for k in range(5):
                            v = c3[:, k, P * c:P * c + P] if k < KT else ckv[:, 2, P * c:P * c + P]
                            i = mm(ps[:, P * c:P * c + P], v, pt[:, k, :], c == 0 and k == 0, k == 4)
                    done(i, ("sV", n))
                    used_last(pe, i, ("sc", b))

            def turn_back(key, rows, source):
                pe.wait_ge(free(source), count(source))
                ps = open_bank(pe, key)
                done(pe.transpose(ps[:, 0:P], rows, ident), key)

            pe.wait_ge(free("cumS"), count("cumS"))
            pe.wait_ge(free("cumN"), count("cumN"))
            turn_keys(0, range(4))
            turn_latents(0)
            for b in range(NB + 1):
                if b < NB:
                    sample_scores(b)
                if b >= 1:
                    for n in (2 * b - 2, 2 * b - 1):
                        sample_turn(n)
                if b + 1 < NB:
                    turn_keys(b + 1, (0, 1))
                if b >= 1:
                    sample_values(2 * b - 2)
                if b + 1 < NB:
                    turn_keys(b + 1, (2, 3))
                    turn_latents(b + 1)
                if b >= 1:
                    sample_values(2 * b - 1)
                    turn_back(("sO", b - 1), fox_rows[b % 2], ("sV", 2 * b - 2))

            s = arrived(pe, "uv")
            uv = kview(s, 2, 512)
            pe.wait_ge(free(("sV", SU - 1)), count(("sV", SU - 1)))
            for g in range(4):
                ps = open_bank(pe, ("mo", g))
                for e in range(2):
                    for c in range(2):
                        h = 2 * g + e
                        i = mm(ps[64 * e:64 * e + 64, 0:P].rearrange("p (b q) -> p b q", q=NQ), uv[:, c, 64 * h:64 * h + 64],
                               qs[:, c, :, h, :], c == 0, c == 1)
                done(i, ("mo", g))
            used_last(pe, i, "uv")
            for j in range(8):
                s = arrived(pe, ("g", j))
                for m in range(2):
                    i = project_T(("g", 2 * j + m), s, P * m, hT)
                used_last(pe, i, ("g", j))
            for g in range(4):
                pe.wait_ge(free(("mo", g)), count(("mo", g)))
            for j in range(2):
                if j:
                    rms_turn("mT", lambda t: (xn_ready, NT + t + 1), range(2))
                for w, src in (("w_o_fox", foxT), ("w_o_mla", mlaT)):
                    arrived(pe, (w, j))
                for n in range(4):
                    for w, src in (("w_o_fox", foxT), ("w_o_mla", mlaT)):
                        s = place[(w, j)] % NRING
                        key = (w, 4 * j + n)
                        ps = open_bank(pe, key)
                        for k in range(4):
                            i = mm(ps[:, 0:TOK], kview(s, 4, 512)[:, k, P * n:P * n + P], src[:, k, :], k == 0, k == 3)
                        done(i, key)
                        if n == 3:
                            used_last(pe, i, (w, j))
            def mem_project(w, halves=range(2)):
                for j in halves:
                    arrived(pe, (w, j))
                    for t in range(2):
                        i = project((w, t, j), (w, j), t, memT)
                    used_last(pe, i, (w, j))

            for t in range(2):
                for half in range(2):
                    pe.wait_ge(free(("mT", t, half)), count(("mT", t, half)))
            mem_project("xk")
            pe.wait_ge(mix_ready, KD)
            for j in range(4):
                arrived(pe, ("out", j))
                for t in range(NT):
                    i = project(("out", t, j), ("out", j), t, hT)
                used_last(pe, i, ("out", j))
            mem_project("xv", (0,))
            rms_turn("xT", lambda t: (xn_ready, NT + 2 + t + 1), range(NT))
            mem_project("xv", (1,))
            for t in range(2):
                for j in range(2):
                    pe.wait_ge(free(("xk", t, j)), count(("xk", t, j)))
            for h in range(XH):
                ps = open_bank(pe, ("mkT", h))
                for t in range(2):
                    i = pe.transpose(ps[:, P * t:P * t + P], mk[:, t, P * h:P * h + P], ident)
                done(i, ("mkT", h))
            for t in range(NT):
                for half in range(2):
                    pe.wait_ge(free(("xT", t, half)), count(("xT", t, half)))
            for j in range(2):
                s = arrived(pe, ("xq", j))
                for m in range(2):
                    i = project_T(("xq", 2 * j + m), s, P * m, hT)
                used_last(pe, i, ("xq", j))
            def mem_turn(b):
                s = arrived(pe, ("cm", b))
                k3 = kview(s, 2, FW)
                for hh in range(2):
                    ps = open_bank(pe, ("cK", b, hh))
                    for h in range(2):
                        for k in range(2):
                            i = pe.transpose(ps[:, 256 * h + P * k:256 * h + P * k + P],
                                             k3[:, k, P * (2 * hh + h):P * (2 * hh + h) + P], ident)
                    done(i, ("cK", b, hh))

            def mem_scores(b):
                for hh in range(2):
                    pe.wait_ge(free(("cK", b, hh)), count(("cK", b, hh)))
                if b == 0:
                    pe.wait_ge(pairs_ready, 2)
                ps = open_bank(pe, ("cS", b))
                for h in range(XH):
                    i = mm(ps[32 * h:32 * h + 32, 0:MEM], xpair[:, b, h, :], xkT[b % 2][:, h, :], True, True)
                done(i, ("cS", b))

            def mem_probs(b):
                pe.wait_ge(prob_ready, U_SMEM + b + 1)
                ps = open_bank(pe, ("cT", b))
                for k in range(2):
                    i = pe.transpose(ps[:, P * k:P * k + P], prob[b % 4][:, P * k:P * k + P], ident)
                done(i, ("cT", b))

            def mem_values(b):
                pe.wait_ge(free(("cT", b)), count(("cT", b)))
                s = place[("cm", b)] % NRING
                v3 = ring[:, s, 1024:2048].rearrange("p (k n) -> p k n", k=2)
                ps = open_bank(pe, ("cV", b))
                for k in range(2):
                    for h in range(XH):
                        i = mm(ps[32 * h:32 * h + 32, 0:P], probT[b % 4][:, P * k + 32 * h:P * k + 32 * h + 32],
                               v3[:, k, P * h:P * h + P], k == 0, k == 1)
                done(i, ("cV", b))
                used_last(pe, i, ("cm", b))

            mem_turn(0)
            for h in range(XH):
                pe.wait_ge(free(("xq", h)), count(("xq", h)))
                pe.wait_ge(free(("mkT", h)), count(("mkT", h)))
            for t in range(2):
                for j in range(2):
                    pe.wait_ge(free(("xv", t, j)), count(("xv", t, j)))
            pipeline(XUNITS, U_MEM, lambda i: mem_turn(1) if i == 1 else None)
            for u in range(NXU):
                pe.wait_ge(free(("V", U_MEM + u)), count(("V", U_MEM + u)))

            def cross_out(t, j):
                s = arrived(pe, ("xo", j))
                ps = open_bank(pe, ("xo", t, j))
                for k in range(4):
                    i = mm(ps[:, :], xoT[:, k, P * t:P * t + P], kview(s, 4, 512)[:, k, :], k == 0, k == 3)
                done(i, ("xo", t, j))
                used_last(pe, i, ("xo", j))

            for b in range(NB + 2):
                if b < NB:
                    mem_scores(b)
                if 1 <= b <= NB:
                    mem_probs(b - 1)
                if b >= 2:
                    turn_back(("cO", b - 2), mem_rows[b % 2], ("cV", b - 2))
                if 1 < b + 1 < NB:
                    mem_turn(b + 1)
                if b in CROSS_AT:
                    cross_out(*CROSS_AT[b])
                if 1 <= b <= NB:
                    mem_values(b - 1)
            pe.wait_ge(free(("cO", NB - 1)), count(("cO", NB - 1)))
            for j in range(2):
                cross_out(2, j)
            for tiles in (range(2), range(2, NT)):
                rms_turn("rT", lambda t: (xn_ready, 2 * NT + 2 + t + 1), tiles)
                for t in tiles:
                    ps = open_bank(pe, ("lg", t))
                    for k in range(KD):
                        if k % 4 == 0:
                            pe.wait_ge(free(("rT", t, k // 4)), count(("rT", t, k // 4)))
                        i = mm(ps[:, 0:NE], hT[:, k, P * t:P * t + P], wr[:, k, :], k == 0, k == KD - 1)
                    done(i, ("lg", t))
            rank = open_bank(pe, "rank")
            for t in range(NT):
                pe.wait_ge(masks_ready, t + 1)
                mm(rank[:, NE * t:NE * t + NE], con[:, t0:t0 + P], chosen[:, t, :], t == 0, True)
                for later in range(t + 1, NT):
                    mm(rank[:, NE * later:NE * later + NE], ones, chosen[:, t, :], False, False)
                i = mm(rank[:, 96:128], ones, chosen[:, t, :], False, t == NT - 1)
            done(i, "rank")
            def pair_table(name, columns):
                for t in range(NT):
                    ps = open_bank(pe, (name, t))
                    for k in range(TOPK):
                        i = mm(ps[:, P * k:P * k + P], bc(columns[:, TOPK * t + k:TOPK * t + k + 1], [P, P]), ident,
                               k == 0, k == TOPK - 1)
                    done(i, (name, t))

            pe.wait_ge(gate_ready, 1)
            pair_table("pair_gate", gatew)
            pe.wait_ge(pick_ready, 1)
            ps = open_bank(pe, "index")
            for n in range(NT * TOPK):
                i = mm(ps[0:CAP, 0:NBLK], pick[:, n, :], blk1[:, n, :], n == 0, n == NT * TOPK - 1)
            done(i, "index")
            pair_table("pair_row", slotf)
            for key in list(groups)[-8:]:
                pe.wait_ge(free(key), count(key))

            gate, up, xTp, aTp, yp = psum[0], psum[1], psum[2], psum[3], psum[4]

            def turn_rows():
                for k in range(KD):
                    i = pe.transpose(xTp[:, CAP * k:CAP * k + CAP], xg[:, P * k:P * k + P], ident[0:CAP, 0:CAP])
                i.then_inc(xT_full, 1)

            def add_shares(b, steps):
                if 0 in steps:
                    pe.wait_ge(share_ready, b + 1)
                for i in steps:
                    t, half = i // 2, i % 2
                    if i >= 3:
                        pe.wait_ge(shares_added, b * 6 + (i - 2))
                    o = slice(CAP * half, CAP * half + CAP)
                    mm(psum[5 + i % 3][:, :], share[o, P * t:P * t + P], ysb[o, :], True, True).then_inc(shares_full, 1)

            pe.wait_ge(blocks_ready, 1)
            nblk = pe.value_load(blocks_i[0:1, 0:1], min_val=NE, max_val=NBLK)
            pe.wait_ge(bias_moved, 96)
            pe.wait_ge(rows_gathered, 16)
            turn_rows()
            with pe.Fori(0, nblk) as b:
                pe.wait_ge(xT_ready, b + 1)
                for half in range(2):
                    o = slice(CAP * half, CAP * half + CAP)
                    mm(gate[o, :], sel, bias3[:, 512 * half:512 * half + 512], True, False)
                    mm(up[o, :], sel, bias3[:, 1024 + 512 * half:1536 + 512 * half], True, False)
                for c in range(KD):
                    s = GU_SLOT[c]
                    pe.wait_ge(ring_loaded[s], b * 16 + (GU_LOADS[c] + 16))
                    for q in range(4):
                        o = (gate, up)[q // 2][CAP * (q % 2):CAP * (q % 2) + CAP, :]
                        i = mm(o, xT[:, c, :], ring[:, s, 512 * q:512 * q + 512], False, c == KD - 1)
                    i.then_inc(ring_used[s], 1)
                pe.wait_ge(y_copied, b + 1)
                pe.wait_ge(rows_gathered, b * 16 + 32)
                for half in range(2):
                    mm(yp[CAP * half:CAP * half + CAP, :], sel, bias3[:, 2048 + 512 * half:2560 + 512 * half], True, False)
                turn_rows()
                add_shares(b, (0, 1, 2))
                pe.wait_ge(act_ready, b + 1)
                for k in range(4):
                    i = pe.transpose(aTp[:, P * k:P * k + P], hid[:, P * k:P * k + P], ident)
                i.then_inc(actT_full, 1)
                add_shares(b, (3, 4, 5))
                pe.wait_ge(actT_ready, b + 1)
                for c in range(KD):
                    s = DOWN_SLOT[c // 2]
                    if c % 2 == 0:
                        pe.wait_ge(ring_loaded[s], b * 16 + 16)
                    l = actT[:, 2 * (c % 4) + c // 4, :]
                    for half in range(2):
                        a = 1024 * (c % 2) + 512 * half
                        i = mm(yp[CAP * half:CAP * half + CAP, :], l, ring[:, s, a:a + 512], False, c == KD - 1)
                    if c % 2:
                        i.then_inc(ring_used[s], 1)
            pe.wait_ge(y_copied, nblk + 1)
            add_shares(nblk, range(6))

        @block.sync
        def _(sp):
            for t in range(NT):
                src = d["x_prompt"][0, P * t:P * t + P, :] if t < 2 else d["x_sample"].rearrange("b q n -> (b q) n")
                sp.dma_start(xr[:, t, :], src).then_inc(x_loaded[t], 16)
            for n, (key, parts) in enumerate(stream):
                if n >= NRING:
                    g = last_group[stream[n - NRING][0]]
                    sp.wait_ge(bank_full[g % 8], g // 8 + 1)
                for dst, src in parts:
                    sp.dma_start(dst(n % NRING), src).then_inc(ring_loaded[n % NRING], 16)
            w_gu = d["w_gu"][0].rearrange("e (k p) n -> e p k n", p=P)
            w_down = d["w_down"][0].rearrange("e (k p) n -> e p k n", p=P)

            def load_in(expert, c):
                sp.dma_start(ring[:, GU_SLOT[c], :], w_gu[expert, :, c, :]).then_inc(ring_loaded[GU_SLOT[c]], 16)

            def load_down(expert, c):
                sp.dma_start(kview(DOWN_SLOT[c], 2, D), w_down[expert, :, 2 * c:2 * c + 2, :])\
                    .then_inc(ring_loaded[DOWN_SLOT[c]], 16)

            for g, c in sorted((last_group[stream[NPRE + c - NRING][0]], c) for c in range(KD)):
                sp.wait_ge(bank_full[g % 8], g // 8 + 1)
                load_in(0, c)
            sp.wait_ge(bias_moved, 96)
            sp.wait_ge(full(("cT", NB - 1)), count(("cT", NB - 1)))
            sp.wait_ge(full(("rT", 2, 1)), count(("rT", 2, 1)))
            sp.wait_ge(scratch_written, 16)
            for c in range(4):
                load_down(0, c)

            def block_loads(expert, b):
                for c in range(KD):
                    sp.wait_ge(ring_used[GU_SLOT[c]], b)
                    load_in(expert, c)
                for c in range(4):
                    sp.wait_ge(ring_used[DOWN_SLOT[c]], b)
                    load_down(expert, c)

            with sp.Fori(1, NE) as b:
                block_loads(b, b)
            sp.wait_ge(blocks_ready, 1)
            nblk = sp.value_load(blocks_i[0:1, 0:1], min_val=NE, max_val=NBLK)
            sp.wait_ge(bexp_ready, 1)
            with sp.If(nblk > NE):
                with sp.Fori(NE, nblk) as b:
                    expert = sp.value_load(bexp_i[0:1, bass.ds(b, 1)], min_val=0, max_val=NE - 1)
                    block_loads(expert, b)
            for t in range(NT):
                sp.wait_ge(fin_ready, t + 1)
                dst = out["y_prompt"][0, P * t:P * t + P, :] if t < 2 else out["y_sample"].rearrange("b q n -> (b q) n")
                sp.dma_start(dst, yout[:, t, :]).then_inc(y_out, 16)
            sp.wait_ge(y_out, 16 * NT)

        @block.gpsimd
        def _(pool):
            def rows3(name, width):
                a = out["p_" + name]
                b = out["s_" + name]
                pa = a.rearrange("l b (t p) h n -> p (l b t) (h n)" if len(a.shape) == 5 else "l b (t p) n -> p (l b t) n", p=P)
                sa = b.rearrange("l b q h n -> (l b q) (h n)" if len(b.shape) == 5 else "l b q n -> (l b q) n")
                return pa, sa

            def put(name, tile3, s):
                pa, sa = rows3(name, 0)
                pool.dma_start(pa, tile3[:, 0:2, :]).then_inc(s, 16)
                pool.dma_start(sa, tile3[:, 2, :]).then_inc(s, 16)

            pool.wait_ge(free(("fk", 2, 1)), count(("fk", 2, 1)))
            put("fox_k", fk, fk_written)
            pool.wait_ge(krope_ready, NT)
            put("mla_krope", krope, outputs_written)
            pool.wait_ge(ckv_ready, NT)
            put("mla_ckv", ckv, ckv_written)
            pool.wait_ge(logf_ready, NT)
            put("fox_logf", logf, outputs_written)
            pool.wait_ge(free(("fv", 2, 1)), count(("fv", 2, 1)))
            put("fox_v", fv, fv_written)
            pool.wait_ge(full(("sS", SU - 1)), count(("sS", SU - 1)))
            pool.wait_ge(full(("mo", 3)), count(("mo", 3)))
            pool.dma_start(memx, d["mem_prompt"].rearrange("b (t p) n -> p (b t) n", p=P)).then_inc(mem_loaded, 16)
            pool.dma_start(xr[:, 0:2, :], d["x_prompt"].rearrange("b (t p) n -> p (b t) n", p=P)).then_inc(x_again, 16)
            pool.dma_start(xr[:, 2, :], d["x_sample"].rearrange("b q n -> (b q) n")).then_inc(x_again, 16)
            for w, m, o in (("xk", mk, "p_mem_k"), ("xv", mv, "p_mem_v")):
                pool.wait_ge(free((w, 1, 1)), count((w, 1, 1)))
                pool.dma_start(out[o].rearrange("l b (t p) h n -> p (l b t) (h n)", p=P), m).then_inc(mk_written, 16)
            pool.wait_ge(mix_ready, KD)
            pool.wait_ge(ckv_written, 32)
            for c in range(3):
                src = d["b_gu"][0, :, 1024 * c:1024 * c + 1024] if c < 2 else d["b_down"][0]
                pool.dma_start(bstage, src).then_inc(bias_loaded, 16)
                pool.wait_ge(bias_loaded, 16 * c + 16)
                o = slice(1024 * c, 1024 * c + 1024)
                nc.gpsimd.tensor_copy(bias3[0:NE, o], bstage).then_inc(bias_step, 1)
                pool.wait_ge(bias_step, 5 * c + 1)
                nc.gpsimd.tensor_tensor(bstage, bstage, bias3[0:NE, o], ALU.subtract).then_inc(bias_step, 1)
                pool.wait_ge(bias_step, 5 * c + 2)
                nc.gpsimd.tensor_copy(bmid, bstage).then_inc(bias_step, 1)
                pool.wait_ge(bias_step, 5 * c + 3)
                pool.dma_start(bias3[32:64, o], bmid).then_inc(bias_moved, 16)
                nc.gpsimd.tensor_tensor(bstage, bstage, bmid, ALU.subtract).then_inc(bias_step, 1)
                pool.wait_ge(bias_moved, 32 * c + 16)
                pool.wait_ge(bias_step, 5 * c + 4)
                nc.gpsimd.tensor_copy(bmid, bstage).then_inc(bias_step, 1)
                pool.wait_ge(bias_step, 5 * c + 5)
                pool.dma_start(bias3[64:96, o], bmid).then_inc(bias_moved, 16)
                pool.wait_ge(bias_moved, 32 * c + 32)
            for t in range(NT):
                pool.wait_ge(xn_ready, 2 * NT + 2 + t + 1)
            pool.dma_start(x3_dram.rearrange("(t p) n -> p t n", p=P), xn2).then_inc(scratch_written, 16)
            pool.wait_ge(free("index"), count("index"))
            pool.wait_ge(blocks_ready, 1)
            pool.wait_ge(scratch_written, 16)
            nblk = pool.value_load(blocks_i[0:1, 0:1], min_val=NE, max_val=NBLK)

            def gather(n, copied, copies):
                nc.gpsimd.tensor_copy(idx_col[:, :], idx_all[:, bass.ds(n, 1)]).then_inc(copied, 1)
                pool.wait_ge(blocks_ready, 1)
                pool.wait_ge(copied, copies)
                pool.indirect_dma_start(out=xg, out_offset=None, in_=x3_dram,
                                        in_offset=bass.IndirectOffsetOnAxis(ap=idx_col[:, 0:1], axis=0))\
                    .then_inc(rows_gathered, 16)

            gather(0, first_copied, 1)
            with pool.Fori(1, nblk + 1) as n:
                pool.wait_ge(rows_gathered, n * 16)
                pool.wait_ge(xT_full, n)
                gather(n, idx_copied, n)
            pool.wait_ge(outputs_written, 64)
            pool.wait_ge(fk_written, 32)
            pool.wait_ge(fv_written, 32)
            pool.wait_ge(mk_written, 32)

        def softmax_cols(u):
            a = 10 * (u % 4)
            return cols[:, a:a + 2], cols[:, a + 2:a + 4], cols[:, a + 4:a + 6], cols[:, a + 6:a + 8], cols[:, a + 8:a + 9]

        ssq = cols[:, 40:54]
        lz, lneg, lexp, lln = (probTs[:, 1536 + 24 * i:1560 + 24 * i].rearrange("p (t h) -> p t h", t=NT) for i in range(4))
        rtmp = probTs[:, 1024:1536].rearrange("p (a h r) -> p a h r", a=4, h=H)
        rstd = sb("rstd", [P, 32])
        nrt = rstd[:, 24:32]
        btmp = [probTs[:, TOK * i:TOK * i + TOK] for i in range(2)]

        def turn_key(u):
            return ("T", u) if u < U_SMEM else ("cT", u - U_SMEM)

        @block.vector
        def _(dve):
            v = nc.vector
            steps = [0]

            def link(ins):
                steps[0] += 1
                ins.then_inc(dve_step, 1)
                dve.wait_ge(dve_step, steps[0])

            def take(key):
                dve.wait_ge(full(key), count(key))
                return bank(key)

            def give(ins, key):
                ins.then_inc(free(key), 1)

            def inverse_root(y, square, width):
                n = y.shape[1]
                x, w = nrt[:, 0:n], nrt[:, 4:4 + n]
                link(v.tensor_scalar(x, square, 1.0 / width, EPS, ALU.mult, ALU.add))
                link(v.tensor_scalar(y.bitcast(I32), x.bitcast(I32), 1, None, ALU.logical_shift_right))
                link(v.tensor_scalar(y.bitcast(I32), y.bitcast(I32), -1.0, float(0x5F3759DF), ALU.mult, ALU.add))
                link(v.tensor_scalar(x, x, -0.5, None, ALU.mult))
                for _ in range(3):
                    link(v.tensor_tensor(w, y, y, ALU.mult))
                    link(v.tensor_tensor(w, w, x, ALU.mult))
                    link(v.scalar_tensor_tensor(y, w, 1.5, y, ALU.add, ALU.mult))

            def rms_rows(n, tiles, src, dst, t0=0):
                dve.wait_ge(square_sum, n + tiles)
                inverse_root(rstd[:, n:n + tiles], ssq[:, n:n + tiles], D)
                for t in range(tiles):
                    v.tensor_scalar(dst[:, t0 + t, :], src[:, t0 + t, :], rstd[:, n + t:n + t + 1], None, ALU.mult)\
                        .then_inc(xn_ready, 1)

            def scale_turned(name, t, g, dst):
                for half in range(2):
                    ps = take((name, t, half))
                    give(v.tensor_tensor(dst[:, 4 * half:4 * half + 4, P * t:P * t + P],
                                         ps[:, :].rearrange("p (c q) -> p c q", c=4),
                                         bc(g[:, 4 * half:4 * half + 4].unsqueeze(2), [P, 4, P]), ALU.mult), (name, t, half))

            def copy_out(key, dst, n=None):
                ps = take(key)
                give(v.tensor_copy(dst, ps[:, 0:n] if n else ps), key)

            def rope(src, dst, t, heads, signal, key):
                h2 = ROPE // 2
                c, s = (bc(cc(n)[:, h2 * t:h2 * t + h2].unsqueeze(1), [P, heads, h2]) for n in ("cos", "sin"))
                x1, x2 = src[:, :, 0:h2], src[:, :, h2:ROPE]
                a = [rtmp[:, n, 0:heads, :] for n in range(4)]
                if t:
                    dve.wait_ge(signal, t)
                v.tensor_tensor(a[0], x1, c, ALU.mult)
                v.tensor_tensor(a[1], x2, s, ALU.mult)
                v.tensor_tensor(a[2], x2, c, ALU.mult)
                give(v.tensor_tensor(a[3], x1, s, ALU.mult), key)
                dve.wait_ge(free(key), count(key))
                link(v.tensor_tensor(dst[:, :, 0:h2], a[0], a[1], ALU.subtract))
                v.tensor_tensor(dst[:, :, h2:ROPE], a[2], a[3], ALU.add).then_inc(signal, 1)

            rms_rows(0, NT, xr, xr)
            dve.wait_ge(g_mix_loaded, 16)
            for t in range(NT):
                scale_turned("hT", t, gm_c, hT)
            v.memset(xflat[:, 0:1024], 0.0).then_inc(zeroed, 1)
            for j in range(2):
                for t in range(NT):
                    copy_out(("fk", t, j), fk[:, t, 256 * j:256 * j + 256], 256)
            dve.wait_ge(consts_loaded, 16 * NLOADS)
            for t in range(NT):
                ps = take(("fl", t))
                link(v.tensor_tensor(lz[:, t, :], ps[:, 0:H], bf_b, ALU.add))
                link(v.tensor_scalar(lneg[:, t, :], lz[:, t, :], -1.0, None, ALU.mult))
                v.tensor_tensor(lneg[:, t, :], lz[:, t, :], lneg[:, t, :], ALU.min).then_inc(logf_part, 1)
                rope(ps[:, H:H + ROPE].unsqueeze(1), krope[:, t:t + 1, :], t, 1, krope_ready, ("fl", t))
            for name, rows, c0 in (("kv", ckv, 54), ("qc", qc, 57)):
                for t in range(NT):
                    copy_out((name, t), rows[:, t, :], 256)
                    dve.wait_ge(free((name, t)), count((name, t)))
                    last = v.tensor_tensor_reduce(junk2, rows[:, t, :], rows[:, t, :], 1.0, 0.0, ALU.mult, ALU.add, cols[:, c0 + t:c0 + t + 1])
                link(last)
                a = 14 if name == "kv" else 17
                inverse_root(rstd[:, a:a + NT], cols[:, c0:c0 + NT], LORA)
                for t in range(NT):
                    if name == "kv":
                        v.scalar_tensor_tensor(ckv[:, t, :], ckv[:, t, :], rstd[:, a + t:a + t + 1], gkv_b[:, :], ALU.mult, ALU.mult)\
                            .then_inc(ckv_ready, 1)
                    else:
                        v.tensor_scalar(qc[:, t, :], qc[:, t, :], rstd[:, a + t:a + t + 1], None, ALU.mult).then_inc(qc_ready, 1)
            for t in range(NT):
                dve.wait_ge(logit_exp, t + 1)
                v.scalar_tensor_tensor(logf[:, t, :], lz[:, t, :], 0.0, lln[:, t, :], ALU.min, ALU.subtract).then_inc(logf_ready, 1)
            dve.wait_ge(logf_ready, NT)
            v.tensor_copy(logfw.rearrange("p (b h) -> p b h", b=NB), bc(logf[:, 2:3, :], [P, NB, H])).then_inc(logf_wide, 1)
            for c in range(2):
                ps = take(("qcT", c))
                give(v.tensor_scalar(qcT[:, c, :], ps[:, 0:TOK], gq_c[:, c:c + 1], None, ALU.mult), ("qcT", c))
            ps = take("cumP")
            v.tensor_copy(cumT[0:H, :], ps[0:H, 0:256])
            give(v.tensor_copy(cumT[64:64 + H, :], ps[0:H, 0:256]), "cumP")
            ps = take("cumS")
            give(v.tensor_copy(cumS[:, 0:512], ps[0:64, :]), "cumS")
            ps = take("cumN")
            give(v.tensor_copy(cumS[:, 512:640], ps[0:64, 0:P]), "cumN")
            for t in range(NT):
                ps = take(("qr", t))
                rope(ps[:, 0:256].rearrange("p (h r) -> p h r", r=ROPE), qrope[:, t, :, :], t, H, qrope_ready, ("qr", t))
            for odd in range(2):
                ps = take(("ql", odd, 0))
                give(v.tensor_copy(qs[:, 0, :, odd::2, :].rearrange("p b h q -> p h b q"),
                                   ps[:, :].rearrange("p (h b q) -> p h b q", h=4, q=NQ)), ("ql", odd, 0))
            dve.wait_ge(zeroed, 1)
            dve.wait_ge(free(("fqT", 3)), count(("fqT", 3)))
            dve.wait_ge(free(("qrT", 1)), count(("qrT", 1)))
            a8 = CONST["neg8"][0]
            v.tensor_copy(sel8.rearrange("p b (h q) -> p (b h) q", h=H), bc(con[64:128, a8:a8 + 64].unsqueeze(2), [64, 64, NQ]))
            for e in range(2):
                v.tensor_copy(qpair[64 * e:64 * e + 64, :, :, NQ * e:NQ * e + NQ],
                              fqT[64 * e:64 * e + 64, :, 256:384].rearrange("p g (b q) -> p b g q", q=NQ))
            for e in range(4):
                for c in range(2):
                    last = v.tensor_copy(qrS[:, :, 4 * c + e, :],
                                         qrT[32 * e:32 * e + 32, c, 256:384].rearrange("p (b q) -> p b q", q=NQ))
            last.then_inc(pairs_ready, 1)

            def part1(u, unit):
                kind, t, hs = unit
                w = width(kind, t)
                mx, nm, sm, rc, _ = softmax_cols(u)
                ps = take(("S", u))
                src = ps[:, 0:2 * w].rearrange("p (n w) -> p n w", n=2)
                if kind != "mem":
                    if u >= 4:
                        dve.wait_ge(full(("T", u - 4)), count(("T", u - 4)))
                    a = CONST["z1" if kind == "fox" else "z2"][0]
                    mask = con[:, a + P * (1 - t):a + 2 * P]
                    dst = prob[u % 4][:, 0:2 * w].rearrange("p (n w) -> p n w", n=2)
                    give(v.tensor_tensor(dst, src, bc(mask.unsqueeze(1), [P, 2, w]), ALU.add), ("S", u))
                    dve.wait_ge(free(("S", u)), count(("S", u)))
                    src = dst
                link(v.tensor_reduce(mx, src, X, ALU.max))
                v.tensor_scalar(nm, mx, -{"fox": FOX_SCALE, "mla": MLA_SCALE, "mem": X_SCALE}[kind], None, ALU.mult)\
                    .then_inc(score_max, 1)

            def part2(u, unit):
                kind, t, hs = unit
                w = width(kind, t)
                mx, nm, sm, rc, _ = softmax_cols(u)
                dve.wait_ge(exp_done, u + 1)
                link(v.reciprocal(rc, sm))
                dst = prob[u % 4][:, 0:2 * w].rearrange("p (n w) -> p n w", n=2)
                v.tensor_tensor(dst, dst, bc(rc.unsqueeze(2), [P, 2, w]), ALU.mult).then_inc(prob_ready, 1)

            def pipeline(units, u0, between=None):
                for i in range(len(units) + 1):
                    if i < len(units):
                        part1(u0 + i, units[i])
                    if between:
                        between(i)
                    if i:
                        part2(u0 + i - 1, units[i - 1])

            def between_units(i):
                if 3 <= i < 7:
                    copy_out(("kn", i - 3), kn[:, i - 3, :], 256)

            pipeline(UNITS, 0, between_units)

            def sample_part1(n):
                b, u = n // 2, U_SAMPLE + n
                mx, nm, sm, rc, m1 = softmax_cols(u)
                p = sprob[n % 3]
                if n % 2 == 0:
                    v.tensor_reduce(mx[:, 0:1], take(("sS", n))[:, :], X, ALU.max)
                new = take(("sN", b))
                if n >= 3:
                    dve.wait_ge(full(("sTn", n - 3)), count(("sTn", n - 3)))
                a = CONST["mlanew" if n % 2 else "foxnew"][0] + NQ * (7 - b)
                i = v.tensor_tensor(p[:, 512:640], new[:, P * (n % 2):P * (n % 2) + P], con[:, a:a + P], ALU.add)
                if n % 2:
                    give(i, ("sN", b))
                    dve.wait_ge(free(("sN", b)), count(("sN", b)))
                else:
                    link(i)
                if n % 2:
                    v.tensor_reduce(mx[:, 0:1], take(("sS", n))[:, :], X, ALU.max)
                link(v.tensor_reduce(mx[:, 1:2], p[:, 512:640], X, ALU.max))
                link(v.tensor_reduce(m1, mx, X, ALU.max))
                v.tensor_scalar(nm[:, 0:1], m1, -(MLA_SCALE if n % 2 else FOX_SCALE), None, ALU.mult).then_inc(score_max, 1)

            def sample_part2(n):
                u = U_SAMPLE + n
                mx, nm, sm, rc, m1 = softmax_cols(u)
                dve.wait_ge(exp_done, u + 1)
                link(v.tensor_tensor(rc[:, 0:1], sm[:, 0:1], sm[:, 1:2], ALU.add))
                link(v.reciprocal(rc[:, 1:2], rc[:, 0:1]))
                v.tensor_scalar(sprob[n % 3], sprob[n % 3], rc[:, 1:2], None, ALU.mult).then_inc(prob_ready, 1)

            def cache_out(b):
                if b >= 2:
                    dve.wait_ge(full(("sS", 2 * b - 3)), count(("sS", 2 * b - 3)))
                for g in range(2):
                    copy_out(("skT", b, g), skT[b % 2][:, g, :])
                copy_out(("scT", b, 0), scT[b % 2][:, 0, :])

            dve.wait_ge(fk_written, 32)
            cache_out(0)
            for b in range(NB):
                sample_part1(2 * b)
                sample_part1(2 * b + 1)
                if b + 1 < NB:
                    cache_out(b + 1)
                sample_part2(2 * b)
                sample_part2(2 * b + 1)
            dve.wait_ge(mem_loaded, 16)
            rms_rows(NT, 2, memx, memx)
            for n in range(KD):
                if n == 4:
                    for t in range(2):
                        scale_turned("mT", t, gmem_c, memT)
                ps = take(("w_o_fox", n))
                dve.wait_ge(gates_ready, KD + n + 1)
                give(v.tensor_tensor(hT[:, n, :], ps[:, 0:TOK], gates[:, n, :], ALU.mult), ("w_o_fox", n))
                ps = take(("w_o_mla", n))
                if n >= 2:
                    dve.wait_ge(mix_ready, n - 1)
                give(v.tensor_tensor(btmp[n % 2], ps[:, 0:TOK], gates[:, KD + n, :], ALU.mult), ("w_o_mla", n))
                dve.wait_ge(free(("w_o_mla", n)), count(("w_o_mla", n)))
                v.tensor_tensor(hT[:, n, :], hT[:, n, :], btmp[n % 2], ALU.add).then_inc(mix_ready, 1)
            dve.wait_ge(x_again, 32)
            for j in range(4):
                for t in range(NT):
                    ps = take(("out", t, j))
                    o = xr[:, t, 256 * j:256 * j + 256]
                    give(v.tensor_tensor(o, o, ps[:, 0:256], ALU.add), ("out", t, j))
            rms_rows(NT + 2, NT, xr, xn2)
            for t in range(NT):
                scale_turned("xT", t, gx_c, hT)
            dve.wait_ge(fv_written, 32)
            link(v.memset(xpair, 0.0))
            dve.wait_ge(free(("xq", 3)), count(("xq", 3)))
            v.tensor_copy(xpair[:, :, :, 0:NQ], xqT[:, :, 256:384].rearrange("p h (b q) -> p b h q", q=NQ)).then_inc(pairs_ready, 1)

            def mem_part1(b):
                u = U_SMEM + b
                mx, nm, sm, rc, _ = softmax_cols(u)
                ps = take(("cS", b))
                link(v.tensor_reduce(mx[:, 0:1], ps[:, 0:MEM], X, ALU.max))
                v.tensor_scalar(nm[:, 0:1], mx[:, 0:1], -X_SCALE, None, ALU.mult).then_inc(score_max, 1)

            def mem_part2(b):
                u = U_SMEM + b
                mx, nm, sm, rc, _ = softmax_cols(u)
                dve.wait_ge(exp_done, u + 1)
                link(v.reciprocal(rc[:, 0:1], sm[:, 0:1]))
                p = prob[b % 4][:, 0:MEM]
                v.tensor_scalar(p, p, rc[:, 0:1], None, ALU.mult).then_inc(prob_ready, 1)

            def mem_out(b):
                if b >= 2:
                    dve.wait_ge(full(("cS", b - 2)), count(("cS", b - 2)))
                ps = take(("cK", b, 0))
                give(v.tensor_copy(xkT[b % 2][:, 0:2, :], ps[:, :].rearrange("p (h s) -> p h s", h=2)), ("cK", b, 0))

            def cross_add(t, j):
                ps = take(("xo", t, j))
                o = xr[:, t, 512 * j:512 * j + 512]
                give(v.tensor_tensor(o, o, ps[:, :], ALU.add), ("xo", t, j))

            mem_out(0)
            pipeline(XUNITS, U_MEM, lambda i: mem_out(1) if i == 1 else None)
            for b in range(NB):
                mem_part1(b)
                if 1 < b + 1 < NB:
                    mem_out(b + 1)
                mem_part2(b)
                if b in CROSS_AT:
                    cross_add(*CROSS_AT[b])
            rms_rows(2 * NT + 2, 2, xr, xn2)
            for j in range(2):
                cross_add(2, j)
            for t in range(2):
                scale_turned("rT", t, gf_c, hT)
            rms_rows(2 * NT + 4, 1, xr, xn2, t0=2)

            iota32 = cc("iota")[:, 0:NE]
            for t in range(NT):
                if t == 1:
                    scale_turned("rT", 2, gf_c, hT)
                ps = take(("lg", t))
                give(v.tensor_tensor(logit[:, t, :], ps[:, 0:NE], br_b, ALU.add), ("lg", t))
                dve.wait_ge(free(("lg", t)), count(("lg", t)))
                link(v.max(top8[:, t, :], logit[:, t, :]))
                link(v.max_index(idx8[:, t, :], top8[:, t, :], logit[:, t, :]))
                link(v.tensor_copy(idxf[:, t, :], idx8[:, t, :]))
                v.tensor_scalar(ntop[:, t:t + 1], top8[:, t, 0:1], -1.0, None, ALU.mult).then_inc(top_shift, 1)
                for k in range(TOPK):
                    last = v.tensor_scalar(onehot[:, 4 * t + k, :], iota32, idxf[:, t, k:k + 1], None, ALU.is_equal)
                link(last)
                v.tensor_reduce(chosen[:, t, :], onehot[:, 4 * t:4 * t + 4, :].rearrange("p k e -> p e k"), X, ALU.add)\
                    .then_inc(masks_ready, 1)
            for t in range(NT):
                dve.wait_ge(top_exp, t + 1)
                link(v.reciprocal(esum[:, t:t + 1], esum[:, t:t + 1]))
                last = v.tensor_scalar(gatew[:, 4 * t:4 * t + 4], top8[:, t, 0:TOPK], esum[:, t:t + 1], None, ALU.mult)
            last.then_inc(gate_ready, 1)
            ps = take("rank")
            link(v.tensor_scalar(cnt, ps[:, 96:128], float(CAP - 1), None, ALU.add))
            link(v.tensor_scalar(cnt, cnt, CAP.bit_length() - 1, None, ALU.logical_shift_right))
            link(v.tensor_scalar(novr, cnt, -1.0, 0.0, ALU.add, ALU.max))
            link(v.tensor_tensor_scan(oincl, novr, cc("zero"), 0.0, ALU.add, ALU.add))
            v.tensor_scalar(blocks_i[0:1, :], oincl[0:1, NE - 1:NE], float(NE), None, ALU.add).then_inc(blocks_ready, 1)
            link(v.tensor_tensor(moved, oincl, novr, ALU.subtract))
            link(v.tensor_scalar(moved, moved, float(CAP), float(CAP * (NE - 1)), ALU.mult, ALU.add))
            link(v.tensor_tensor(moved, moved, cc("i64")[:, 0:NE], ALU.subtract))
            rank = ps[:, 0:96].rearrange("p (t e) -> p t e", t=NT)
            link(v.tensor_scalar(slot_d, rank, float(CAP), None, ALU.is_ge))
            link(v.tensor_tensor(slot_d, slot_d, bc(moved.unsqueeze(1), [P, NT, NE]), ALU.mult))
            link(v.tensor_tensor(slot_d, slot_d, bc(cc("i64")[:, 0:NE].unsqueeze(1), [P, NT, NE]), ALU.add))
            give(v.tensor_tensor(slot_e, slot_d, rank, ALU.add), "rank")
            dve.wait_ge(free("rank"), count("rank"))
            for t in range(NT):
                last = v.tensor_tensor(e_tmp[:, 4 * t:4 * t + 4, :], onehot[:, 4 * t:4 * t + 4, :],
                                       bc(slot_e[:, t:t + 1, :], [P, TOPK, NE]), ALU.mult)
            link(last)
            v.tensor_reduce(slotf, e_tmp, X, ALU.add).then_inc(slot_ready, 1)
            dve.wait_ge(slot_ready, 1)
            n12 = NT * TOPK
            link(v.tensor_copy(slot_i, slotf))
            link(v.tensor_scalar(row_i, slot_i, CAP - 1, None, ALU.bitwise_and))
            link(v.tensor_scalar(blk_i, slot_i, CAP.bit_length() - 1, None, ALU.logical_shift_right))
            link(v.tensor_copy(inblk, row_i))
            link(v.tensor_copy(blkf, blk_i))
            link(v.tensor_tensor(blk1, bc(blkf.unsqueeze(2), [P, n12, NBLK]), bc(cc("iota")[:, 0:NBLK].unsqueeze(1), [P, n12, NBLK]), ALU.is_equal))
            by_tile = blk1.rearrange("p (t k) b -> p t k b", t=NT)
            v.tensor_tensor(pick, bc(inblk.unsqueeze(2), [P, n12, CAP]), bc(cc("iota").unsqueeze(1), [P, n12, CAP]), ALU.is_equal)
            v.tensor_tensor(by_tile, by_tile, bc(cc("tokid").unsqueeze(2).unsqueeze(3), [P, NT, TOPK, NBLK]), ALU.mult)\
                .then_inc(pick_ready, 1)
            dve.wait_ge(mk_written, 32)
            link(v.memset(idx_all[:, NBLK:NBLK + 1], 0))
            ps = take("index")
            give(v.tensor_copy(idx_all[:, 0:NBLK], ps[0:CAP, 0:NBLK]), "index")
            link(v.tensor_tensor(o_cmp, bc(oincl.unsqueeze(1), [P, OVER, NE]), bc(cc("iota")[:, 0:OVER].unsqueeze(2), [P, OVER, NE]), ALU.is_le))
            link(v.tensor_reduce(bexp[:, NE:NBLK], o_cmp, X, ALU.add))
            link(v.tensor_copy(bexp[:, 0:NE], iota32))
            link(v.memset(bexp[:, NBLK:NBLK + 1], 0.0))
            v.tensor_scalar(bexp_i, bexp[0:1, 0:NBLK], float(NE - 1), None, ALU.min).then_inc(bexp_ready, 1)
            link(v.memset(ysb, 0.0))
            v.memset(share, 0.0).then_inc(share_ready, 1)

            gate, up, xTp = psum[0], psum[1], psum[2]

            def xT_out(n):
                dve.wait_ge(xT_full, n)
                v.tensor_tensor(xT, xTp[:, :].rearrange("p (k t) -> p k t", k=KD), bc(gf_c.unsqueeze(2), [P, KD, CAP]), ALU.mult)\
                    .then_inc(xT_ready, 1)

            def choose(dst, b):
                return v.tensor_scalar(dst, bc(cc("pmod", 96), [96, CAP]), bexp[0:96, b], None, ALU.is_equal)

            def add_shares(b):
                for i in range(6):
                    dve.wait_ge(shares_full, b * 6 + (i + 1))
                    x = xr[:, i // 2, 512 * (i % 2):512 * (i % 2) + 512]
                    v.tensor_tensor(x, x, psum[5 + i % 3][:, :], ALU.add).then_inc(shares_added, 1)

            dve.wait_ge(blocks_ready, 1)
            nblk = dve.value_load(blocks_i[0:1, 0:1], min_val=NE, max_val=NBLK)
            choose(sel, slice(0, 1))
            xT_out(1)
            with dve.Fori(0, nblk) as b:
                dve.wait_ge(ring_used[GU_SLOT[KD - 1]], b + 1)
                v.tensor_scalar(gS, gate[:, :], LIMIT, None, ALU.min).then_inc(gate_clipped, 1)
                v.tensor_scalar(uS, up[:, :], LIMIT, -LIMIT, ALU.min, ALU.max).then_inc(up_clipped, 1)
                dve.wait_ge(gate_clipped, b + 1)
                dve.wait_ge(up_clipped, b + 1)
                v.scalar_tensor_tensor(tS, uS, 1.0, gS, ALU.add, ALU.mult).then_inc(product, 1)
                dve.wait_ge(gate_sig, b + 1)
                dve.wait_ge(product, b + 1)
                v.tensor_tensor(hid, tS, sS, ALU.mult).then_inc(act_ready, 1)
                dve.wait_ge(xT_full, b + 2)
                choose(sel, bass.ds(b + 1, 1))
                v.tensor_tensor(xT, xTp[:, :].rearrange("p (k t) -> p k t", k=KD), bc(gf_c.unsqueeze(2), [P, KD, CAP]), ALU.mult)\
                    .then_inc(xT_ready, 1)
                add_shares(b)
                v.scalar_tensor_tensor(pair_hit, pair_row, cc("i64")[:, bass.ds(b, 1)], pair_gate, ALU.is_equal, ALU.mult)\
                    .then_inc(hits_ready, 1)
                dve.wait_ge(hits_ready, b + 1)
                v.tensor_reduce(share, pair_hit.rearrange("p k j -> p j k"), X, ALU.add).then_inc(share_ready, 1)
            add_shares(nblk)
            dve.wait_ge(gfin_loaded, 16)
            n0 = 3 * NT + 2
            dve.wait_ge(square_sum, n0 + NT)
            inverse_root(rstd[:, n0:n0 + NT], ssq[:, n0:n0 + NT], D)
            for t in range(NT):
                n = n0 + t
                v.scalar_tensor_tensor(yout[:, t, :], xr[:, t, :], rstd[:, n:n + 1], gfin, ALU.mult, ALU.mult).then_inc(fin_ready, 1)

        @block.scalar
        def _(act):
            a = nc.scalar

            def load(dst, src, slow=False, signal=consts_loaded):
                act.dma_start(dst, src, allow_slow_non_contiguous=slow).then_inc(signal, 16)

            def turned(g, k):
                return g.rearrange("(k p) -> p k", p=P)

            load(con[:, 0:P], d["constants"][:, 0:P], signal=ident_loaded)
            load(gm_c, turned(d["g_mix"][0], KD), slow=True, signal=g_mix_loaded)
            def take(key):
                act.wait_ge(full(key), count(key))
                return bank(key)

            def give(ins, key):
                ins.then_inc(free(key), 1)

            def copy_out(key, dst, n=None, rows=P):
                ps = take(key)
                give(a.copy(dst, ps[0:rows, 0:n] if n else ps), key)

            def squares(n, src, junk=junk):
                if n:
                    act.wait_ge(square_sum, n)
                a.activation(junk, src, ACT.Square, accum_out=ssq[:, n:n + 1]).then_inc(square_sum, 1)

            for t in range(NT):
                act.wait_ge(x_loaded[t], 16)
                squares(t, xr[:, t, :])
            load(con[:, P:NCONST], d["constants"][:, P:NCONST])
            load(gx_c, turned(d["g_x"][0], KD), slow=True)
            load(gf_c, turned(d["g_ffn"][0], KD), slow=True)
            load(gmem_c[:, :], turned(d["g_mem"][0], KD), slow=True)
            load(gq_c, turned(d["g_q"][0], 2), slow=True)
            load(gkv_b[:, :], bc(d["g_kv"], [P, LORA]))
            load(bf_b, bc(d["b_f"], [P, H]))
            load(br_b, bc(d["b_router"], [P, NE]))
            load(wr[:, :, :], d["w_router"][0].rearrange("(k p) e -> p k e", p=P))
            for k in range(KT):
                act.dma_start(lgc[:, k, :, :], d["cache_fox_logf"][0].rearrange("b (p k) h -> p k b h", k=KT)[:, k, :, :])\
                    .then_inc(lgc_loaded, 16)
            for g in range(4):
                copy_out(("fqT", g), fqT[:, g, :], TOK)
            for t in range(NT):
                act.wait_ge(logf_part, t + 1)
                a.activation(lexp[:, t, :], lneg[:, t, :], ACT.Exp).then_inc(act_step, 1)
                act.wait_ge(act_step, t + 1)
                a.activation(lln[:, t, :], lexp[:, t, :], ACT.Ln, bias=1.0).then_inc(logit_exp, 1)
            for c in range(2):
                copy_out(("ukT", c), ukT[:, :, P * c:P * c + P])
            for g in range(4):
                copy_out(("fkT", g), fkT[:, g, :], TOK)
            ps = take("krT")
            for e in range(4):
                last = a.copy(krT[32 * e:32 * e + 32, :], ps[0:ROPE, 0:TOK])
            give(last, "krT")
            for c in range(2):
                copy_out(("ckvT", c), ckvT[:, c, :], TOK)
            for g in range(4):
                copy_out(("qn", g), qnT[:, g, :], TOK)
            def fox_values_out(j, t):
                copy_out(("fv", t, j), fv[:, t, 256 * j:256 * j + 256], 256)

            for t in range(2):
                fox_values_out(0, t)
            for odd in range(2):
                ps = take(("ql", odd, 1))
                give(a.copy(qs[:, 1, :, odd::2, :].rearrange("p b h q -> p h b q"),
                            ps[:, :].rearrange("p (h b q) -> p h b q", h=4, q=NQ)), ("ql", odd, 1))
            for c in range(2):
                copy_out(("qrT", c), qrT[:, c, :], TOK)
            fox_values_out(0, 2)

            SCALES = {"fox": FOX_SCALE, "mla": MLA_SCALE, "mem": X_SCALE}

            def exps(u, unit):
                kind, t, hs = unit
                w = width(kind, t)
                mx, nm, sm, rc, _ = softmax_cols(u)
                act.wait_ge(score_max, u + 1)
                if kind == "mem" and u - 4 >= U_MEM:
                    act.wait_ge(full(turn_key(u - 4)), count(turn_key(u - 4)))
                for n in range(2):
                    dst = prob[u % 4][:, w * n:w * n + w]
                    src = bank(("S", u))[:, w * n:w * n + w] if kind == "mem" else dst
                    last = a.activation(dst, src, ACT.Exp, bias=nm[:, n:n + 1], scale=SCALES[kind], accum_out=sm[:, n:n + 1])
                last.then_inc(exp_done, 1)
                if kind == "mem":
                    act.wait_ge(exp_done, u + 1)
                    give(a.nop(), ("S", u))

            def probs_out(u, unit):
                kind, t, hs = unit
                n = 2 * width(kind, t)
                if u - 4 >= (0 if kind != "mem" else U_MEM):
                    act.wait_ge(full(("V", u - 4)), count(("V", u - 4)))
                copy_out(("T", u), probT[u % 4][:, 0:n], n)

            def values_out(u, unit):
                kind, t, hs = unit
                ps = take(("V", u))
                c = slice(P * t, P * t + P)
                if kind != "mem":
                    e, g = 64 * (hs[0] % 2), hs[0] // 2
                    dst = foxT[e:e + 64, g:g + 2, c] if kind == "fox" else mlaT[e:e + 64, g::2, c]
                    last = a.copy(dst, ps[e:e + 64, 0:256].rearrange("p (n q) -> p n q", n=2))
                else:
                    last = a.copy(xoT[:, hs[0]:hs[0] + 2, c], ps[:, 0:256].rearrange("p (n q) -> p n q", n=2))
                give(last, ("V", u))

            def between_units(i):
                if 1 <= i < 1 + NT:
                    fox_values_out(1, i - 1)
                if 4 <= i < 6:
                    copy_out(("vn", i - 4), vn[:, i - 4, :])

            def pipeline(units, u0, between=None):
                n = len(units)
                for i in range(n + LAG_V):
                    if i < n:
                        exps(u0 + i, units[i])
                    if between:
                        between(i)
                    if LAG_T <= i < n + LAG_T:
                        probs_out(u0 + i - LAG_T, units[i - LAG_T])
                    if i >= LAG_V:
                        values_out(u0 + i - LAG_V, units[i - LAG_V])

            pipeline(UNITS, 0, between_units)

            def keys_out(b):
                if b >= 2:
                    act.wait_ge(full(("sS", 2 * b - 3)), count(("sS", 2 * b - 3)))
                for g in range(2, 4):
                    copy_out(("skT", b, g), skT[b % 2][:, g, :])

            def latents_out(b):
                copy_out(("scT", b, 1), scT[b % 2][:, 1, :])
                copy_out(("srT", b), srT[b % 2], 512, ROPE)

            def sample_exps(n):
                u = U_SAMPLE + n
                mx, nm, sm, rc, m1 = softmax_cols(u)
                act.wait_ge(score_max, u + 1)
                p = sprob[n % 3]
                sc = MLA_SCALE if n % 2 else FOX_SCALE
                give(a.activation(p[:, 0:512], bank(("sS", n))[:, :], ACT.Exp, bias=nm[:, 0:1], scale=sc, accum_out=sm[:, 0:1]), ("sS", n))
                a.activation(p[:, 512:640], p[:, 512:640], ACT.Exp, bias=nm[:, 0:1], scale=sc, accum_out=sm[:, 1:2]).then_inc(exp_done, 1)

            def sample_probs_out(n):
                if n >= 3:
                    act.wait_ge(full(("sV", n - 3)), count(("sV", n - 3)))
                ps = take(("sT", n))
                give(a.copy(sprobT[n % 3][:, 0:4, :], ps[:, :].rearrange("p (k m) -> p k m", k=4)), ("sT", n))
                copy_out(("sTn", n), sprobT[n % 3][:, 4, :], P)

            def sample_values_out(n):
                b = n // 2
                c = slice(256 + NQ * b, 256 + NQ * b + NQ)
                ps = take(("sV", n))
                if n % 2:
                    last = a.copy(qs[:, :, b, :, :], ps[:, 0:256].rearrange("p (c h q) -> p c h q", c=2, h=H))
                else:
                    if b >= 2:
                        act.wait_ge(full(("sO", b - 2)), count(("sO", b - 2)))
                    last = a.copy(fox_rows[(b + 1) % 2], ps[:, 0:P])
                give(last, ("sV", n))

            def sample_outputs(b):
                c = slice(256 + NQ * b, 256 + NQ * b + NQ)
                pair = take(("sO", b))[:, 0:P].rearrange("p (g m) -> p g m", g=4)
                a.copy(foxT[0:64, :, c], pair[0:64, :, 0:NQ])
                give(a.copy(foxT[64:128, :, c], pair[64:128, :, NQ:2 * NQ]), ("sO", b))

            act.wait_ge(fk_written, 32)
            keys_out(0)
            latents_out(0)
            for b in range(NB + 1):
                for n in (2 * b, 2 * b + 1):
                    if b < NB:
                        sample_exps(n)
                    if b >= 1:
                        sample_probs_out(n - 2)
                if b >= 1:
                    sample_values_out(2 * b - 2)
                if b + 1 < NB:
                    keys_out(b + 1)
                    latents_out(b + 1)
                if b >= 1:
                    sample_values_out(2 * b - 1)
                    sample_outputs(b - 1)
            for g in range(4):
                copy_out(("mo", g), mlaT[:, g, 256:384], P)
            for n in range(16):
                ps = take(("g", n))
                give(a.activation(gates[:, n, :], ps[:, 0:TOK], ACT.Sigmoid), ("g", n))
                act.wait_ge(free(("g", n)), count(("g", n)))
                a.nop().then_inc(gates_ready, 1)
                if n == KD:
                    act.wait_ge(mem_loaded, 16)
                    for t in range(2):
                        squares(NT + t, memx[:, t, :])

            def mem_rows_out(w, m):
                for j in range(2):
                    for t in range(2):
                        copy_out((w, t, j), m[:, t, 256 * j:256 * j + 256], 256)

            mem_rows_out("xk", mk)
            for t in range(NT):
                act.wait_ge(free(("out", t, 3)), count(("out", t, 3)))
                squares(NT + 2 + t, xr[:, t, :])
            mem_rows_out("xv", mv)
            for h in range(XH):
                copy_out(("mkT", h), mkTs[:, h, :], MEM)
            for h in range(XH):
                copy_out(("xq", h), xqT[:, h, :], TOK)

            def mem_out(b):
                if b >= 2:
                    act.wait_ge(full(("cS", b - 2)), count(("cS", b - 2)))
                ps = take(("cK", b, 1))
                give(a.copy(xkT[b % 2][:, 2:4, :], ps[:, :].rearrange("p (h s) -> p h s", h=2)), ("cK", b, 1))

            def mem_exps(b):
                u = U_SMEM + b
                mx, nm, sm, rc, _ = softmax_cols(u)
                act.wait_ge(score_max, u + 1)
                act.wait_ge(full(turn_key(u - 4)), count(turn_key(u - 4)))
                give(a.activation(prob[b % 4][:, 0:MEM], bank(("cS", b))[:, 0:MEM], ACT.Exp, bias=nm[:, 0:1], scale=X_SCALE,
                                  accum_out=sm[:, 0:1]), ("cS", b))
                act.wait_ge(free(("cS", b)), count(("cS", b)))
                a.nop().then_inc(exp_done, 1)

            def mem_probs_out(b):
                key = ("V", U_MEM + b) if b < 4 else ("cV", b - 4)
                act.wait_ge(full(key), count(key))
                copy_out(("cT", b), probT[b % 4][:, 0:256], 256)

            def mem_values_out(b):
                if b >= 2:
                    act.wait_ge(full(("cO", b - 2)), count(("cO", b - 2)))
                ps = take(("cV", b))
                give(a.copy(mem_rows[b % 2], ps[:, 0:P]), ("cV", b))

            def mem_outputs(b):
                ps = take(("cO", b))
                c = slice(256 + NQ * b, 256 + NQ * b + NQ)
                give(a.copy(xoT[:, :, c], ps[:, 0:P].rearrange("p (h m) -> p h m", h=XH)[:, :, 0:NQ]), ("cO", b))

            def cross_squares(t):
                act.wait_ge(free(("xo", t, 1)), count(("xo", t, 1)))
                squares(2 * NT + 2 + t, xr[:, t, :], junk=mlaf[:, 0:D])

            mem_out(0)
            pipeline(XUNITS, U_MEM, lambda i: mem_out(1) if i == 1 else None)
            for b in range(NB + 2):
                if b < NB:
                    mem_exps(b)
                if 1 <= b <= NB:
                    mem_probs_out(b - 1)
                if b >= 2:
                    mem_outputs(b - 2)
                if 1 < b + 1 < NB:
                    mem_out(b + 1)
                if 1 <= b <= NB:
                    mem_values_out(b - 1)
                if b in (6, 7):
                    cross_squares(b - 6)
            cross_squares(2)
            for t in range(NT):
                act.wait_ge(top_shift, t + 1)
                a.activation(top8[:, t, 0:TOPK], top8[:, t, 0:TOPK], ACT.Exp, bias=ntop[:, t:t + 1],
                             accum_out=esum[:, t:t + 1]).then_inc(top_exp, 1)

            for name, pairs, shift in (("pair_gate", pair_gate, 0.0), ("pair_row", pair_row, cc("row"))):
                for t in range(NT):
                    ps = take((name, t))
                    give(a.activation(pairs[:, :, P * t:P * t + P], ps[:, :].rearrange("p (k j) -> p k j", k=TOPK),
                                      ACT.Identity, bias=shift), (name, t))

            act.wait_ge(fv_written, 32)
            act.dma_start(gfin, bc(d["g_final"].unsqueeze(0), [P, D])).then_inc(gfin_loaded, 16)
            act.wait_ge(blocks_ready, 1)
            nblk = act.value_load(blocks_i[0:1, 0:1], min_val=NE, max_val=NBLK)
            aTp, yp = psum[3], psum[4]
            a.nop().then_inc(y_copied, 1)
            act.wait_ge(y_copied, 1)
            with act.Fori(0, nblk) as b:
                act.wait_ge(gate_clipped, b + 1)
                a.activation(sS, gS, ACT.Sigmoid, scale=ALPHA).then_inc(gate_sig, 1)
                act.wait_ge(actT_full, b + 1)
                a.copy(actT, aTp[:, :].rearrange("p (k t) -> p k t", t=CAP)).then_inc(actT_ready, 1)
                act.wait_ge(ring_used[DOWN_SLOT[3]], b + 1)
                a.copy(ysb, yp[:, :]).then_inc(y_copied, 1)
            for t in range(NT):
                act.wait_ge(shares_added, nblk * 6 + (2 * t + 2))
                squares(3 * NT + 2 + t, xr[:, t, :])


_INS = ["x_prompt", "x_sample", "mem_prompt", "cache_fox_k", "cache_fox_v", "cache_fox_logf", "cache_mla_ckv",
        "cache_mla_krope", "cache_mem_k", "cache_mem_v", "g_mix", "w_in", "b_f", "g_q", "w_uq", "g_kv", "w_uk", "w_uv",
        "w_o_fox", "w_o_mla", "w_out", "g_x", "g_mem", "w_xq", "w_xk", "w_xv", "w_xo", "g_ffn", "w_router", "b_router",
        "w_gu", "b_gu", "w_down", "b_down", "g_final"]
_OUTS = [("y_prompt", (1, 256, 1024)), ("y_sample", (8, 16, 1024)), ("p_fox_k", (1, 1, 256, 8, 64)),
         ("p_fox_v", (1, 1, 256, 8, 64)), ("p_fox_logf", (1, 1, 256, 8)), ("p_mla_ckv", (1, 1, 256, 256)),
         ("p_mla_krope", (1, 1, 256, 32)), ("p_mem_k", (1, 1, 256, 4, 128)), ("p_mem_v", (1, 1, 256, 4, 128)),
         ("s_fox_k", (1, 8, 16, 8, 64)), ("s_fox_v", (1, 8, 16, 8, 64)), ("s_fox_logf", (1, 8, 16, 8)),
         ("s_mla_ckv", (1, 8, 16, 256)), ("s_mla_krope", (1, 8, 16, 32))]


def kernel(**inputs):
    import concourse.bacc as _bacc
    from concourse.bass_utils import run_bass_kernel_spmd as _run

    nc = _bacc.Bacc("TRN2", target_bir_lowering=False, num_devices=1)
    arrays = {"in_" + name: np.ascontiguousarray(inputs[name]) for name in _INS}
    arrays["in_constants"] = constants()
    ins = {name[3:]: nc.dram_tensor(name, a.shape, F32, kind="ExternalInput").ap() for name, a in arrays.items()}
    outs = {name: nc.dram_tensor(name, shape, F32, kind="ExternalOutput").ap() for name, shape in _OUTS}
    build(nc, ins, outs)
    r = _run(nc, [arrays], core_ids=[0])
    return tuple(r.results[0][name] for name, _ in _OUTS)
```
